# Optimizing a Trainium2 kernel written in Bass

```python
import math, functools
import jax, jax.numpy as jnp
from jax import lax
import numpy as np

D_MODEL = 1024
BATCH = 1
SEQ = 256
DEPTH = 2
DEC_BATCH = 8
DEC_SEQ = 8
PAST_LEN = 2048
PAGE_SIZE = 128

RET_HEADS = 8
RET_DK = D_MODEL // 2 // RET_HEADS
RET_DV = 2 * RET_DK
RET_CHUNK = 128
MOBA_HEADS = 8
MOBA_HD = D_MODEL // 2 // MOBA_HEADS
MOBA_BLOCK = 256
MOBA_TOPK = 3
MOBA_QCHUNK = 128
ROPE_THETA = 10000.0
D_INNER = 2 * D_MODEL
SSM_HEAD_DIM = 64
SSM_HEADS = D_INNER // SSM_HEAD_DIM
SSM_GROUPS = 8
D_STATE = 128
CONV_W = 4
CONV_DIM = D_INNER + 2 * SSM_GROUPS * D_STATE
SSD_CHUNK = 128
MOE_GROUPS = 4
MOE_EXPERTS_PER_GROUP = 4
N_EXPERTS = MOE_GROUPS * MOE_EXPERTS_PER_GROUP
MOE_TOPK = 2
EXPERT_FF = D_MODEL // 2
MOE_TOKEN_BLOCK = 1024
NORM_EPS = 1e-6
EVEN_IN = 2 * RET_HEADS * RET_DK + 2 * RET_HEADS * RET_DV + 3 * MOBA_HEADS * MOBA_HD
EVEN_OUT = RET_HEADS * RET_DV + MOBA_HEADS * MOBA_HD
ODD_IN = D_INNER + CONV_DIM + SSM_HEADS
F32 = jnp.float32

kernel_name = "hybrid_retention_moba_ssd_hmoe_step"

def _split(x, sizes):
    idx, acc = [], 0
    for s in sizes[:-1]:
        acc += s
        idx.append(acc)
    return jnp.split(x, idx, axis=-1)

def rmsnorm(x, g=None):
    xf = x.astype(F32)
    y = xf * lax.rsqrt(jnp.mean(xf * xf, axis=-1, keepdims=True) + NORM_EPS)
    if g is not None:
        y = y * g.astype(F32)
    return y.astype(x.dtype)

def rope(x, pos):
    d = x.shape[-1]
    half = d // 2
    inv = jnp.power(ROPE_THETA, -jnp.arange(half, dtype=F32) * 2.0 / d)
    ang = pos[:, None] * inv[None, :]
    cos = jnp.cos(ang)[:, None, :]
    sin = jnp.sin(ang)[:, None, :]
    xf = x.astype(F32)
    x1, x2 = xf[..., :half], xf[..., half:]
    return jnp.concatenate([x1 * cos - x2 * sin, x2 * cos + x1 * sin], axis=-1).astype(x.dtype)

def scan_chunks(step, s0, xs, chunk):
    n = xs[0].shape[1] // chunk
    xs_c = tuple(jnp.moveaxis(a.reshape(a.shape[0], n, chunk, *a.shape[2:]), 1, 0) for a in xs)

    def body(s, inp):
        y, s_new = step(*inp, s)
        return s_new, y

    s_fin, ys = lax.scan(body, s0, xs_c)
    ys = jnp.moveaxis(ys, 0, 1)
    return ys.reshape(ys.shape[0], n * chunk, *ys.shape[3:]), s_fin

def retention_log_decay():
    return jnp.log1p(-jnp.exp2(-5.0 - jnp.arange(RET_HEADS, dtype=F32)))

def retention_chunk(q, k, v, s0, log_g):
    l = q.shape[1]
    i = jnp.arange(l, dtype=F32)
    diff = i[:, None] - i[None, :]
    dmat = jnp.where(diff[None] >= 0, jnp.exp(jnp.maximum(diff, 0.0)[None] * log_g[:, None, None]), 0.0)
    qf, kf, vf = q.astype(F32), k.astype(F32), v.astype(F32)
    scores = jnp.einsum('blhk,bmhk->bhlm', qf, kf) * dmat
    inter = jnp.einsum('blhk,bhkv->blhv', qf, s0) * jnp.exp((i + 1.0)[:, None] * log_g)[None, :, :, None]
    o = jnp.einsum('bhlm,bmhv->blhv', scores, vf) + inter
    k_dec = kf * jnp.exp((l - 1.0 - i)[:, None] * log_g)[None, :, :, None]
    s_new = s0 * jnp.exp(l * log_g)[None, :, None, None] + jnp.einsum('blhk,blhv->bhkv', k_dec, vf)
    return o, s_new

def ssd_chunk(x, dt, bm, cm, s0, a):
    b, l, h, p = x.shape
    g, n = bm.shape[2], bm.shape[3]
    r = h // g
    cs = jnp.cumsum(dt * a, axis=1)
    causal = jnp.tril(jnp.ones((l, l), dtype=bool))
    seg = cs[:, :, None, :] - cs[:, None, :, :]
    decay = jnp.exp(jnp.where(causal[None, :, :, None], seg, -jnp.inf))
    bf, cf = bm.astype(F32), cm.astype(F32)
    cb = jnp.einsum('bign,bjgn->bijg', cf, bf)
    wts = decay.reshape(b, l, l, g, r) * cb[..., None]
    xdt = (x.astype(F32) * dt[..., None]).reshape(b, l, g, r, p)
    y_intra = jnp.einsum('bijgr,bjgrp->bigrp', wts, xdt)
    s0g = s0.reshape(b, g, r, p, n)
    y_inter = jnp.einsum('bign,bgrpn->bigrp', cf, s0g) * jnp.exp(cs).reshape(b, l, g, r)[..., None]
    tail = jnp.exp(cs[:, -1:, :] - cs).reshape(b, l, g, r)[..., None]
    s_new = s0 * jnp.exp(cs[:, -1])[:, :, None, None] + jnp.einsum('bjgrp,bjgn->bgrpn', xdt * tail, bf).reshape(b, h, p, n)
    return (y_intra + y_inter).reshape(b, l, h, p), s_new

def moba_prompt(q, k, v):
    bsz, seq, nh, hd = q.shape
    nb = -(-seq // MOBA_BLOCK)
    pad = nb * MOBA_BLOCK - seq
    kp = jnp.pad(k, ((0, 0), (0, pad), (0, 0), (0, 0)))
    vp = jnp.pad(v, ((0, 0), (0, pad), (0, 0), (0, 0)))
    kb = kp.reshape(bsz, nb, MOBA_BLOCK, nh, hd)
    vb = vp.reshape(bsz, nb, MOBA_BLOCK, nh, hd)
    kbar = jnp.mean(kb.astype(F32), axis=2)
    qf = q.astype(F32)
    gate = jnp.einsum('bshd,bnhd->bshn', qf, kbar)
    qblk = jnp.arange(seq) // MOBA_BLOCK
    fully_past = jnp.arange(nb)[None, :] < qblk[:, None]
    gate = jnp.where(fully_past[None, :, None, :], gate, -jnp.inf)
    n_sel = max(1, min(MOBA_TOPK, nb - 1))
    _, sel = lax.top_k(gate, n_sel)
    kbt = kb.transpose(0, 3, 1, 2, 4)
    vbt = vb.transpose(0, 3, 1, 2, 4)
    nqc = seq // MOBA_QCHUNK
    h_idx = jnp.arange(nh)[None, :, None]
    scale = hd ** -0.5
    n_s = n_sel * MOBA_BLOCK

    def one_chunk(args):
        b, c, q_c, sel_c = args
        start = c * MOBA_QCHUNK
        qb = start // MOBA_BLOCK
        own0 = qb * MOBA_BLOCK
        k_own = lax.dynamic_slice_in_dim(kp[b], own0, MOBA_BLOCK, axis=0).astype(F32)
        v_own = lax.dynamic_slice_in_dim(vp[b], own0, MOBA_BLOCK, axis=0).astype(F32)
        qpos = start + jnp.arange(MOBA_QCHUNK)
        kpos = own0 + jnp.arange(MOBA_BLOCK)
        s_own = jnp.einsum('qhd,khd->qhk', q_c, k_own) * scale
        s_own = jnp.where((kpos[None, :] <= qpos[:, None])[:, None, :], s_own, -jnp.inf)
        k_sel = kbt[b][h_idx, sel_c].astype(F32)
        v_sel = vbt[b][h_idx, sel_c].astype(F32)
        s_sel = jnp.einsum('qhd,qhjkd->qhjk', q_c, k_sel) * scale
        s_sel = jnp.where((sel_c < qb)[..., None], s_sel, -jnp.inf)
        s = jnp.concatenate([s_sel.reshape(MOBA_QCHUNK, nh, n_s), s_own], axis=-1)
        p = jax.nn.softmax(s, axis=-1)
        o = jnp.einsum('qhjk,qhjkd->qhd', p[..., :n_s].reshape(s_sel.shape), v_sel)
        return o + jnp.einsum('qhk,khd->qhd', p[..., n_s:], v_own)

    b_ids = jnp.repeat(jnp.arange(bsz), nqc)
    c_ids = jnp.tile(jnp.arange(nqc), bsz)
    out = lax.map(one_chunk, (b_ids, c_ids, qf.reshape(bsz * nqc, MOBA_QCHUNK, nh, hd),
                              sel.reshape(bsz * nqc, MOBA_QCHUNK, nh, n_sel)))
    return out.reshape(bsz, seq, nh, hd).astype(q.dtype)

def moba_sample(q, k_new, v_new, pool_k, pool_v, page_table):
    db, t, nh, hd = q.shape
    ppb = MOBA_BLOCK // PAGE_SIZE
    n_pages = page_table.shape[1]
    n_full = n_pages // ppb
    n_own_pages = n_pages - n_full * ppb
    scale = hd ** -0.5
    qf = q.astype(F32)
    k_own, v_own = k_new.astype(F32), v_new.astype(F32)
    if n_own_pages > 0:
        own_pt = page_table[:, n_full * ppb:]
        k_own = jnp.concatenate([pool_k[own_pt].reshape(db, -1, nh, hd).astype(F32), k_own], axis=1)
        v_own = jnp.concatenate([pool_v[own_pt].reshape(db, -1, nh, hd).astype(F32), v_own], axis=1)
    n_op = n_own_pages * PAGE_SIZE
    kpos = jnp.arange(n_op + t)
    qpos = n_op + jnp.arange(t)
    s_own = jnp.einsum('bthd,bkhd->bthk', qf, k_own) * scale
    s_own = jnp.where((kpos[None, :] <= qpos[:, None])[None, :, None, :], s_own, -jnp.inf)
    if n_full > 0:
        n_sel = min(MOBA_TOPK, n_full)
        k_past = pool_k[page_table[:, :n_full * ppb]].astype(F32).reshape(db, n_full, MOBA_BLOCK, nh, hd)
        kbar = jnp.mean(k_past, axis=2)
        gate = jnp.einsum('bthd,bnhd->bthn', qf, kbar)
        _, sel = lax.top_k(gate, n_sel)
        pages = page_table[jnp.arange(db)[:, None, None, None, None], sel[..., None] * ppb + jnp.arange(ppb)]
        h_idx = jnp.arange(nh)[None, None, :, None, None]
        k_sel = pool_k[pages, :, h_idx, :].astype(F32).reshape(db, t, nh, n_sel, MOBA_BLOCK, hd)
        v_sel = pool_v[pages, :, h_idx, :].astype(F32).reshape(db, t, nh, n_sel, MOBA_BLOCK, hd)
        s_sel = jnp.einsum('bthd,bthjkd->bthjk', qf, k_sel) * scale
        n_s = n_sel * MOBA_BLOCK
        s = jnp.concatenate([s_sel.reshape(db, t, nh, n_s), s_own], axis=-1)
        p = jax.nn.softmax(s, axis=-1)
        o = jnp.einsum('bthjk,bthjkd->bthd', p[..., :n_s].reshape(s_sel.shape), v_sel)
        o = o + jnp.einsum('bthk,bkhd->bthd', p[..., n_s:], v_own)
    else:
        o = jnp.einsum('bthk,bkhd->bthd', jax.nn.softmax(s_own, axis=-1), v_own)
    return o.astype(q.dtype)

def even_mixer(xn, pos, ret_s0, moba_fn, w_in, w_out, q_g, k_g):
    bsz, t, _ = xn.shape
    rq, rk, rv, rg, mq, mk, mv = _split(xn @ w_in, [RET_HEADS * RET_DK, RET_HEADS * RET_DK,
                                                   RET_HEADS * RET_DV, RET_HEADS * RET_DV,
                                                   MOBA_HEADS * MOBA_HD, MOBA_HEADS * MOBA_HD,
                                                   MOBA_HEADS * MOBA_HD])
    rq = rope(rq.reshape(bsz, t, RET_HEADS, RET_DK), pos)
    rk = rope(rk.reshape(bsz, t, RET_HEADS, RET_DK), pos) * (RET_DK ** -0.5)
    rv = rv.reshape(bsz, t, RET_HEADS, RET_DV)
    step = functools.partial(retention_chunk, log_g=retention_log_decay())
    ro, ret_state = scan_chunks(step, ret_s0.astype(F32), (rq, rk, rv), min(RET_CHUNK, t))
    ro = jax.nn.silu(rg.astype(F32)) * rmsnorm(ro).reshape(bsz, t, RET_HEADS * RET_DV)
    mq = rope(rmsnorm(mq.reshape(bsz, t, MOBA_HEADS, MOBA_HD), q_g), pos)
    mk = rope(rmsnorm(mk.reshape(bsz, t, MOBA_HEADS, MOBA_HD), k_g), pos)
    mv = mv.reshape(bsz, t, MOBA_HEADS, MOBA_HD)
    mo = moba_fn(mq, mk, mv).reshape(bsz, t, MOBA_HEADS * MOBA_HD)
    y = jnp.concatenate([ro.astype(xn.dtype), mo.astype(xn.dtype)], axis=-1) @ w_out
    return y, ret_state, mk, mv

def odd_mixer(xn, conv_buf, ssm_s0, w_in, conv_w, conv_b, dt_bias, a_log, d_skip, norm_g, w_out):
    bsz, t, _ = xn.shape
    z, xbc, dt = _split(xn @ w_in, [D_INNER, CONV_DIM, SSM_HEADS])
    xbc_full = jnp.concatenate([conv_buf.astype(xbc.dtype), xbc], axis=1)
    new_buf = xbc_full[:, -(CONV_W - 1):]
    xc = lax.conv_general_dilated(xbc_full, conv_w[:, None, :].astype(xbc_full.dtype), window_strides=(1,),
                                  padding='VALID', dimension_numbers=('NWC', 'WIO', 'NWC'),
                                  feature_group_count=CONV_DIM)
    xc = jax.nn.silu(xc + conv_b)
    xs, bm, cm = _split(xc, [D_INNER, SSM_GROUPS * D_STATE, SSM_GROUPS * D_STATE])
    xs = xs.reshape(bsz, t, SSM_HEADS, SSM_HEAD_DIM)
    bm = bm.reshape(bsz, t, SSM_GROUPS, D_STATE)
    cm = cm.reshape(bsz, t, SSM_GROUPS, D_STATE)
    dt = jax.nn.softplus(dt.astype(F32) + dt_bias.astype(F32))
    a = -jnp.exp(a_log.astype(F32))
    step = functools.partial(ssd_chunk, a=a)
    y, s_fin = scan_chunks(step, ssm_s0.astype(F32), (xs, dt, bm, cm), min(SSD_CHUNK, t))
    y = y + d_skip.astype(F32)[None, None, :, None] * xs.astype(F32)
    yz = y.reshape(bsz, t, D_INNER) * jax.nn.silu(z.astype(F32))
    yz = rmsnorm(yz.reshape(bsz, t, SSM_GROUPS, D_INNER // SSM_GROUPS), norm_g.reshape(SSM_GROUPS, -1))
    return yz.reshape(bsz, t, D_INNER).astype(xn.dtype) @ w_out, new_buf, s_fin

def hier_moe(xn, w_rg, w_re, w_g, w_u, w_d):
    shp = xn.shape
    tok = xn.reshape(-1, shp[-1])
    n = tok.shape[0]
    blk = MOE_TOKEN_BLOCK if n % MOE_TOKEN_BLOCK == 0 else n

    def block_fn(t):
        lg = (t @ w_rg).astype(F32)
        pg = jax.nn.softmax(lg, axis=-1)
        gi = jnp.argmax(lg, axis=-1)
        wg = jnp.take_along_axis(pg, gi[:, None], axis=-1)
        le = (t @ w_re).astype(F32).reshape(-1, MOE_GROUPS, MOE_EXPERTS_PER_GROUP)
        le = jnp.take_along_axis(le, gi[:, None, None], axis=1)[:, 0]
        pe = jax.nn.softmax(le, axis=-1)
        top_p, top_i = lax.top_k(pe, MOE_TOPK)
        top_p = top_p / jnp.sum(top_p, axis=-1, keepdims=True)
        local = jnp.sum(jax.nn.one_hot(top_i, MOE_EXPERTS_PER_GROUP, dtype=F32) * top_p[..., None], axis=1)
        gate = (jax.nn.one_hot(gi, MOE_GROUPS, dtype=F32)[:, :, None] * local[:, None, :] * wg[:, :, None])
        gate = gate.reshape(-1, N_EXPERTS)
        h = jax.nn.silu(jnp.einsum('nd,edf->nef', t, w_g)) * jnp.einsum('nd,edf->nef', t, w_u)
        h = h * gate[..., None].astype(h.dtype)
        return jnp.einsum('nef,efd->nd', h, w_d)

    out = lax.map(block_fn, tok.reshape(n // blk, blk, shp[-1]))
    return out.reshape(shp)

def setup_inputs(seed: int = 0) -> dict:
    key = jax.random.key(seed)
    ks = iter(jax.random.split(key, 40))
    n_even = (DEPTH + 1) // 2
    n_odd = DEPTH // 2
    n_pages = PAST_LEN // PAGE_SIZE
    n_pool = (DEC_BATCH * n_pages * 5) // 4

    def nrm(shape, scale):
        return jax.random.normal(next(ks), shape, F32) * scale

    x_prompt = nrm((BATCH, SEQ, D_MODEL), 1.0)
    x_sample = nrm((DEC_BATCH, DEC_SEQ, D_MODEL), 1.0)
    state_ret = nrm((n_even, DEC_BATCH, RET_HEADS, RET_DK, RET_DV), 0.3)
    cache_k = nrm((n_even, n_pool, PAGE_SIZE, MOBA_HEADS, MOBA_HD), 1.0)
    cache_v = nrm((n_even, n_pool, PAGE_SIZE, MOBA_HEADS, MOBA_HD), 1.0)
    page_table = jax.random.permutation(next(ks), n_pool)[:DEC_BATCH * n_pages].reshape(DEC_BATCH, n_pages).astype(jnp.int32)
    state_ssm = nrm((n_odd, DEC_BATCH, SSM_HEADS, SSM_HEAD_DIM, D_STATE), 0.3)
    state_conv = nrm((n_odd, DEC_BATCH, CONV_W - 1, CONV_DIM), 1.0)
    norm_mix = 1.0 + nrm((DEPTH, D_MODEL), 0.02)
    norm_ffn = 1.0 + nrm((DEPTH, D_MODEL), 0.02)
    w_in_even = nrm((n_even, D_MODEL, EVEN_IN), D_MODEL ** -0.5)
    w_out_even = nrm((n_even, EVEN_OUT, D_MODEL), EVEN_OUT ** -0.5)
    q_norm = 1.0 + nrm((n_even, MOBA_HD), 0.02)
    k_norm = 1.0 + nrm((n_even, MOBA_HD), 0.02)
    w_in_odd = nrm((n_odd, D_MODEL, ODD_IN), D_MODEL ** -0.5)
    conv_w = nrm((n_odd, CONV_W, CONV_DIM), 0.5)
    conv_b = nrm((n_odd, CONV_DIM), 0.02)
    dt0 = jnp.exp(jax.random.uniform(next(ks), (n_odd, SSM_HEADS), F32, math.log(1e-3), math.log(1e-1)))
    dt_bias = dt0 + jnp.log(-jnp.expm1(-dt0))
    a_log = jnp.log(jax.random.uniform(next(ks), (n_odd, SSM_HEADS), F32, 1.0, 16.0))
    d_skip = 1.0 + nrm((n_odd, SSM_HEADS), 0.1)
    ssd_norm = 1.0 + nrm((n_odd, D_INNER), 0.02)
    w_out_odd = nrm((n_odd, D_INNER, D_MODEL), D_INNER ** -0.5)
    w_router_group = nrm((DEPTH, D_MODEL, MOE_GROUPS), D_MODEL ** -0.5)
    w_router_expert = nrm((DEPTH, D_MODEL, N_EXPERTS), D_MODEL ** -0.5)
    w_expert_gate = nrm((DEPTH, N_EXPERTS, D_MODEL, EXPERT_FF), D_MODEL ** -0.5)
    w_expert_up = nrm((DEPTH, N_EXPERTS, D_MODEL, EXPERT_FF), D_MODEL ** -0.5)
    w_expert_down = nrm((DEPTH, N_EXPERTS, EXPERT_FF, D_MODEL), EXPERT_FF ** -0.5)
    return {"x_prompt": x_prompt, "x_sample": x_sample, "state_ret": state_ret, "cache_k": cache_k,
            "cache_v": cache_v, "page_table": page_table, "state_ssm": state_ssm, "state_conv": state_conv,
            "norm_mix": norm_mix, "norm_ffn": norm_ffn, "w_in_even": w_in_even, "w_out_even": w_out_even,
            "q_norm": q_norm, "k_norm": k_norm, "w_in_odd": w_in_odd, "conv_w": conv_w, "conv_b": conv_b,
            "dt_bias": dt_bias, "a_log": a_log, "d_skip": d_skip, "ssd_norm": ssd_norm, "w_out_odd": w_out_odd,
            "w_router_group": w_router_group, "w_router_expert": w_router_expert,
            "w_expert_gate": w_expert_gate, "w_expert_up": w_expert_up, "w_expert_down": w_expert_down}

def reference(x_prompt, x_sample, state_ret, cache_k, cache_v, page_table, state_ssm, state_conv,
              norm_mix, norm_ffn, w_in_even, w_out_even, q_norm, k_norm, w_in_odd, conv_w, conv_b,
              dt_bias, a_log, d_skip, ssd_norm, w_out_odd, w_router_group, w_router_expert,
              w_expert_gate, w_expert_up, w_expert_down):
    bp, seq, _ = x_prompt.shape
    bs, dec_seq, _ = x_sample.shape
    past_len = page_table.shape[1] * PAGE_SIZE
    pos_p = jnp.arange(seq, dtype=F32)
    pos_s = past_len + jnp.arange(dec_seq, dtype=F32)
    hp, hs = x_prompt, x_sample
    ret_p, ret_s, k_p, v_p, k_s, v_s = [], [], [], [], [], []
    ssm_p, ssm_s, conv_p, conv_s = [], [], [], []
    for layer in range(DEPTH):
        if layer % 2 == 0:
            e = layer // 2
            mix = functools.partial(even_mixer, w_in=w_in_even[e], w_out=w_out_even[e], q_g=q_norm[e], k_g=k_norm[e])
            yp, rs1, kk1, vv1 = mix(rmsnorm(hp, norm_mix[layer]), pos_p,
                                    jnp.zeros((bp, RET_HEADS, RET_DK, RET_DV), F32), moba_prompt)
            paged = functools.partial(moba_sample, pool_k=cache_k[e], pool_v=cache_v[e], page_table=page_table)
            ys, rs2, kk2, vv2 = mix(rmsnorm(hs, norm_mix[layer]), pos_s, state_ret[e], paged)
            ret_p.append(rs1); ret_s.append(rs2)
            k_p.append(kk1); v_p.append(vv1); k_s.append(kk2); v_s.append(vv2)
        else:
            o = layer // 2
            mix = functools.partial(odd_mixer, w_in=w_in_odd[o], conv_w=conv_w[o], conv_b=conv_b[o],
                                    dt_bias=dt_bias[o], a_log=a_log[o], d_skip=d_skip[o],
                                    norm_g=ssd_norm[o], w_out=w_out_odd[o])
            yp, cb1, ss1 = mix(rmsnorm(hp, norm_mix[layer]), jnp.zeros((bp, CONV_W - 1, CONV_DIM), x_prompt.dtype),
                               jnp.zeros((bp, SSM_HEADS, SSM_HEAD_DIM, D_STATE), F32))
            ys, cb2, ss2 = mix(rmsnorm(hs, norm_mix[layer]), state_conv[o], state_ssm[o])
            ssm_p.append(ss1); ssm_s.append(ss2); conv_p.append(cb1); conv_s.append(cb2)
        hp = hp + yp
        hs = hs + ys
        ffn = functools.partial(hier_moe, w_rg=w_router_group[layer], w_re=w_router_expert[layer],
                                w_g=w_expert_gate[layer], w_u=w_expert_up[layer], w_d=w_expert_down[layer])
        hp = hp + ffn(rmsnorm(hp, norm_ffn[layer]))
        hs = hs + ffn(rmsnorm(hs, norm_ffn[layer]))
    return (hp, hs, jnp.stack(ret_p), jnp.stack(ret_s), jnp.stack(k_p), jnp.stack(v_p), jnp.stack(k_s),
            jnp.stack(v_s), jnp.stack(ssm_p), jnp.stack(ssm_s), jnp.stack(conv_p), jnp.stack(conv_s))


_drawn_inputs = setup_inputs


def setup_inputs(seed=0):
    import zlib

    import numpy as np

    out = dict(_drawn_inputs(seed))
    spreads = {}
    factors = {'q_norm': 2.696, 'k_norm': 2.812, 'ssd_norm': 3.004}
    for name, (base, spread) in spreads.items():
        noise = np.random.default_rng([zlib.crc32(name.encode()), seed]).standard_normal(out[name].shape)
        drawn = base * np.exp(spread * noise) if base else spread * noise
        out[name] = __import__('jax').numpy.asarray(drawn.astype(out[name].dtype))
    for name, factor in factors.items():
        out[name] = (out[name] * factor).astype(out[name].dtype)
    return out
```

```python
from contextlib import ExitStack

import numpy as np

import concourse.bass as bass
from concourse import mybir

F32 = mybir.dt.float32
I32 = mybir.dt.int32
ALU = mybir.AluOpType
ACT = mybir.ActivationFunctionType
AX_X = mybir.AxisListType.X

P = 128
D_MODEL, SEQ, DEC_BATCH, DEC_SEQ, PAST_LEN, PAGE = 1024, 256, 8, 8, 2048, 128
KC = D_MODEL // P
NS = DEC_BATCH * DEC_SEQ
NT = SEQ + NS
NTP = 3 * P
HEADS, HD, DV = 8, 64, 128
N_PAGES = PAST_LEN // PAGE
BLOCK = 256
N_BLOCKS = PAST_LEN // BLOCK
TOPK = 3
QK_SCALE = HD ** -0.5
GROUPS, D_STATE, D_INNER, SSM_HEADS, CONV_W = 8, 128, 2048, 32, 4
N_EXPERTS, EXPERT_FF, MOE_GROUPS = 16, 512, 4
FC = EXPERT_FF // P
EPS = 1e-6
NEG = -1e30
TRI = 2 * P + P + NS
SLOT = 4096
N_SLOTS = 6
EVEN_COLS = [0, 512, 3072, 3584, 4096, 1024, 1536, 2048, 2560]
RQ, RK, MQ, MK, MV, RV = 0, 512, 1024, 1536, 2048, 2560
QKV_W = 3584


def shape_constants():
    f = np.float32
    tok = np.arange(NTP)
    sample = tok >= SEQ
    t_in = np.where(sample, (tok - SEQ) % DEC_SEQ, tok)
    pos = np.where(sample, PAST_LEN + t_in, tok).astype(f)
    inv = np.power(f(10000.0), -np.arange(HD // 2, dtype=f) * f(2.0) / f(HD)).astype(f)
    ang = pos[:, None] * inv[None, :]
    by_tile = lambda a: np.ascontiguousarray(a.reshape(3, P, -1).transpose(1, 0, 2)).astype(f)
    cos = by_tile(np.concatenate([np.cos(ang), np.cos(ang)], 1))
    sin = by_tile(np.concatenate([-np.sin(ang), np.sin(ang)], 1))
    lg = np.log1p(-np.exp2(-5.0 - np.arange(HEADS)))
    key = np.concatenate([np.repeat(np.arange(P)[:, None], 2 * P, 1),
                          np.repeat(P + np.arange(P)[:, None], P, 1),
                          np.repeat(SEQ + np.arange(P)[:, None], NS, 1)], 1)
    qry = np.concatenate([np.arange(2 * P), P + np.arange(P), SEQ + np.arange(NS)])[None, :].repeat(P, 0)
    same = (key < SEQ) & (qry < SEQ) | (key >= SEQ) & (key < NT) & ((key - SEQ) // 8 == (qry - SEQ) // 8)
    ok = same & (qry >= key)
    dist = np.where(ok, qry - key, 0)
    dmat = np.where(ok[None], np.exp(dist[None] * lg[:, None, None]), 0.0) * HD ** -0.5
    left = np.where(sample, DEC_SEQ - 1 - t_in, SEQ - 1 - t_in)
    kdec = np.where((tok < NT)[:, None], np.exp(left[:, None] * lg[None, :]) * HD ** -0.5, 0.0)
    qdec = np.exp((np.arange(NS) % 8 + 1)[:, None] * lg[None, :])
    stdec = np.exp(DEC_SEQ * lg).reshape(4, 2).T.repeat(HD, 0)
    bmask = (np.arange(NS)[:, None] // 8 == np.arange(8)[None, :])
    q, k = np.arange(P)[:, None], np.arange(2 * P)[None, :]
    maskp = np.concatenate([np.where(k[:, :P] <= q, 0.0, NEG), np.where(k <= q + P, 0.0, NEG)], 1)
    row, own = np.arange(NS) % 8, np.arange(NS)
    masks = np.where((own[None, None, :] // 8 == np.arange(8)[None, :, None])
                     & (own[None, None, :] % 8 <= row[:, None, None]), 0.0, NEG)
    before = np.broadcast_to(np.arange(8)[None, :] < np.arange(8)[:, None], (NS, 8, 8))
    reset = np.ones((SSM_HEADS, NT))
    reset[:, SEQ::DEC_SEQ] = 0.0
    out = dict(cos=cos, sin=sin, dmat=dmat, kdec=by_tile(kdec), qdec=qdec, stdec=stdec, bmask=bmask, maskp=maskp,
               masks=masks, before=before, causal=ok, reset=reset, ident=np.eye(P), ones=np.ones((P, P)))
    return {k: np.ascontiguousarray(v).astype(f) for k, v in out.items()}


class Own:

    def __init__(self, eng, sem):
        self.eng, self.sem, self.base, self.n, self.others = eng, sem, 0, 0, []

    def __call__(self, ins):
        ins.then_inc(self.sem, 1)
        self.n += 1

    def step_to(self, ins, sem, value):
        ins.then_inc(sem, 1)
        self.others = [(s, v) for s, v in self.others if s is not sem] + [(sem, value)]

    def settle(self):
        for sem, value in self.others:
            self.eng.wait_ge(sem, value)
        self.others = []
        if not (isinstance(self.base, int) and self.base + self.n == 0):
            self.eng.wait_ge(self.sem, self.base + self.n)

    def turn(self, i, start, steps):
        self.before_loop = self.base + self.n
        self.base, self.n, self.steps = self.before_loop + (i - start) * steps, 0, steps

    def end(self, turns):
        assert self.n == self.steps, f"the loop's body takes {self.n} steps"
        self.base, self.n = self.before_loop + turns * self.steps, 0


def build(nc, d):
    with ExitStack() as ctx:
        def sb(name, shape, dt=F32):
            return ctx.enter_context(nc.sbuf_tensor(name, shape, dt))

        sems = {}

        def sem(name):
            if name not in sems:
                sems[name] = ctx.enter_context(nc.semaphore(name))
            return sems[name]

        ring = sb("ring", [P, N_SLOTS, SLOT])
        hT = sb("hT", [P, KC, NT])
        xnT = sb("xnT", [P, KC, NTP])
        catT = sb("catT", [P, 12, NT])
        arena = sb("arena", [P, 17200])
        ident = sb("ident", [P, P])
        ones = sb("ones", [P, P])
        cos, sin = sb("cos", [P, 3, HD]), sb("sin", [P, 3, HD])
        qg, kg = sb("qg", [P, HD]), sb("kg", [P, HD])
        g_mix, g_ffn = sb("g_mix", [P, 2, KC]), sb("g_ffn", [P, 2, KC])
        kdec = sb("kdec", [P, 3, HEADS])
        qdec = sb("qdec", [NS, HEADS])
        stdec = sb("stdec", [P, 4])
        bmask = sb("bmask", [NS, 8])
        small = sb("small", [P, 256])
        eps = sb("eps", [P, 1])
        wr = sb("wr", [P, 2, KC, MOE_GROUPS + N_EXPERTS])
        cs_dram, e_dram, el_dram = (nc.dram_tensor(n, [SSM_HEADS, w], F32).ap()
                                    for n, w in (("cs_rows_dram", NT), ("e_rows_dram", NS), ("e_last_dram", 8)))
        gate_dram = nc.dram_tensor("gate_rows", [2, N_EXPERTS, NT], F32).ap()
        pages = sb("pages", [1, DEC_BATCH * N_PAGES], I32)
        bank = [ctx.enter_context(nc.psum_tensor(f"bank{i}", [P, 512], F32)) for i in range(8)]

        def part(off, *shape, of=arena):
            n = int(np.prod(shape))
            v = of[:, off:off + n]
            names = "abcd"[:len(shape)]
            return v.rearrange(f"p ({' '.join(names)}) -> p {' '.join(names)}", **dict(zip(names[1:], shape[1:])))

        xn_flat = xnT[:, :, :].rearrange("p a b -> p (a b)")
        cat_flat = catT[:, :, :].rearrange("p a b -> p (a b)")
        slot_k = [ring[:, s, :].rearrange("p (k n) -> p k n", k=KC) for s in range(N_SLOTS)]
        slot_f = [ring[:, s, :].rearrange("p (f n) -> p f n", f=FC) for s in range(N_SLOTS)]

        x_tok = part(0, 3, D_MODEL)
        sq_all = part(14000, KC * NT)
        rs_all = part(16600, NT)
        q_tok = {"rq": part(0, 3, 512), "rk": part(1536, 3, 512), "mq": part(3072, 3, 512),
                 "mk": part(4608, 3, 512), "mv": part(6144, 3, 512), "rv": part(7680, 3, 1024)}
        rqT, rkT, mqT, mkT = (part(10752 + 1280 * i, 4, NT) for i in range(4))
        rope_a, rope_b = part(10752, 3, 512), part(10752 + 1536, 3, 512)
        q_dec = part(14592, 512)
        dmat = part(15872, 2, TRI)
        st = [part(0, 8, DV), part(3072, 8, DV)]
        ret_p = part(4096, 4, DV)
        qdT = part(0, 4, NS, of=xn_flat)
        sc_sb = part(256, 2, TRI, of=xn_flat)
        rv_bd = part(1152, 8, DV, of=xn_flat)
        ro_sq = part(2176, NT, of=xn_flat)
        ro_rs = part(2496, NT, of=xn_flat)
        pm_s = part(0, 2, 3 * P, of=xn_flat)
        pm_T = part(768, 2, 3 * P, of=xn_flat)
        maskp = part(1536, 3 * P, of=xn_flat)

        def causal_parts(t):
            return t[:, 0:3 * P], t[0:NS, 3 * P:TRI]

        block = ctx.enter_context(nc.Block())

        def load_slot(sp, s, src, cols=None):
            k = src.shape[0] // P
            dst = ring[:, s, 0:k * src.shape[1]].rearrange("p (k n) -> p k n", k=k)
            sp.dma_start(dst, src.rearrange("(k p) n -> p k n", p=P)).then_inc(sem(f"slot{s}_loaded"), 16)

        def slot_loaded(pe, s, use):
            pe.wait_ge(sem(f"slot{s}_loaded"), 16 * use)

        def even_weights(sp):
            for n, c in enumerate(EVEN_COLS):
                if n >= N_SLOTS:
                    sp.wait_ge(sem("proj_done"), 3 * (n - N_SLOTS + 1))
                load_slot(sp, n % N_SLOTS, d["w_in_even"][0][:, c:c + 512])
            for n in range(3):
                s = 3 + n
                sp.wait_ge(sem("proj_done"), 3 * (s + 1))
                load_slot(sp, s, d["w_out_even"][0][512 * n:512 * n + 512, :])

        def norm_act(act, own, k, ready):
            ready(act)
            own.step_to(act.activation(sq_all, hT[:, :, :].rearrange("p a b -> p (a b)"), ACT.Square), sem("norm_sq"), k + 1)
            act.wait_ge(sem("norm_sum"), k + 1)
            own.step_to(act.activation(rs_all, bank[0][:, 0:NT], ACT.Sqrt, bias=eps[:, :], scale=1.0 / D_MODEL),
                       sem("norm_root"), k + 1)

        def norm_pe(pe, k):
            pe.wait_ge(sem("norm_sq"), k + 1)
            for c in range(KC):
                mm = pe.matmul(bank[0][:, 0:NT], ones[:, :], sq_all[:, NT * c:NT * c + NT], start=(c == 0), stop=(c == KC - 1))
            mm.then_inc(sem("norm_sum"), 1)

        def norm_dve(dve, own, k, gain):
            own(dve.memset(xnT[:, :, NT:NTP], 0.0))
            dve.wait_ge(sem("norm_root"), k + 1)
            own(dve.reciprocal(rs_all, rs_all))
            own.settle()
            for c in range(KC):
                ins = dve.scalar_tensor_tensor(out=xnT[:, c, 0:NT], in0=hT[:, c, :], scalar=gain[:, c:c + 1],
                                               in1=rs_all, op0=ALU.mult, op1=ALU.mult)
                if c < KC - 1:
                    own(ins)
            own.step_to(ins, sem("xn_ready"), k + 1)

        def transpose_x_pe(pe):
            pe.wait_ge(sem("x_loaded"), 48)
            pe.wait_ge(sem("consts_loaded"), 16 * N_CONSTS)
            for c in range(KC):
                for t, n in ((0, P), (1, P), (2, NS)):
                    mm = pe.transpose(bank[c][:, P * t:P * t + n], x_tok[0:n, t, P * c:P * c + P], ident[0:n, 0:n])
                mm.then_inc(sem("x_turned"), 1)

        def transpose_x_dve(dve, own):
            for c in range(KC):
                dve.wait_ge(sem("x_turned"), c + 1)
                own.step_to(dve.tensor_copy(hT[:, c, :], bank[c][:, 0:NT]), sem("h_ready"), c + 1)
            own.settle()

        PROJ_BANKS = 4

        def even_proj_pe(pe):
            pe.wait_ge(sem("xn_ready"), 1)
            idx = 0
            for n in range(7):
                slot_loaded(pe, n % N_SLOTS, n // N_SLOTS + 1)
                for t in range(3):
                    if idx >= PROJ_BANKS:
                        pe.wait_ge(sem("proj_taken"), idx - PROJ_BANKS + 1)
                    b = bank[1 + idx % PROJ_BANKS]
                    for k in range(KC):
                        mm = pe.matmul(b[:, :], xnT[:, k, P * t:P * t + P], slot_k[n % N_SLOTS][:, k, :],
                                       start=(k == 0), stop=(k == KC - 1))
                    mm.then_inc(sem("proj_done"), 1)
                    idx += 1
            for c in range(8):
                n = 7 + c // 4
                slot_loaded(pe, n % N_SLOTS, n // N_SLOTS + 1)
                pe.wait_ge(sem("proj_taken"), idx - PROJ_BANKS + 1)
                b = bank[1 + idx % PROJ_BANKS]
                for k in range(KC):
                    mm = pe.matmul(b[:, 0:NT], slot_k[n % N_SLOTS][:, k, P * (c % 4):P * (c % 4) + P], xnT[:, k, 0:NT],
                                   start=(k == 0), stop=(k == KC - 1))
                mm.then_inc(sem("proj_done"), 1)
                idx += 1

        def even_proj_act(act, own):
            dests = [(q_tok[x], 0) for x in ("rq", "rk", "mq", "mk", "mv", "rv")] + [(q_tok["rv"], 512)]
            roots = {2: 0, 3: 1}
            idx = 0
            for n, (dst, c0) in enumerate(dests):
                for t in range(3):
                    act.wait_ge(sem("proj_done"), idx + 1)
                    own.step_to(act.copy(dst[:, t, c0:c0 + 512], bank[1 + idx % PROJ_BANKS][:, :]), sem("proj_taken"), idx + 1)
                    idx += 1
            for i in range(2):
                act.wait_ge(sem("qk_sums"), i + 1)
                own.step_to(act.activation(small[:, 24 * i:24 * i + 24], small[:, 24 * i:24 * i + 24], ACT.Sqrt,
                                          bias=eps[:, :], scale=1.0 / HD), sem("qk_roots"), i + 1)
            for c in range(8):
                act.wait_ge(sem("proj_done"), idx + 1)
                own.step_to(act.activation(catT[:, c, :], bank[1 + idx % PROJ_BANKS][:, 0:NT], ACT.Silu), sem("proj_taken"), idx + 1)
                idx += 1

        def heads(x):
            return x.rearrange("p t (h e) -> p t h e", h=HEADS)

        def even_rope_dve(dve, own):
            H2 = HD // 2
            over = lambda table: table.unsqueeze(2).to_broadcast([P, 3, HEADS, table.shape[2]])

            def rope(x, k):
                xh, a, b = heads(x), heads(rope_a), heads(rope_b)
                own.settle()
                own(dve.tensor_tensor(a, xh, over(cos[:, :, :]), ALU.mult))
                own(dve.tensor_tensor(b[:, :, :, 0:H2], xh[:, :, :, H2:HD], over(sin[:, :, 0:H2]), ALU.mult))
                own(dve.tensor_tensor(b[:, :, :, H2:HD], xh[:, :, :, 0:H2], over(sin[:, :, H2:HD]), ALU.mult))
                own.settle()
                own.step_to(dve.tensor_tensor(x, rope_a, rope_b, ALU.add), sem("roped"), k)

            def head_sums(x, i):
                own.settle()
                own(dve.tensor_tensor(rope_a, x, x, ALU.mult))
                own.settle()
                own.step_to(dve.tensor_reduce(small[:, 24 * i:24 * i + 24].rearrange("p (t h) -> p t h", t=3),
                                             heads(rope_a), AX_X, ALU.add), sem("qk_sums"), i + 1)
                own.settle()

            def qk_norm(x, i, gain):
                dve.wait_ge(sem("qk_roots"), i + 1)
                r = small[:, 24 * i:24 * i + 24]
                own(dve.reciprocal(r, r))
                own.settle()
                own(dve.tensor_tensor(heads(x), heads(x), r.rearrange("p (t h) -> p t h", t=3).unsqueeze(3)
                                      .to_broadcast([P, 3, HEADS, HD]), ALU.mult))
                own.settle()
                own(dve.tensor_tensor(heads(x), heads(x), gain[:, :].unsqueeze(1).unsqueeze(1)
                                      .to_broadcast([P, 3, HEADS, HD]), ALU.mult))

            dve.wait_ge(sem("proj_taken"), 3)
            rope(q_tok["rq"], 1)
            dve.wait_ge(sem("proj_taken"), 6)
            rope(q_tok["rk"], 2)
            dve.wait_ge(sem("proj_taken"), 9)
            head_sums(q_tok["mq"], 0)
            dve.wait_ge(sem("proj_taken"), 12)
            head_sums(q_tok["mk"], 1)
            qk_norm(q_tok["mq"], 0, qg)
            rope(q_tok["mq"], 3)
            qk_norm(q_tok["mk"], 1, kg)
            rope(q_tok["mk"], 4)
            own.step_to(dve.tensor_tensor(q_dec[0:NS, :].rearrange("p (h e) -> p h e", h=HEADS),
                                         heads(q_tok["rq"])[0:NS, 2, :, :],
                                         qdec[:, :].unsqueeze(2).to_broadcast([NS, HEADS, HD]), ALU.mult), sem("roped"), 5)
            own.settle()

        TURNS = [("rq", j) for j in range(4)] + [("rk", j) for j in range(4)] + [("mq", j) for j in range(4)] \
            + [("dec", 0)] + [("mk", j) for j in range(4)]
        TURN_OF = {"rq": (1, rqT), "rk": (2, rkT), "mq": (3, mqT), "mk": (4, mkT)}

        def even_turn_pe(pe):
            for r, (x, j) in enumerate(TURNS):
                if r >= 2:
                    pe.wait_ge(sem("turn_taken"), r - 1)
                b = bank[5 + r % 2]
                if x == "dec":
                    pe.wait_ge(sem("roped"), 5)
                    for jj in range(4):
                        mm = pe.transpose(b[:, NS * jj:NS * jj + NS], q_dec[0:NS, P * jj:P * jj + P], ident[0:NS, 0:NS])
                else:
                    pe.wait_ge(sem("roped"), 5)
                    for t, n in ((0, P), (1, P), (2, NS)):
                        mm = pe.transpose(b[:, P * t:P * t + n], q_tok[x][0:n, t, P * j:P * j + P], ident[0:n, 0:n])
                mm.then_inc(sem("turned"), 1)

        def even_turn_act(act, own):
            act.wait_ge(sem("proj_done"), 29)
            for r, (x, j) in enumerate(TURNS):
                act.wait_ge(sem("turned"), r + 1)
                b = bank[5 + r % 2]
                if x == "dec":
                    ins = act.copy(qdT, b[:, 0:4 * NS].rearrange("p (j t) -> p j t", j=4))
                else:
                    if x == "mk" and j == 0:
                        act.wait_ge(sem("turned"), 13)
                    ins = act.copy(TURN_OF[x][1][:, j, :], b[:, 0:NT])
                own.step_to(ins, sem("turn_taken"), r + 1)

        def rows(h):
            return slice(HD * (h % 2), HD * (h % 2) + HD)

        def retention_pe(pe):
            rv, rk = q_tok["rv"], q_tok["rk"]

            def scores(h):
                if h >= 2:
                    pe.wait_ge(sem("ret_scaled"), h - 1)
                b, r, j = bank[h % 2], rows(h), h // 2
                pe.matmul(b[:, 0:2 * P], rkT[r, j, 0:P], rqT[r, j, 0:2 * P], start=True, stop=True)
                pe.matmul(b[:, 2 * P:3 * P], rkT[r, j, P:2 * P], rqT[r, j, P:2 * P], start=True, stop=True)
                pe.matmul(b[0:NS, 3 * P:TRI], rkT[r, j, 2 * P:NT], rqT[r, j, 2 * P:NT], start=True, stop=True)\
                    .then_inc(sem("ret_scores"), 1)

            def outputs(h):
                pe.wait_ge(sem("ret_scaled"), h + 1)
                if h >= 2:
                    pe.wait_ge(sem("ret_out"), h - 1)
                if h % 2 == 0:
                    pe.wait_ge(sem(f"st{h // 2 % 2}_loaded"), 16 * (h // 4 + 1))
                b, s, v = bank[2 + h % 2], sc_sb[:, h % 2, :], slice(DV * h, DV * h + DV)
                pe.matmul(b[:, 0:2 * P], rv[:, 0, v], s[:, 0:2 * P], start=True, stop=False)
                pe.matmul(b[:, P:2 * P], rv[:, 1, v], s[:, 2 * P:3 * P], start=False, stop=True)
                mm = pe.matmul(b[:, 2 * P:NT], rv[0:NS, 2, v], s[0:NS, 3 * P:TRI], start=True, stop=False)
                if h % 2 == 1:
                    mm.then_inc(sem("ret_own_done"), 1)
                    pe.wait_ge(sem("ret_own_done"), h // 2 + 1)
                for n in range(DEC_BATCH):
                    at = slice(2 * P + 8 * n, 2 * P + 8 * n + 8)
                    mm = pe.matmul(b[:, at], st[h // 2 % 2][rows(h), n, :], qdT[rows(h), h // 2, 8 * n:8 * n + 8],
                                   start=False, stop=(n == DEC_BATCH - 1))
                mm.then_inc(sem("ret_o"), 1)

            def states(h):
                if h == 0:
                    pe.wait_ge(sem("k_decayed"), 1)
                kd = slice(HD * h, HD * h + HD)
                if h % 2 == 0 and h >= 2:
                    pe.wait_ge(sem("ret_p_taken"), h // 2)
                    pe.wait_ge(sem("st_updated"), h // 2)
                pe.matmul(bank[5][rows(h), 0:DV], rk[:, 0, kd], rv[:, 0, DV * h:DV * h + DV], start=True, stop=False)
                pe.matmul(bank[5][rows(h), 0:DV], rk[:, 1, kd], rv[:, 1, DV * h:DV * h + DV], start=False, stop=True)\
                    .then_inc(sem("ret_p_state"), 1)
                pe.wait_ge(sem("rv_spread"), h + 1)
                for half in range(2):
                    mm = pe.matmul(bank[6 + half][rows(h), :], rk[0:NS, 2, kd],
                                   rv_bd[0:NS, 4 * half:4 * half + 4, :], start=True, stop=True)
                mm.then_inc(sem("ret_s_state"), 1)

            def sums(h):
                pe.wait_ge(sem("ret_sq"), h + 1)
                if h >= 1:
                    pe.wait_ge(sem("ret_root"), h)
                pe.matmul(bank[4][:, 0:NT], ones[:, :], ro_sq, start=True, stop=True).then_inc(sem("ret_sum"), 1)

            pe.wait_ge(sem("turn_taken"), len(TURNS))
            scores(0)
            for h in range(HEADS):
                if h + 1 < HEADS:
                    scores(h + 1)
                outputs(h)
                states(h)
                if h:
                    sums(h - 1)
            sums(HEADS - 1)

        def retention_dve(dve, own):
            rk, rv = q_tok["rk"], q_tok["rv"]
            dve.wait_ge(sem("turned"), 8)
            own.step_to(dve.tensor_tensor(heads(rk), heads(rk), kdec[:, :, :].unsqueeze(3).to_broadcast([P, 3, HEADS, HD]),
                                         ALU.mult), sem("k_decayed"), 1)

            def scale(h):
                dve.wait_ge(sem("ret_scores"), h + 1)
                dve.wait_ge(sem(f"dmat{h % 2}_loaded"), 16 * (h // 2 + 1))
                if h >= 2:
                    dve.wait_ge(sem("ret_o"), h - 1)
                (bp, bs), (dp, ds), (sp_, ss) = (causal_parts(x) for x in (bank[h % 2], dmat[:, h % 2, :], sc_sb[:, h % 2, :]))
                own(dve.tensor_tensor(sp_, bp, dp, ALU.mult))
                own.step_to(dve.tensor_tensor(ss, bs, ds, ALU.mult), sem("ret_scaled"), h + 1)

            def spread(h):
                if h:
                    dve.wait_ge(sem("ret_s_state"), h)
                own.step_to(dve.tensor_tensor(rv_bd[0:NS, :, :],
                                             rv[0:NS, 2, DV * h:DV * h + DV].unsqueeze(1).to_broadcast([NS, 8, DV]),
                                             bmask[:, :].unsqueeze(2).to_broadcast([NS, 8, DV]), ALU.mult),
                           sem("rv_spread"), h + 1)

            def update(p):
                dve.wait_ge(sem("ret_s_state"), 2 * p + 2)
                for half in range(2):
                    s = st[p % 2][:, 4 * half:4 * half + 4, :].rearrange("p a b -> p (a b)")
                    ins = dve.scalar_tensor_tensor(out=s, in0=s, scalar=stdec[:, p:p + 1], in1=bank[6 + half][:, :],
                                                   op0=ALU.mult, op1=ALU.add)
                    if half == 0:
                        own(ins)
                own.step_to(ins, sem("st_updated"), p + 1)

            def out(h):
                dve.wait_ge(sem("ret_root"), h + 1)
                own(dve.reciprocal(ro_rs, ro_rs))
                own.settle()
                own(dve.tensor_tensor(ro_sq, bank[2 + h % 2][:, 0:NT], ro_rs, ALU.mult))
                own.settle()
                own.step_to(dve.tensor_tensor(catT[:, h, :], catT[:, h, :], ro_sq, ALU.mult), sem("ret_out"), h + 1)

            for h in range(HEADS):
                if h == 0:
                    dve.wait_ge(sem("proj_done"), 29)
                scale(h)
                spread(h)
                if h >= 2 and h % 2 == 0:
                    update(h // 2 - 1)
                if h:
                    if h == 1:
                        dve.wait_ge(sem("proj_taken"), 29)
                    out(h - 1)
            update(3)
            out(HEADS - 1)
            own.settle()

        def retention_act(act, own):
            for h in range(HEADS):
                act.wait_ge(sem("ret_o"), h + 1)
                if h:
                    act.wait_ge(sem("ret_out"), h)
                own.step_to(act.activation(ro_sq, bank[2 + h % 2][:, 0:NT], ACT.Square), sem("ret_sq"), h + 1)
                if h % 2 == 1:
                    act.wait_ge(sem("ret_p_state"), h + 1)
                    own.step_to(act.copy(ret_p[:, h // 2, :], bank[5][:, 0:DV]), sem("ret_p_taken"), h // 2 + 1)
                act.wait_ge(sem("ret_sum"), h + 1)
                own.step_to(act.activation(ro_rs, bank[4][:, 0:NT], ACT.Sqrt, bias=eps[:, :], scale=1.0 / DV),
                           sem("ret_root"), h + 1)

        def retention_pool(pool):
            def load_state(p):
                if p < 2:
                    pool.wait_ge(sem("turned"), [13, 13][p])
                    pool.wait_ge(sem("turn_taken"), 12)
                else:
                    pool.wait_ge(sem(f"st{p % 2}_stored"), 16)
                pool.dma_start(st[p % 2], d["state_ret"][0][:, 2 * p:2 * p + 2].rearrange("b h k v -> (h k) b v"))\
                    .then_inc(sem(f"st{p % 2}_loaded"), 16)

            load_state(0)
            load_state(1)
            for h in range(HEADS):
                if h >= 2:
                    pool.wait_ge(sem("ret_scaled"), h - 1)
                pool.dma_start(dmat[:, h % 2, :], d["c_dmat"][h]).then_inc(sem(f"dmat{h % 2}_loaded"), 16)
                if h >= 3 and h % 2 == 1:
                    store_state(pool, h // 2 - 1)
                    if h // 2 + 1 < 4:
                        load_state(h // 2 + 1)
            store_state(pool, 3)
            pool.wait_ge(sem("ret_p_taken"), 4)
            pool.dma_start(d["ret_prompt"][0, 0].rearrange("(j h) k v -> (h k) j v", h=2), ret_p)\
                .then_inc(sem("stored"), 16)

        def store_state(pool, p):
            pool.wait_ge(sem("st_updated"), p + 1)
            pool.dma_start(d["ret_sample"][0][:, 2 * p:2 * p + 2].rearrange("b h k v -> (h k) b v"), st[p % 2])\
                .then_inc(sem(f"st{p % 2}_stored"), 16)

        def kv_pool(pool):
            for name, ready, n in (("k", "roped", 4), ("v", "proj_taken", 15)):
                pool.wait_ge(sem(ready), n)
                x = q_tok["m" + name]
                pool.dma_start(d[name + "_prompt"][0, 0].rearrange("(t p) h e -> p t (h e)", p=P), x[:, 0:2, :])\
                    .then_inc(sem("kv_stored"), 16)
                pool.dma_start(d[name + "_sample"][0].rearrange("b t h e -> (b t) (h e)"), x[0:NS, 2, :])\
                    .then_inc(sem("kv_stored"), 16)

        def prompt_attn_pe(pe):
            mv = q_tok["mv"]

            def scores(h):
                if h < 2:
                    pe.wait_ge(sem("ret_scaled"), HEADS)
                else:
                    pe.wait_ge(sem("pm_masked"), h - 1)
                b, r, j = bank[h % 2], rows(h), h // 2
                pe.matmul(b[:, 0:P], mqT[r, j, 0:P], mkT[r, j, 0:P], start=True, stop=True)
                pe.matmul(b[:, P:3 * P], mqT[r, j, P:2 * P], mkT[r, j, 0:2 * P], start=True, stop=True)\
                    .then_inc(sem("pm_scores"), 1)

            scores(0)
            scores(1)
            for h in range(HEADS):
                pe.wait_ge(sem("pm_probs"), h + 1)
                if h < 2:
                    pe.wait_ge(sem("ret_out"), HEADS)
                if h >= 2:
                    pe.wait_ge(sem("pm_T_taken"), h - 1)
                b = bank[2 + h % 2]
                for i in range(3):
                    mm = pe.transpose(b[:, P * i:P * i + P], pm_s[:, h % 2, P * i:P * i + P], ident[:, :])
                mm.then_inc(sem("pm_T"), 1)
                if h + 2 < HEADS:
                    scores(h + 2)
                pe.wait_ge(sem("pm_T_taken"), h + 1)
                if h in (0, 2):
                    pe.wait_ge(sem("ret_root"), HEADS)
                    pe.wait_ge(sem("ret_p_taken"), 4)
                if h >= 4 and h % 2 == 0:
                    pe.wait_ge(sem("pm_out"), h // 2 - 1)
                o, v, pT = bank[4 + h // 2 % 2], slice(HD * h, HD * h + HD), pm_T[:, h % 2, :]
                pe.matmul(o[rows(h), 0:2 * P], mv[:, 0, v], pT[:, 0:2 * P], start=True, stop=False)
                pe.matmul(o[rows(h), P:2 * P], mv[:, 1, v], pT[:, 2 * P:3 * P], start=False, stop=True)\
                    .then_inc(sem("pm_o"), 1)

        def prompt_attn_dve(dve, own):
            def mask(h):
                dve.wait_ge(sem("pm_scores"), h + 1)
                if h == 0:
                    dve.wait_ge(sem("ret_o"), HEADS)
                    dve.wait_ge(sem("ret_s_state"), HEADS)
                    dve.wait_ge(sem("maskp_loaded"), 16)
                if h >= 2:
                    dve.wait_ge(sem("pm_T"), h - 1)
                s, m = pm_s[:, h % 2, :], small[:, 64 + 8 * (h % 2):72 + 8 * (h % 2)]
                own.step_to(dve.tensor_tensor(s, bank[h % 2][:, 0:3 * P], maskp, ALU.add), sem("pm_masked"), h + 1)
                own.settle()
                own(dve.tensor_reduce(m[:, 0:1], s[:, 0:P], AX_X, ALU.max))
                own(dve.tensor_reduce(m[:, 1:2], s[:, P:3 * P], AX_X, ALU.max))
                own.settle()
                own.step_to(dve.tensor_scalar(m[:, 2:4], m[:, 0:2], -QK_SCALE, None, ALU.mult), sem("pm_max"), h + 1)

            def probs(h):
                dve.wait_ge(sem("pm_exp"), h + 1)
                s, m = pm_s[:, h % 2, :], small[:, 64 + 8 * (h % 2):72 + 8 * (h % 2)]
                own(dve.reciprocal(m[:, 6:8], m[:, 4:6]))
                own.settle()
                own(dve.tensor_scalar(s[:, 0:P], s[:, 0:P], m[:, 6:7], None, ALU.mult))
                own.step_to(dve.tensor_scalar(s[:, P:3 * P], s[:, P:3 * P], m[:, 7:8], None, ALU.mult), sem("pm_probs"), h + 1)

            mask(0)
            for h in range(HEADS):
                if h + 1 < HEADS:
                    mask(h + 1)
                probs(h)
            own.settle()

        def prompt_attn_act(act, own):
            def exps(h):
                act.wait_ge(sem("pm_max"), h + 1)
                s, m = pm_s[:, h % 2, :], small[:, 64 + 8 * (h % 2):72 + 8 * (h % 2)]
                own(act.activation(s[:, 0:P], s[:, 0:P], ACT.Exp, bias=m[:, 2:3], scale=QK_SCALE, accum_out=m[:, 4:5]))
                own.step_to(act.activation(s[:, P:3 * P], s[:, P:3 * P], ACT.Exp, bias=m[:, 3:4], scale=QK_SCALE,
                                          accum_out=m[:, 5:6]), sem("pm_exp"), h + 1)

            exps(0)
            for h in range(HEADS):
                if h + 1 < HEADS:
                    exps(h + 1)
                act.wait_ge(sem("pm_T"), h + 1)
                if h >= 2:
                    act.wait_ge(sem("pm_o"), h - 1)
                own.step_to(act.copy(pm_T[:, h % 2, :], bank[2 + h % 2][:, 0:3 * P]), sem("pm_T_taken"), h + 1)
                if h % 2 == 1:
                    act.wait_ge(sem("pm_o"), h + 1)
                    own.step_to(act.copy(catT[:, 8 + h // 2, 0:SEQ], bank[4 + h // 2 % 2][:, 0:SEQ]), sem("pm_out"), h // 2 + 1)

        def load_consts(act):
            loads = [(ident[:, :], d["c_ident"]), (ones[:, :], d["c_ones"]), (cos[:, :, :], d["c_cos"]),
                     (sin[:, :, :], d["c_sin"]), (kdec[:, :, :], d["c_kdec"]), (qdec[:, :], d["c_qdec"]),
                     (stdec[:, :], d["c_stdec"]), (bmask[:, :], d["c_bmask"]),
                     (g_mix[:, :, :], d["norm_mix"]), (g_ffn[:, :, :], d["norm_ffn"]),
                     (qg[:, :], d["q_norm"].to_broadcast([P, HD])), (kg[:, :], d["k_norm"].to_broadcast([P, HD])),
                     (pages[:, :], d["page_table"].rearrange("b n -> (b n)").rearrange("(a n) -> a n", a=1))]
            assert len(loads) == N_CONSTS
            for dst, src in loads:
                act.dma_start(dst, src).then_inc(sem("consts_loaded"), 16)

        free1, free2 = ring[:, 1, :], ring[:, 2, :]
        k_pg = part(0, 2, 4, 512)
        v_pg = part(4096, 4, 4, 512)
        kT = part(12288, 2, 4, 512)
        own_kT = part(16384, 4, NS)
        own_v = part(16640, 512)
        q_diag = part(0, 8, 4, NS, of=xn_flat)
        pT = part(2048, N_PAGES, NS, of=xn_flat)
        sc_mask = part(0, 8, NS, of=free1)
        q_now = part(512, 4, NS, of=free1)
        s_own = part(768, 2, NS, of=free1)
        pT_own = part(896, NS, of=free1)
        before = part(960, 8, 8, of=free1)
        rank_a, rank_b = part(1024, 8, 8, of=free1), part(1088, 8, 8, of=free1)
        blk_sum = part(1152, 2, 8, of=free1)
        rank, blk_off = part(1168, 8, of=free1), part(1176, 8, of=free1)
        blk_max = part(1184, 16, of=free1)
        exp_off = part(1200, 2, 16, of=free1)
        exp_sum = part(1232, 2, 16, of=free1)
        probs = part(0, 2, PAST_LEN, of=free2)
        R = slice(0, NS)

        def sample_setup_dve(dve, own):
            dve.wait_ge(sem("pm_o"), HEADS)
            dve.wait_ge(sem("pm_T"), HEADS)
            own(dve.memset(q_diag, 0.0))
            own(dve.tensor_copy(own_kT, mkT[:, :, 2 * P:NT]))
            own(dve.tensor_copy(own_v[R, :], q_tok["mv"][R, 2, :]))
            own.settle()
            for h in range(HEADS):
                ins = dve.tensor_copy(q_diag[rows(h), :, h // 2, 8 * h:8 * h + 8],
                                      mqT[rows(h), h // 2, 2 * P:NT].rearrange("p (b t) -> p b t", t=DEC_SEQ))
                if h < HEADS - 1:
                    own(ins)
            own.step_to(ins, sem("sm_ready"), 1)
            own.settle()

        def pages_sp(sp):
            def load(cache, dst, b, q, s):
                for k in range(4):
                    page = sp.value_load(pages[0:1, bass.ds(16 * b + 4 * q + k, 1)], min_val=0, max_val=d["cache_k"].shape[1] - 1)
                    sp.dma_start(dst[:, k, :], d[cache][0][bass.ds(page, 1)].rearrange("a s h e -> s (a h e)"))\
                        .then_inc(sem(s), 16)

            def keys(b, q):
                if not (isinstance(b, int) and 4 * b + q < 2):
                    sp.wait_ge(sem("kt_turned"), 16 * b + 4 * q - 4)
                load("cache_k", k_pg[:, q % 2], b, q, f"k{q % 2}_loaded")

            def values(b):
                if not (isinstance(b, int) and b == 0):
                    sp.wait_ge(sem("sm_o"), b)
                for q in range(4):
                    load("cache_v", v_pg[:, q], b, q, "v_loaded")

            sp.wait_ge(sem("consts_loaded"), 16 * N_CONSTS)
            sp.wait_ge(sem("sm_ready"), 1)
            sp.wait_ge(sem("stored"), 16)
            sp.wait_ge(sem("kv_stored"), 64)
            sp.wait_ge(sem("st0_stored"), 32)
            sp.wait_ge(sem("st1_stored"), 32)
            keys(0, 0)
            keys(0, 1)

            def turn(b, last=False):
                keys(b, 2)
                keys(b, 3)
                if not last:
                    keys(b + 1, 0)
                    keys(b + 1, 1)
                values(b)

            turn(0)
            with sp.Fori(1, DEC_BATCH - 1) as b:
                turn(b)
            turn(DEC_BATCH - 1, last=True)

        def over_samples(eng, own, turn, steps):
            turn(0, 0, first=True)
            turn(1, 1)
            with eng.Fori(1, DEC_BATCH // 2) as i:
                if own:
                    own.turn(i, 1, steps)
                turn(2 * i, 0)
                turn(2 * i + 1, 1)
                if own:
                    own.end(DEC_BATCH // 2 - 1)
            turn(DEC_BATCH, 0, last=True)

        def wait_pos(eng, s, value):
            if not (isinstance(value, int) and value <= 0):
                eng.wait_ge(sem(s), value)

        def sample_attn_pe(pe):
            def turn_keys(b, q):
                pe.wait_ge(sem(f"k{q % 2}_loaded"), 64 * (2 * b + q // 2 + 1))
                for j in range(4):
                    wait_pos(pe, ["kt_taken_a", "kt_taken_d"][j % 2], 8 * b + 2 * q + j // 2)
                    for k in range(4):
                        mm = pe.transpose(bank[j % 2][:, P * k:P * k + P], k_pg[:, q % 2, k, P * j:P * j + P], ident[:, :])
                    mm.then_inc(sem("kt_turned"), 1)

            def scores(b, q):
                pe.wait_ge(sem("kt_taken_a"), 8 * b + 2 * q + 2)
                pe.wait_ge(sem("kt_taken_d"), 8 * b + 2 * q + 2)
                wait_pos(pe, "s_taken", 4 * b + q - 1)
                if q == 0:
                    pe.wait_ge(sem("q_now_set"), b + 1)
                for j in range(4):
                    mm = pe.matmul(bank[2 + q % 2][R, :], q_now[:, j, :], kT[:, q % 2, j, :], start=(j == 0), stop=(j == 3))
                mm.then_inc(sem("s_done"), 1)

            def own_scores(b):
                wait_pos(pe, "own_taken", b)
                wait_pos(pe, "sm_out", b - 1)
                for j in range(4):
                    mm = pe.matmul(bank[4][R, 0:NS], q_now[:, j, :], own_kT[:, j, :], start=(j == 0), stop=(j == 3))
                mm.then_inc(sem("own_done"), 1)

            def values(b, par):
                pe.wait_ge(sem("sm_ready"), 1)
                pe.wait_ge(sem("sm_p"), b + 1)
                for pg in range(N_PAGES):
                    pe.transpose(bank[5 + pg // 8][:, NS * (pg % 8):NS * (pg % 8) + NS], probs[R, par, PAGE * pg:PAGE * pg + PAGE],
                                 ident[R, R])
                pe.transpose(bank[7][R, 0:NS], s_own[R, par, :], ident[R, R]).then_inc(sem("p_turned"), 1)
                pe.wait_ge(sem("p_taken"), b + 1)
                pe.wait_ge(sem("v_loaded"), 256 * (b + 1))
                for j in range(4):
                    o, r = bank[7][:, 64 + 16 * j:80 + 16 * j], slice(16 * j, 16 * j + 16)
                    for pg in range(N_PAGES):
                        pe.matmul(o, v_pg[:, pg // 4, pg % 4, P * j:P * j + P], pT[:, pg, r], start=(pg == 0), stop=False)
                    mm = pe.matmul(o, own_v[R, P * j:P * j + P], pT_own[R, r], start=False, stop=True)
                mm.then_inc(sem("sm_o"), 1)

            def turn(b, par, first=False, last=False):
                if not last:
                    turn_keys(b, 0)
                    turn_keys(b, 1)
                    scores(b, 0)
                    turn_keys(b, 2)
                    scores(b, 1)
                    turn_keys(b, 3)
                    scores(b, 2)
                    scores(b, 3)
                    own_scores(b)
                if last:
                    pe.wait_ge(sem("sm_out"), DEC_BATCH - 1)
                if not first:
                    values(b - 1, 1 - par)

            pe.wait_ge(sem("sm_ready"), 1)
            pe.wait_ge(sem("pm_out"), 4)
            over_samples(pe, None, turn, 0)

        def sample_attn_act(act, own):
            def keys(b, q):
                wait_pos(act, "s_done", 4 * b + q - 1)
                for j in (0, 2):
                    act.wait_ge(sem("kt_turned"), 16 * b + 4 * q + j + 1)
                    act.copy(kT[:, q % 2, j, :], bank[0][:, :]).then_inc(sem("kt_taken_a"), 1)

            def scores(b, q, par):
                act.wait_ge(sem("s_done"), 4 * b + q + 1)
                if q == 0:
                    wait_pos(act, "p_turned", b - 1)
                for half in range(2):
                    n = 2 * q + half
                    ins = act.activation(probs[R, par, BLOCK * n:BLOCK * n + BLOCK],
                                         bank[2 + q % 2][R, BLOCK * half:BLOCK * half + BLOCK], ACT.Identity,
                                         accum_out=blk_sum[R, par, n:n + 1])
                    if half == 0:
                        own(ins)
                ins.then_inc(sem("s_taken"), 1)

            def exps(b, par):
                act.wait_ge(sem("sm_max"), b + 1)
                for n in range(N_BLOCKS):
                    p = probs[R, par, BLOCK * n:BLOCK * n + BLOCK]
                    own(act.activation(p, p, ACT.Exp, bias=exp_off[R, par, n:n + 1], scale=QK_SCALE,
                                       accum_out=exp_sum[R, par, n:n + 1]))
                act.activation(s_own[R, par, :], s_own[R, par, :], ACT.Exp, bias=exp_off[R, par, 8:9], scale=QK_SCALE,
                               accum_out=exp_sum[R, par, 8:9]).then_inc(sem("sm_exp"), 1)

            def turned(b):
                act.wait_ge(sem("p_turned"), b + 1)
                for half in range(2):
                    own(act.copy(pT[:, 8 * half:8 * half + 8, :], bank[5 + half][:, :].rearrange("p (a r) -> p a r", a=8)))
                act.copy(pT_own[R, :], bank[7][R, 0:NS]).then_inc(sem("p_taken"), 1)

            def turn(b, par, first=False, last=False):
                if not last:
                    keys(b, 0)
                    keys(b, 1)
                    scores(b, 0, par)
                if not first:
                    exps(b - 1, 1 - par)
                if not last:
                    keys(b, 2)
                    scores(b, 1, par)
                    keys(b, 3)
                    scores(b, 2, par)
                    scores(b, 3, par)
                if not first:
                    turned(b - 1)

            act.wait_ge(sem("sm_ready"), 1)
            over_samples(act, own, turn, 2 * (4 + 8 + 2))

        def sample_attn_dve(dve, own):
            def set_queries(b):
                wait_pos(dve, "own_done", b)
                dve.tensor_scalar(q_now, q_diag[:, bass.ds(b, 1), :, :].rearrange("p a j r -> p (a j) r"), 1.0, None,
                                  ALU.mult).then_inc(sem("q_now_set"), 1)

            def keys(b, q):
                wait_pos(dve, "s_done", 4 * b + q - 1)
                for j in (1, 3):
                    dve.wait_ge(sem("kt_turned"), 16 * b + 4 * q + j + 1)
                    dve.tensor_copy(kT[:, q % 2, j, :], bank[1][:, :]).then_inc(sem("kt_taken_d"), 1)

            def maxima(b, par):
                dve.wait_ge(sem("own_done"), b + 1)
                dve.tensor_tensor(s_own[R, par, :], bank[4][R, 0:NS],
                                  sc_mask[R, bass.ds(b, 1), :].rearrange("p a n -> p (a n)"), ALU.add).then_inc(sem("own_taken"), 1)
                dve.wait_ge(sem("s_taken"), 4 * b + 4)
                own(dve.tensor_reduce(blk_max[R, 0:8], probs[R, par, :].rearrange("p (n k) -> p n k", k=BLOCK), AX_X, ALU.max))
                g = blk_sum[R, par, :]
                theirs, mine = g.unsqueeze(1).to_broadcast([NS, 8, 8]), g.unsqueeze(2).to_broadcast([NS, 8, 8])
                own(dve.tensor_tensor(rank_a[R], theirs, mine, ALU.is_gt))
                own(dve.tensor_tensor(rank_b[R], theirs, mine, ALU.is_equal))
                own.settle()
                own(dve.tensor_tensor(rank_b[R], rank_b[R], before[R], ALU.mult))
                own.settle()
                own(dve.tensor_tensor(rank_a[R], rank_a[R], rank_b[R], ALU.add))
                dve.wait_ge(sem("own_taken"), b + 1)
                own(dve.tensor_reduce(blk_max[R, 8:9], s_own[R, par, :], AX_X, ALU.max))
                own.settle()
                own(dve.tensor_reduce(rank[R, :], rank_a[R], AX_X, ALU.add))
                own.settle()
                own(dve.tensor_scalar(blk_off[R, :], rank[R, :], float(TOPK), NEG, ALU.is_ge, ALU.mult))
                own.settle()
                own(dve.tensor_tensor(blk_max[R, 0:8], blk_max[R, 0:8], blk_off[R, :], ALU.add))
                own.settle()
                own(dve.tensor_reduce(blk_max[R, 9:10], blk_max[R, 0:9], AX_X, ALU.max))
                own.settle()
                own(dve.tensor_scalar(exp_off[R, par, 8:9], blk_max[R, 9:10], -QK_SCALE, None, ALU.mult))
                own.settle()
                dve.tensor_scalar(exp_off[R, par, 0:8], blk_off[R, :], QK_SCALE, exp_off[R, par, 8:9], ALU.mult, ALU.add)\
                    .then_inc(sem("sm_max"), 1)

            def normalise(b, par):
                dve.wait_ge(sem("sm_exp"), b + 1)
                own(dve.tensor_reduce(exp_sum[R, par, 9:10], exp_sum[R, par, 0:9], AX_X, ALU.add))
                own.settle()
                own(dve.reciprocal(exp_sum[R, par, 10:11], exp_sum[R, par, 9:10]))
                own.settle()
                own(dve.tensor_scalar(probs[R, par, :], probs[R, par, :], exp_sum[R, par, 10:11], None, ALU.mult))
                dve.tensor_scalar(s_own[R, par, :], s_own[R, par, :], exp_sum[R, par, 10:11], None, ALU.mult)\
                    .then_inc(sem("sm_p"), 1)

            def outputs(b):
                dve.wait_ge(sem("sm_o"), b + 1)
                o = bank[7][:, 64:128].rearrange("p (j g t) -> p j g t", j=4, g=2)
                for g in range(2):
                    r = slice(HD * g, HD * g + HD)
                    ins = dve.tensor_scalar(catT[r, 8:12, bass.ds(SEQ + DEC_SEQ * b, DEC_SEQ)], o[r, :, g, :], 1.0, None, ALU.mult)
                    if g == 0:
                        own(ins)
                ins.then_inc(sem("sm_out"), 1)

            def turn(b, par, first=False, last=False):
                if not last:
                    set_queries(b)
                    keys(b, 0)
                    keys(b, 1)
                if not first:
                    maxima(b - 1, 1 - par)
                if not last:
                    keys(b, 2)
                    keys(b, 3)
                if not first:
                    normalise(b - 1, 1 - par)
                    outputs(b - 1)

            dve.wait_ge(sem("masks_loaded"), 32)
            over_samples(dve, own, turn, 2 * 15)
            dve.wait_ge(sem("sm_out"), 8)

        def even_out_pe(pe):
            pe.wait_ge(sem("sm_out"), DEC_BATCH)
            for s in (3, 4, 5):
                slot_loaded(pe, s, 2)
            for c in range(KC):
                if c >= 4:
                    pe.wait_ge(sem("h_ready"), KC + c - 3)
                for k in range(12):
                    mm = pe.matmul(bank[c % 4][:, 0:NT], slot_f[3 + k // 4][:, k % 4, P * c:P * c + P], catT[:, k, :],
                                   start=(k == 0), stop=(k == 11))
                mm.then_inc(sem("even_out"), 1)

        def even_out_dve(dve, own):
            for c in range(KC):
                dve.wait_ge(sem("even_out"), c + 1)
                own.step_to(dve.tensor_tensor(hT[:, c, :], hT[:, c, :], bank[c % 4][:, 0:NT], ALU.add), sem("h_ready"), KC + c + 1)
            own.settle()

        gates = part(0, N_EXPERTS, NT)
        hid = part(5120, 2, FC, NT)
        sil = part(7680, 2, NT)
        gu = part(8320, 2, NT)
        logit = part(9000, 3, 20)
        ra, rb, rc, rd, re_, rf = (part(9100 + 12 * i, 3, 4) for i in range(6))
        r16 = part(9200, 3, 16)
        gate_tok = part(9260, 3, 16)
        r1 = [part(9320 + 3 * i, 3, 1) for i in range(8)]
        gate_T = part(9400, NT)

        def route_pe(pe, l):
            pe.wait_ge(sem("xn_ready"), 2 + 2 * l)
            pe.wait_ge(sem("wr_loaded"), 64)
            for t in range(3):
                for k in range(KC):
                    mm = pe.matmul(bank[0][:, 20 * t:20 * t + 20], xnT[:, k, P * t:P * t + P], wr[:, l, k, :],
                                   start=(k == 0), stop=(k == KC - 1))
            mm.then_inc(sem("routed"), 1)
            pe.wait_ge(sem("gate_tok_set"), l + 1)
            for t, n in ((0, P), (1, P), (2, NS)):
                mm = pe.transpose(bank[0][0:16, P * t:P * t + n], gate_tok[0:n, t, :], ident[0:n, 0:n])
            mm.then_inc(sem("gate_turned"), 1)

        def route_act(act, own, l):
            for i in range(2):
                act.wait_ge(sem("route_exp_in"), 2 * l + i + 1)
                own.step_to(act.activation(ra, ra, ACT.Exp), sem("route_exp"), 2 * l + i + 1)
            act.wait_ge(sem("gate_turned"), l + 1)
            own(act.copy(gate_T[0:16, :], bank[0][0:16, 0:NT]))
            own.settle()
            act.dma_start(gate_dram[l], gate_T[0:16, :]).then_inc(sem("gate_out"), 16)
            act.wait_ge(sem("gate_out"), 16 * (l + 1))
            act.dma_start(gates, gate_dram[l].rearrange("e n -> (e n)").rearrange("(a m) -> a m", a=1)
                          .to_broadcast([P, N_EXPERTS * NT]).rearrange("p (e n) -> p e n", e=N_EXPERTS))\
                .then_inc(sem("gates_loaded"), 16)

        def route_dve(dve, own, l):
            def step(ins):
                own(ins)
                own.settle()

            wide = lambda x, n=4: x.to_broadcast([P, 3, n])

            def first_hot(eq, rem):
                step(dve.tensor_scalar(rem, eq[:, :, 0:1], -1.0, 1.0, ALU.mult, ALU.add))
                for i in range(1, 4):
                    step(dve.tensor_tensor(eq[:, :, i:i + 1], eq[:, :, i:i + 1], rem, ALU.mult))
                    if i < 3:
                        step(dve.tensor_tensor(rem, rem, eq[:, :, i:i + 1], ALU.subtract))

            def shifted_exp(x, m, i):
                step(dve.tensor_reduce(m, x, AX_X, ALU.max))
                own.step_to(dve.tensor_tensor(ra, x, wide(m), ALU.subtract), sem("route_exp_in"), 2 * l + i + 1)

            def exp_sum_of(m, i):
                dve.wait_ge(sem("route_exp"), 2 * l + i + 1)
                step(dve.tensor_reduce(m, ra, AX_X, ALU.add))
                step(dve.reciprocal(m, m))

            dve.wait_ge(sem("routed"), l + 1)
            step(dve.tensor_copy(logit, bank[0][:, 0:60].rearrange("p (t n) -> p t n", t=3)))
            lg, le = logit[:, :, 0:4], logit[:, :, 4:20].rearrange("p t (g e) -> p t g e", g=4)
            mg, wg, rem, m2, v, v2, ts = r1[:7]
            step(dve.tensor_reduce(mg, lg, AX_X, ALU.max))
            step(dve.tensor_tensor(rb, lg, wide(mg), ALU.is_equal))
            shifted_exp(lg, wg, 0)
            first_hot(rb, rem)
            exp_sum_of(wg, 0)
            step(dve.tensor_tensor(r16.rearrange("p t (g e) -> p t g e", g=4), le,
                                   rb.unsqueeze(3).to_broadcast([P, 3, 4, 4]), ALU.mult))
            step(dve.tensor_reduce(rc, r16.rearrange("p t (g e) -> p t e g", g=4), AX_X, ALU.add))
            shifted_exp(rc, m2, 1)
            exp_sum_of(m2, 1)
            step(dve.tensor_tensor(rc, ra, wide(m2), ALU.mult))
            step(dve.tensor_reduce(v, rc, AX_X, ALU.max))
            step(dve.tensor_tensor(rd, rc, wide(v), ALU.is_equal))
            first_hot(rd, rem)
            step(dve.scalar_tensor_tensor(out=re_, in0=rd, scalar=-2.0, in1=rc, op0=ALU.mult, op1=ALU.add))
            step(dve.tensor_reduce(v2, re_, AX_X, ALU.max))
            step(dve.tensor_tensor(rf, re_, wide(v2), ALU.is_equal))
            first_hot(rf, rem)
            step(dve.tensor_tensor(rd, rd, rf, ALU.add))
            step(dve.tensor_tensor(rc, rc, rd, ALU.mult))
            step(dve.tensor_reduce(ts, rc, AX_X, ALU.add))
            step(dve.reciprocal(ts, ts))
            step(dve.tensor_tensor(ts, ts, wg, ALU.mult))
            step(dve.tensor_tensor(rc, rc, wide(ts), ALU.mult))
            own.step_to(dve.tensor_tensor(gate_tok.rearrange("p t (g e) -> p t g e", g=4),
                                         rb.unsqueeze(3).to_broadcast([P, 3, 4, 4]),
                                         rc.unsqueeze(2).to_broadcast([P, 3, 4, 4]), ALU.mult), sem("gate_tok_set"), l + 1)
            own.settle()

        def over_experts(eng, own, turn, steps):
            turn(0, 0, 0, first=True)
            turn(1, 1, 0)
            with eng.Fori(1, N_EXPERTS // 2) as i:
                if own:
                    own.turn(i, 1, steps)
                turn(2 * i, 0, i)
                turn(2 * i + 1, 1, i)
                if own:
                    own.end(N_EXPERTS // 2 - 1)
            turn(N_EXPERTS, 0, N_EXPERTS // 2, last=True)

        def slots_before(l, s):
            return 2 if l == 0 else 19 if s < 4 else 10

        UP, DN = FC * N_EXPERTS, KC * N_EXPERTS

        def experts_pe(pe, l):
            def gate_up(e, par, half, f):
                if f == 0:
                    for q in range(2):
                        slot_loaded(pe, 3 * par + q, slots_before(l, 3 * par + q) + half + 1)
                wait_pos(pe, "sil_done", 4 * e + f - 1 + UP * l)
                for q, b in ((0, bank[1 + f % 2]), (1, bank[3 + f % 2])):
                    if q == 1:
                        wait_pos(pe, "gu_done", 4 * e + f - 1 + UP * l)
                    for k in range(KC):
                        mm = pe.matmul(b[:, 0:NT], slot_k[3 * par + q][:, k, P * f:P * f + P], xnT[:, k, 0:NT],
                                       start=(k == 0), stop=(k == KC - 1))
                mm.then_inc(sem("gu_ready"), 1)

            def down(e, par, half):
                slot_loaded(pe, 3 * par + 2, slots_before(l, 3 * par + 2) + half + 1)
                pe.wait_ge(sem("hid_done"), 4 * e + 4 + UP * l)
                for c in range(KC):
                    wait_pos(pe, "acc_done", 8 * e + c - 3 + DN * l)
                    for f in range(FC):
                        mm = pe.matmul(bank[(5 + c % 4) % 8][:, 0:NT], slot_f[3 * par + 2][:, f, P * c:P * c + P],
                                       hid[:, par, f, :], start=(f == 0), stop=(f == FC - 1))
                    mm.then_inc(sem("down_done"), 1)

            def turn(e, par, half, first=False, last=False):
                if not last:
                    gate_up(e, par, half, 0)
                if not first:
                    down(e - 1, 1 - par, half if par else half - 1)
                if not last:
                    for f in range(1, FC):
                        gate_up(e, par, half, f)

            over_experts(pe, None, turn, 0)

        def experts_act(act, l):
            def turn(e, par, half, first=False, last=False):
                if not last:
                    for f in range(FC):
                        act.wait_ge(sem("gu_ready"), 4 * e + f + 1 + UP * l)
                        wait_pos(act, "gu_done", 4 * e + f - 1 + UP * l)
                        act.activation(sil[:, f % 2, :], bank[1 + f % 2][:, 0:NT], ACT.Silu).then_inc(sem("sil_done"), 1)

            over_experts(act, None, turn, 0)

        def experts_dve(dve, l):
            def hidden(e, par, f):
                dve.wait_ge(sem("sil_done"), 4 * e + f + 1 + UP * l)
                wait_pos(dve, "hid_done", 4 * e + f - 1 + UP * l)
                dve.tensor_tensor(gu[:, f % 2, :], sil[:, f % 2, :], bank[3 + f % 2][:, 0:NT], ALU.mult)\
                    .then_inc(sem("gu_done"), 1)
                dve.wait_ge(sem("gu_done"), 4 * e + f + 1 + UP * l)
                wait_pos(dve, "down_done", 8 * e - 8 + DN * l)
                dve.tensor_tensor(hid[:, par, f, :], gu[:, f % 2, :],
                                  gates[:, bass.ds(e, 1), :].rearrange("p a n -> p (a n)"), ALU.mult).then_inc(sem("hid_done"), 1)

            def turn(e, par, half, first=False, last=False):
                if not last:
                    hidden(e, par, 0)
                if not first:
                    for c in range(KC):
                        dve.wait_ge(sem("down_done"), 8 * (e - 1) + c + 1 + DN * l)
                        dve.tensor_tensor(hT[:, c, :], hT[:, c, :], bank[(5 + c % 4) % 8][:, 0:NT], ALU.add)\
                            .then_inc(sem("acc_done"), 1)
                if not last:
                    for f in range(1, FC):
                        hidden(e, par, f)

            dve.wait_ge(sem("gates_loaded"), 16 * (l + 1))
            over_experts(dve, None, turn, 0)
            dve.wait_ge(sem("acc_done"), 8 * N_EXPERTS + DN * l)

        def expert_piece(sp, l, e, par, q):
            w = d[["w_expert_gate", "w_expert_up", "w_expert_down"][q]][l][bass.ds(e, 1)].rearrange("a k n -> (a k) n")
            load_slot(sp, 3 * par + q, w)

        def experts_sp(sp, l):
            with sp.Fori(1, N_EXPERTS // 2) as i:
                for par in range(2):
                    e = 2 * i + par
                    sp.wait_ge(sem("gu_ready"), 4 * e - 4 + UP * l)
                    expert_piece(sp, l, e, par, 0)
                    expert_piece(sp, l, e, par, 1)
                    sp.wait_ge(sem("down_done"), 8 * e - 8 + DN * l)
                    expert_piece(sp, l, e, par, 2)

        y_tok = part(0, 3, D_MODEL)

        def finish_pe(pe, ready):
            ready(pe)
            for t, n in ((0, P), (1, P), (2, NS)):
                for half in range(2):
                    b = bank[2 * t + half]
                    for c in range(4):
                        mm = pe.transpose(b[0:n, P * c:P * c + P], hT[:, 4 * half + c, P * t:P * t + n], ident[:, :])
                    mm.then_inc(sem("y_turned"), 1)

        def finish_act(act, own):
            for t, n in ((0, P), (1, P), (2, NS)):
                for half in range(2):
                    act.wait_ge(sem("y_turned"), 2 * t + half + 1)
                    own(act.copy(y_tok[0:n, t, 512 * half:512 * half + 512], bank[2 * t + half][0:n, :]))
                own.settle()
                dst = d["y_prompt"][0][P * t:P * t + P, :] if t < 2 else d["y_sample"].rearrange("b t n -> (b t) n")
                act.dma_start(dst, y_tok[0:n, t, :]).then_inc(sem("y_stored"), 16)
            act.wait_ge(sem("y_stored"), 48)

        half1, half3 = ring[:, 1, SLOT // 2:], ring[:, 3, SLOT // 2:]
        slots45 = ring[:, 4:6, :].rearrange("p a b -> p (a b)")
        RAW = 3 + SEQ + DEC_BATCH * (3 + DEC_SEQ)
        raw = part(0, 4, RAW)
        conv = part(1400, 2, NT)
        xc = part(2040, 2, 4, NT)
        xdt, xtl = part(4600, 3, 256), part(5368, 3, 256)
        b_tok = part(6136, 3, D_STATE)
        cb = part(7544, TRI)
        cs_rows = part(7992, 2, 4, NT)
        wts = part(10552, 4, TRI)
        y_sb, y_sq, y_rs = part(12344, 2, NT), part(12984, 2, NT), part(13624, NT)
        tails = part(14000, 32, 27)
        p_st = part(14864, 2, 256)
        cin_tok = part(9800, 4096)
        dt_v, dt_e, dt_w, dt_l, dt_m, dt, cs, tail, dtl = (part(10552 + 330 * i, NT) for i in range(9))
        b_diag = part(0, 8, D_STATE, of=half1)
        cin = half1[:, 1024:1792].rearrange("p (c r) -> p c r", c=32)
        stT = half3[:, 0:2048].rearrange("p (c b n) -> p c b n", c=2, b=8)
        causal = part(15504, TRI)
        y_cat = part(0, 16, NT, of=slots45)
        stb = [[part(5120, 8, D_STATE, of=slots45), part(6144, 8, D_STATE, of=slots45)],
               [part(7168, 8, D_STATE, of=slots45), part(0, 8, D_STATE, of=cat_flat)]]
        z_s = part(1024, 2, 2, NT, of=cat_flat)
        e_rows = part(2304, 16, NS, of=cat_flat)
        e_last = part(3328, 16, 8, of=cat_flat)
        tok3 = part(3456, 3, 96, of=cat_flat)
        y_in = part(3744, NS, of=cat_flat)
        w_dt = small[:, :].rearrange("p (k n) -> p k n", k=KC)
        cos_flat, sin_flat = (x[:, :, :].rearrange("p a b -> p (a b)") for x in (cos, sin))
        cw = part(0, 32, CONV_W, of=cos_flat)
        cbias = part(128, 32, of=cos_flat)
        skip, gain = part(0, 16, of=sin_flat), part(16, 16, of=sin_flat)
        dtb, alog, aexp = (sin_flat[0:32, 32 + i:33 + i] for i in range(3))
        H = slice(0, SSM_HEADS)

        def odd_setup_pool(pool):
            pool.wait_ge(sem("sm_ready"), 1)
            for dst, src in ((w_dt, d["w_in_odd"][0][:, 6144:6176].rearrange("(k p) n -> p k n", p=P)), (cw, d["conv_w"]),
                             (cbias, d["conv_b"]), (gain, d["ssd_norm"]), (dtb, d["dt_bias"]), (alog, d["a_log"])):
                pool.dma_start(dst, src).then_inc(sem("odd_consts"), 16)
            for g in range(2):
                pool.dma_start(skip[HD * g:HD * g + HD], d["d_skip"][g:g + 1].to_broadcast([HD, 16])).then_inc(sem("odd_consts"), 16)
            pool.wait_ge(sem("even_out"), KC)
            pool.dma_start(cin_tok[0:24], d["state_conv"][0].rearrange("b r c -> (b r) c")).then_inc(sem("cin_loaded"), 16)
            pool.wait_ge(sem("xn_ready"), 3)
            pool.dma_start(causal, d["c_causal"]).then_inc(sem("odd_consts"), 16)

        ODD_CONSTS = 16 * 8

        def odd_weights(sp, g, par):
            for s, cols in ((2 * par, ((0, 256, 256), (2048, 256, 256))), (2 * par + 1, ((4096, 128, 128), (5120, 128, 128)))):
                width = cols[0][2] * 2
                dst = ring[:, s, 0:KC * width].rearrange("p (k n) -> p k n", k=KC)
                for i, (base, stride, n) in enumerate(cols):
                    src = d["w_in_odd"][0][:, bass.ds(base + stride * g, n)].rearrange("(k p) n -> p k n", p=P)
                    sp.dma_start(dst[:, :, n * i:n * i + n], src).then_inc(sem(f"slot{s}_loaded"), 16)

        def odd_sp(sp):
            def group_loads(g, par):
                for c in range(2):
                    src = d["state_ssm"][0].rearrange("b (c h) p n -> c (h p) b n", h=2)[bass.ds(2 * g + c, 1)]
                    sp.dma_start(stb[par][c], src.rearrange("a q b n -> (a q) b n")).then_inc(sem(f"s{par}{c}_loaded"), 16)
                if isinstance(g, int) and g == 0:
                    sp.wait_ge(sem("rows_out"), 48)
                wait_pos(sp, "seg_done", g - 1)
                src = cs_dram[bass.ds(4 * g, 4)].rearrange("h n -> (h n)").rearrange("(a m) -> a m", a=1)
                sp.dma_start(cs_rows[:, par], src.to_broadcast([P, 4 * NT]).rearrange("p (h n) -> p h n", h=4))\
                    .then_inc(sem(f"cs{par}_loaded"), 16)

            def group_stores(g, par):
                for c in range(2):
                    sp.wait_ge(sem("st_new"), 2 * g + c + 1)
                    dst = d["ssm_sample"][0].rearrange("b (c h) p n -> c (h p) b n", h=2)[bass.ds(2 * g + c, 1)]
                    sp.dma_start(dst.rearrange("a q b n -> (a q) b n"), stb[par][c]).then_inc(sem(f"s{par}{c}_stored"), 16)
                sp.wait_ge(sem("ps_taken"), g + 1)
                dst = d["ssm_prompt"][0, 0].rearrange("(g c h) p n -> g (h p) c n", h=2, c=2)[bass.ds(g, 1)]
                sp.dma_start(dst.rearrange("a q c n -> (a q) c n"), p_st[:, par].rearrange("p (c n) -> p c n", c=2))\
                    .then_inc(sem(f"ps{par}_stored"), 16)

            def turn(g, par, first=False, last=False):
                early = isinstance(g, int) and g < 2
                if not last:
                    if not early:
                        sp.wait_ge(sem("op_done"), 6 * g - 6)
                        odd_weights(sp, g, par)
                if not early:
                    group_stores(g - 2, par)
                if not last:
                    if not early:
                        for c in range(2):
                            sp.wait_ge(sem(f"s{par}{c}_stored"), 8 * (g - par))
                    group_loads(g, par)
                else:
                    group_stores(7, 1)

            for par, e in ((0, 14), (1, 15)):
                sp.wait_ge(sem("gu_ready"), 4 * e + 4)
                if par == 0:
                    sp.wait_ge(sem("down_done"), 8 * e + 8)
                odd_weights(sp, par, par)
            sp.wait_ge(sem("down_done"), 8 * N_EXPERTS)
            over_samples(sp, None, turn, 0)

        def odd_out_sp(sp):
            for s in range(4):
                if s == 0:
                    sp.wait_ge(sem("op_done"), 48)
                if s == 1:
                    sp.wait_ge(sem("ss_done"), 16)
                if s == 3:
                    sp.wait_ge(sem("yi_done"), 8)
                load_slot(sp, s, d["w_out_odd"][0][512 * s:512 * s + 512, :])

        def odd_setup_pe(pe):
            pe.wait_ge(sem("cin_loaded"), 16)
            pe.wait_ge(sem("acc_done"), 8 * N_EXPERTS)
            for c in range(32):
                mm = pe.transpose(bank[3 + c // 16][:, 24 * (c % 16):24 * (c % 16) + 24], cin_tok[0:24, P * c:P * c + P],
                                  ident[0:24, 0:24])
            mm.then_inc(sem("cin_turned"), 1)
            pe.wait_ge(sem("xn_ready"), 3)
            pe.wait_ge(sem("odd_consts"), ODD_CONSTS + 16)
            for k in range(KC):
                mm = pe.matmul(bank[5][H, 0:NT], w_dt[:, k, :], xnT[:, k, 0:NT], start=(k == 0), stop=(k == KC - 1))
            mm.then_inc(sem("dt_done"), 1)

        def odd_turn_pe(pe):
            pe.wait_ge(sem("dt_vector"), 4)
            pe.wait_ge(sem("cin_taken"), 1)
            for i, x in enumerate((cs, dt, dtl)):
                for t, n in ((0, P), (1, P), (2, NS)):
                    mm = pe.transpose(bank[4][0:n, 96 * t + 32 * i:96 * t + 32 * i + 32], x[H, P * t:P * t + n], ident[H, H])
            mm.then_inc(sem("tok3_turned"), 1)

        def odd_setup_act(act, own):
            act.wait_ge(sem("cin_turned"), 1)
            act.wait_ge(sem("gu_ready"), 60)
            for i in range(2):
                own(act.copy(cin[:, 16 * i:16 * i + 16, :], bank[3 + i][:, 0:384].rearrange("p (c r) -> p c r", c=16)))
            own.settle()
            act.sem_inc(sem("cin_taken"), 1)
            act.wait_ge(sem("dt_vector"), 1)
            own(act.activation(dt_e[H], dt_v[H], ACT.Abs))
            own(act.activation(aexp, alog, ACT.Exp))
            own.settle()
            own.step_to(act.activation(dt_e[H], dt_e[H], ACT.Exp, scale=-1.0), sem("dt_scalar"), 1)
            act.wait_ge(sem("dt_vector"), 2)
            own.step_to(act.activation(dt_l[H], dt_w[H], ACT.Ln), sem("dt_scalar"), 2)
            act.wait_ge(sem("dt_vector"), 3)
            own(act.activation(tail[H, 0:SEQ], cs[H, 0:SEQ], ACT.Exp, bias=cs[H, SEQ - 1:SEQ], scale=-1.0))
            own(act.activation(tail[H, SEQ:NT], tail[H, SEQ:NT], ACT.Exp))
            own.step_to(act.activation(dt_e[H, 0:NS], cs[H, SEQ:NT], ACT.Exp), sem("dt_scalar"), 3)
            own.settle()
            act.wait_ge(sem("dt_vector"), 5)
            act.dma_start(cs_dram, cs[H]).then_inc(sem("rows_out"), 16)
            act.dma_start(e_dram, dt_e[H, 0:NS]).then_inc(sem("rows_out"), 16)
            act.dma_start(el_dram, dt_w[H, 0:8]).then_inc(sem("rows_out"), 16)
            act.wait_ge(sem("tok3_turned"), 1)
            own(act.copy(tok3[:, 0:2, :], bank[4][:, 0:192].rearrange("p (t n) -> p t n", t=2)))
            own.step_to(act.copy(tok3[R, 2, :], bank[4][R, 192:288]), sem("tok3_set"), 1)
            own.settle()
            act.wait_ge(sem("rows_out"), 48)
            for g in range(2):
                r = slice(HD * g, HD * g + HD)
                for dst, src, n in ((e_rows, e_dram, NS), (e_last, el_dram, 8)):
                    act.dma_start(dst[r], src.rearrange("(c h) n -> h c n", h=2)[g].unsqueeze(0).to_broadcast([HD, 16, n]))\
                        .then_inc(sem("e_loaded"), 16)

        def odd_setup_dve(dve, own):
            def step(ins):
                own(ins)
                own.settle()

            dve.wait_ge(sem("cin_turned"), 1)
            dve.wait_ge(sem("odd_consts"), ODD_CONSTS + 16)
            own(dve.memset(raw[:, :, 0:3], 0.0))
            dve.wait_ge(sem("dt_done"), 1)
            own.step_to(dve.tensor_scalar(dt_v[H], bank[5][H, 0:NT], dtb, None, ALU.add), sem("dt_vector"), 1)
            own.settle()
            dve.wait_ge(sem("dt_scalar"), 1)
            own.step_to(dve.tensor_scalar(dt_w[H], dt_e[H], 1.0, None, ALU.add), sem("dt_vector"), 2)
            own.settle()
            step(dve.tensor_scalar(dt_m[H], dt_w[H], 1.0, None, ALU.is_equal))
            step(dve.scalar_tensor_tensor(out=dt[H], in0=dt_w[H], scalar=-1.0, in1=dt_m[H], op0=ALU.add, op1=ALU.add))
            step(dve.reciprocal(dt[H], dt[H]))
            step(dve.tensor_tensor(dt[H], dt[H], dt_e[H], ALU.mult))
            dve.wait_ge(sem("dt_scalar"), 2)
            step(dve.tensor_tensor(dt_l[H], dt_l[H], dt_m[H], ALU.add))
            step(dve.tensor_tensor(dt[H], dt[H], dt_l[H], ALU.mult))
            step(dve.scalar_tensor_tensor(out=dt[H], in0=dt_v[H], scalar=0.0, in1=dt[H], op0=ALU.max, op1=ALU.add))
            step(dve.tensor_scalar(dt_l[H], dt[H], aexp, -1.0, ALU.mult, ALU.mult))
            step(dve.memset(dt_v[H], 1.0))
            step(dve.memset(dt_v[H, SEQ:NT].rearrange("p (b t) -> p b t", t=DEC_SEQ)[:, :, 0:1], 0.0))
            step(dve.tensor_tensor_scan(cs[H], dt_v[H], dt_l[H], 0.0, ALU.mult, ALU.add))
            smp = lambda x: x.rearrange("p (b t) -> p b t", t=DEC_SEQ)
            css = smp(cs[H, SEQ:NT])
            own.step_to(dve.tensor_tensor(smp(tail[H, SEQ:NT]), css[:, :, 7:8].to_broadcast([SSM_HEADS, 8, 8]), css, ALU.subtract),
                       sem("dt_vector"), 3)
            dve.wait_ge(sem("dt_scalar"), 3)
            own.step_to(dve.tensor_tensor(dtl[H], dt[H], tail[H], ALU.mult), sem("dt_vector"), 4)
            own.step_to(dve.tensor_copy(dt_w[H, 0:8].unsqueeze(2), smp(dt_e[H, 0:NS])[:, :, 7:8]), sem("dt_vector"), 5)
            own.settle()
            dve.wait_ge(sem("tok3_set"), 1)
            dve.wait_ge(sem("e_loaded"), 64)

        def odd_groups_pe(pe):
            def proj(g, par, c):
                if c == 0:
                    pe.wait_ge(sem(f"slot{2 * par}_loaded"), 192 + 16 * (g - par))
                if c == 4:
                    pe.wait_ge(sem(f"slot{2 * par + 1}_loaded"), 192 + 16 * (g - par))
                wait_pos(pe, "op_taken", 6 * g + c - 2)
                w = slot_k[2 * par] if c < 4 else ring[:, 2 * par + 1, 0:2048].rearrange("p (k n) -> p k n", k=KC)
                for k in range(KC):
                    mm = pe.matmul(bank[c % 3][:, 0:NT], w[:, k, P * (c % 4):P * (c % 4) + P], xnT[:, k, 0:NT],
                                   start=(k == 0), stop=(k == KC - 1))
                mm.then_inc(sem("op_done"), 1)

            def turn_state(s, par, c):
                pe.wait_ge(sem(f"s{par}{c}_loaded"), 16 + 8 * (s - par))
                for half in range(2):
                    if c == 0:
                        wait_pos(pe, "st_new", 2 * s)
                    else:
                        pe.wait_ge(sem("stT_taken"), 4 * s + half + 1)
                    for b in range(4):
                        mm = pe.transpose(bank[3 + half][:, P * b:P * b + P], stb[par][c][:, 4 * half + b, :], ident[:, :])
                    mm.then_inc(sem("st_turned"), 1)

            def turn_x(s, par, tiles):
                for t, n in tiles:
                    if t < 2:
                        pe.wait_ge(sem("xc_done"), 4 * s + 4)
                        pe.wait_ge(sem("stT_taken"), 4 * s + 3 + t)
                    for i in range(3):
                        mm = pe.transpose(bank[3 + t % 2][0:n, P * i:P * i + P], xc[:, par, i, P * t:P * t + n], ident[:, :])
                    mm.then_inc(sem("x_turned2"), 1)

            def c_by_b(s, par):
                wait_pos(pe, "y_root", s)
                pe.wait_ge(sem("x_tok_set"), 3 * s + 1)
                pe.wait_ge(sem("b_tok_set"), 3 * s + 1)
                B, C, b = xc[:, par, 2, :], xc[:, par, 3, :], bank[5]
                pe.matmul(b[:, 0:2 * P], B[:, 0:P], C[:, 0:2 * P], start=True, stop=True)
                pe.matmul(b[:, 2 * P:3 * P], B[:, P:2 * P], C[:, P:2 * P], start=True, stop=True)
                pe.matmul(b[R, 3 * P:TRI], B[:, 2 * P:NT], C[:, 2 * P:NT], start=True, stop=True).then_inc(sem("cb_done"), 1)

            def y_start(s, par):
                wait_pos(pe, "y_taken", 2 * s)
                pe.wait_ge(sem("stT_taken"), 4 * s + 4)
                for c in range(2):
                    for n in range(DEC_BATCH):
                        mm = pe.matmul(bank[6 + c][:, NT + 8 * n:NT + 8 * n + 8], stT[:, c, n, :],
                                       xc[:, par, 3, SEQ + 8 * n:SEQ + 8 * n + 8], start=True, stop=True)
                mm.then_inc(sem("yi_done"), 1)

            def new_states(s, c):
                pe.wait_ge(sem("x_tok_set"), 3 * s + 3)
                if c == 0:
                    pe.wait_ge(sem("b_tok_set"), 3 * s + 3)
                else:
                    pe.wait_ge(sem("st_new"), 2 * s + 1)
                for half in range(2):
                    mm = pe.matmul(bank[3 + half][:, :], xtl[R, 2, P * c:P * c + P], b_diag[R, 4 * half:4 * half + 4, :],
                                   start=True, stop=True)
                mm.then_inc(sem("ss_done"), 1)

            def prompt_state(s):
                pe.wait_ge(sem("cb_taken"), s + 1)
                for c in range(2):
                    for t in range(2):
                        mm = pe.matmul(bank[5][:, P * c:P * c + P], xtl[:, t, P * c:P * c + P], b_tok[:, t, :],
                                       start=(t == 0), stop=(t == 1))
                mm.then_inc(sem("ps_done"), 1)

            def y_within(s):
                pe.wait_ge(sem("wts_set"), s + 1)
                for h in range(4):
                    o, x, w = bank[6 + h // 2][HD * (h % 2):HD * (h % 2) + HD, :], slice(HD * h, HD * h + HD), wts[:, h, :]
                    pe.matmul(o[:, 0:2 * P], xdt[:, 0, x], w[:, 0:2 * P], start=True, stop=False)
                    pe.matmul(o[:, P:2 * P], xdt[:, 1, x], w[:, 2 * P:3 * P], start=False, stop=True)
                    mm = pe.matmul(o[:, 2 * P:NT], xdt[R, 2, x], w[R, 3 * P:TRI], start=True, stop=True)
                    if h % 2 == 1:
                        mm.then_inc(sem("y_done"), 1)

            def square_sums(s):
                pe.wait_ge(sem("ps_taken"), s + 1)
                pe.wait_ge(sem("y_sq_set"), 2 * s + 2)
                for c in range(2):
                    mm = pe.matmul(bank[5][:, 0:NT], ones[:, :], y_sq[:, c, :], start=(c == 0), stop=(c == 1))
                mm.then_inc(sem("y_sum"), 1)

            def turn(g, par, first=False, last=False):
                s, sp_ = g - 1, 1 - par
                if not last:
                    proj(g, par, 0)
                if not first:
                    turn_state(s, sp_, 0)
                    turn_state(s, sp_, 1)
                if not last:
                    proj(g, par, 1)
                if not first:
                    turn_x(s, sp_, ((0, P), (1, P)))
                    c_by_b(s, sp_)
                    turn_x(s, sp_, ((2, NS),))
                if not last:
                    proj(g, par, 2)
                if not first:
                    y_start(s, sp_)
                    new_states(s, 0)
                if not last:
                    proj(g, par, 3)
                if not first:
                    prompt_state(s)
                    y_within(s)
                if not last:
                    proj(g, par, 4)
                if not first:
                    new_states(s, 1)
                if not last:
                    proj(g, par, 5)
                if not first:
                    square_sums(s)

            pe.wait_ge(sem("tok3_set"), 1)
            over_samples(pe, None, turn, 0)

        def odd_groups_act(act, own):
            def take(g, par, c):
                act.wait_ge(sem("op_done"), 6 * g + c + 1)
                b = bank[c % 3]
                if c < 2:
                    wait_pos(act, "yz_set", 2 * g - 2)
                    act.activation(z_s[:, par, c, :], b[:, 0:NT], ACT.Silu).then_inc(sem("op_taken"), 1)
                else:
                    wait_pos(act, "conv_done", 4 * g + c - 5)
                    own(act.copy(raw[:, c - 2, 3:3 + SEQ], b[:, 0:SEQ]))
                    act.copy(raw[:, c - 2, 3 + SEQ:RAW].rearrange("p (b t) -> p b t", b=8)[:, :, 3:11],
                             b[:, SEQ:NT].rearrange("p (b t) -> p b t", b=8)).then_inc(sem("op_taken"), 1)

            def state(s, f):
                act.wait_ge(sem("st_turned"), 4 * s + f + 1)
                if f == 0:
                    wait_pos(act, "yi_done", s)
                act.copy(stT[:, f // 2, 4 * (f % 2):4 * (f % 2) + 4, :], bank[3 + f % 2][:, :].rearrange("p (b n) -> p b n", b=4))\
                    .then_inc(sem("stT_taken"), 1)

            def exps(s):
                act.wait_ge(sem("seg_done"), s + 1)
                own(act.activation(wts[:, :, 0:3 * P], wts[:, :, 0:3 * P], ACT.Exp))
                act.activation(wts[R, :, 3 * P:TRI], wts[R, :, 3 * P:TRI], ACT.Exp).then_inc(sem("wts_exp"), 1)

            def b_to_tok(s, t, n):
                act.wait_ge(sem("x_tok_set"), 3 * s + t + 1)
                wait_pos(act, "ps_done", s)
                act.copy(b_tok[0:n, t, :], bank[3 + t % 2][0:n, 2 * P:3 * P]).then_inc(sem("b_tok_set"), 1)

            def silu(g, par, c):
                act.wait_ge(sem("conv_done"), 4 * g + c + 1)
                act.activation(xc[:, par, c, :], conv[:, c % 2, :], ACT.Silu).then_inc(sem("xc_done"), 1)

            def prompt_state(s, par):
                act.wait_ge(sem("ps_done"), s + 1)
                wait_pos(act, f"ps{par}_stored", 8 * (s - par))
                act.copy(p_st[:, par, :], bank[5][:, 0:256]).then_inc(sem("ps_taken"), 1)

            def squares(s, c):
                act.wait_ge(sem("yz_set"), 2 * s + c + 1)
                if c == 0:
                    wait_pos(act, "y_sum", s)
                act.activation(y_sq[:, c, :], y_sb[:, c, :], ACT.Square).then_inc(sem("y_sq_set"), 1)

            def root(s):
                act.wait_ge(sem("y_sum"), s + 1)
                wait_pos(act, "y_normed", s)
                act.activation(y_rs, bank[5][:, 0:NT], ACT.Sqrt, bias=eps[:, :], scale=1.0 / 256).then_inc(sem("y_root"), 1)

            def turn(g, par, first=False, last=False):
                s, sp_ = g - 1, 1 - par
                if not first:
                    exps(s)
                if not last:
                    take(g, par, 0)
                if not first:
                    for f in range(4):
                        state(s, f)
                if not last:
                    take(g, par, 1)
                if not first:
                    for t, n in ((0, P), (1, P), (2, NS)):
                        b_to_tok(s, t, n)
                if not last:
                    take(g, par, 2)
                    take(g, par, 3)
                if not first:
                    prompt_state(s, sp_)
                if not last:
                    silu(g, par, 0)
                    silu(g, par, 1)
                    take(g, par, 4)
                if not first:
                    squares(s, 0)
                    squares(s, 1)
                if not last:
                    take(g, par, 5)
                    silu(g, par, 2)
                    silu(g, par, 3)
                if not first:
                    root(s)

            over_samples(act, own, turn, 2 * 5)

        def odd_groups_dve(dve, own):
            def segments(s, par):
                dve.wait_ge(sem(f"cs{par}_loaded"), 16 + 8 * (s - par))
                wait_pos(dve, "y_done", 2 * s)
                for h in range(4):
                    for rws, cols, q, t in ((slice(0, P), slice(0, 2 * P), slice(0, 2 * P), 0),
                                            (slice(0, P), slice(2 * P, 3 * P), slice(P, 2 * P), 1),
                                            (R, slice(3 * P, TRI), slice(2 * P, NT), 2)):
                        ins = dve.tensor_scalar(wts[rws, h, cols], cs_rows[rws, par, h, q],
                                                tok3[rws, t, bass.ds(4 * s + h, 1)], 0.0, ALU.subtract, ALU.min)
                        if (h, t) != (3, 2):
                            own(ins)
                ins.then_inc(sem("seg_done"), 1)

            def x_to_tok(s, t, n):
                dve.wait_ge(sem("x_turned2"), 3 * s + t + 1)
                if t == 0:
                    wait_pos(dve, "ss_done", 2 * s)
                b = bank[3 + t % 2][0:n, :]
                x = b[:, 0:256].rearrange("p (h e) -> p h e", h=4)
                for dst, at in ((xdt, 32), (xtl, 64)):
                    ins = dve.tensor_tensor(dst[0:n, t, :].rearrange("p (h e) -> p h e", h=4), x,
                                            tok3[0:n, t, bass.ds(at + 4 * s, 4)].unsqueeze(2).to_broadcast([n, 4, HD]), ALU.mult)
                    if dst is xdt or t == 2:
                        own(ins)
                if t == 2:
                    ins = dve.tensor_tensor(b_diag[R], b[:, 256:384].unsqueeze(1).to_broadcast([NS, 8, D_STATE]),
                                            bmask[:, :].unsqueeze(2).to_broadcast([NS, 8, D_STATE]), ALU.mult)
                ins.then_inc(sem("x_tok_set"), 1)

            def weights(s):
                dve.wait_ge(sem("cb_done"), s + 1)
                (bp, bs), (mp, ms), (cp, cs_) = (causal_parts(x) for x in (bank[5], causal, cb))
                own(dve.tensor_tensor(cp, bp, mp, ALU.mult))
                own.step_to(dve.tensor_tensor(cs_, bs, ms, ALU.mult), sem("cb_taken"), s + 1)
                own.settle()
                dve.wait_ge(sem("wts_exp"), s + 1)
                own(dve.tensor_tensor(wts[:, :, 0:3 * P], wts[:, :, 0:3 * P], cp.unsqueeze(1).to_broadcast([P, 4, 3 * P]), ALU.mult))
                dve.tensor_tensor(wts[R, :, 3 * P:TRI], wts[R, :, 3 * P:TRI], cs_.unsqueeze(1).to_broadcast([NS, 4, NS]),
                                  ALU.mult).then_inc(sem("wts_set"), 1)

            def convolve(g, c):
                ch = (2 * g + c) if c < 2 else (8 * c + g)
                dve.wait_ge(sem("op_taken"), 6 * g + c + 3)
                r = raw[:, c, :]
                rs = r[:, 3 + SEQ:RAW].rearrange("p (b t) -> p b t", b=8)
                dyn = lambda x: x[:, bass.ds(ch, 1)]
                own(dve.tensor_scalar(rs[:, :, 0:3], dyn(cin).rearrange("p a (b t) -> p (a b) t", b=8), 1.0, None, ALU.mult))
                own(dve.tensor_scalar(dyn(tails)[:, :, 0:3].rearrange("p a t -> p (a t)"), r[:, SEQ:SEQ + 3], 1.0, None, ALU.mult))
                own(dve.tensor_scalar(dyn(tails)[:, :, 3:27].rearrange("p a (b t) -> p (a b) t", b=8), rs[:, :, 8:11], 1.0, None, ALU.mult))
                wait_pos(dve, "xc_done", 4 * g + c - 1)
                acc_p, acc_s = conv[:, c % 2, 0:SEQ], conv[:, c % 2, SEQ:NT].rearrange("p (b t) -> p b t", b=8)
                for k in range(CONV_W):
                    w = cw[:, bass.ds(ch, 1), k]
                    own.settle()
                    if k == 0:
                        own(dve.tensor_scalar(acc_p, r[:, 0:SEQ], w, cbias[:, bass.ds(ch, 1)], ALU.mult, ALU.add))
                        own(dve.tensor_scalar(acc_s, rs[:, :, 0:8], w, cbias[:, bass.ds(ch, 1)], ALU.mult, ALU.add))
                    else:
                        own(dve.scalar_tensor_tensor(out=acc_p, in0=r[:, k:k + SEQ], scalar=w, in1=acc_p, op0=ALU.mult, op1=ALU.add))
                        ins = dve.scalar_tensor_tensor(out=acc_s, in0=rs[:, :, k:k + 8], scalar=w, in1=acc_s, op0=ALU.mult, op1=ALU.add)
                        if k < CONV_W - 1:
                            own(ins)
                own.step_to(ins, sem("conv_done"), 4 * g + c + 1)

            def update(s, par, c):
                dve.wait_ge(sem("st_turned"), 4 * s + 4)
                x = stb[par][c]
                own(dve.tensor_tensor(x, x, e_last[:, bass.ds(2 * s + c, 1), :].rearrange("p a b -> p (a b)").unsqueeze(2)
                                      .to_broadcast([P, 8, D_STATE]), ALU.mult))
                dve.wait_ge(sem("ss_done"), 2 * s + c + 1)
                own.settle()
                for half in range(2):
                    xh = x[:, 4 * half:4 * half + 4, :].rearrange("p b n -> p (b n)")
                    ins = dve.tensor_tensor(xh, xh, bank[3 + half][:, :], ALU.add)
                    if half == 0:
                        own(ins)
                ins.then_inc(sem("st_new"), 1)

            def y_out(s, par, c):
                dve.wait_ge(sem("y_done"), 2 * s + c + 1)
                dve.wait_ge(sem("yi_done"), s + 1)
                b, y = bank[6 + c], y_sb[:, c, :]
                own(dve.tensor_tensor(y_in, b[:, NT:NT + NS], e_rows[:, bass.ds(2 * s + c, 1), :].rearrange("p a n -> p (a n)"), ALU.mult))
                own.step_to(dve.scalar_tensor_tensor(out=y, in0=xc[:, par, c, :], scalar=skip[:, bass.ds(2 * s + c, 1)],
                                                    in1=b[:, 0:NT], op0=ALU.mult, op1=ALU.add), sem("y_taken"), 2 * s + c + 1)
                own.settle()
                own(dve.tensor_tensor(y[:, SEQ:NT], y[:, SEQ:NT], y_in, ALU.add))
                own.settle()
                own.step_to(dve.tensor_tensor(y, y, z_s[:, par, c, :], ALU.mult), sem("yz_set"), 2 * s + c + 1)
                own.settle()

            def normalise(s):
                dve.wait_ge(sem("y_root"), s + 1)
                own(dve.reciprocal(y_rs, y_rs))
                own.settle()
                for c in range(2):
                    ins = dve.scalar_tensor_tensor(out=y_cat[:, bass.ds(2 * s + c, 1), :].rearrange("p a n -> p (a n)"),
                                                   in0=y_sb[:, c, :], scalar=gain[:, bass.ds(2 * s + c, 1)], in1=y_rs,
                                                   op0=ALU.mult, op1=ALU.mult)
                    if c == 0:
                        own(ins)
                ins.then_inc(sem("y_normed"), 1)

            def turn(g, par, first=False, last=False):
                s, sp_ = g - 1, 1 - par
                if not first:
                    segments(s, sp_)
                    for t, n in ((0, P), (1, P), (2, NS)):
                        x_to_tok(s, t, n)
                    weights(s)
                    update(s, sp_, 0)
                if not last:
                    convolve(g, 0)
                    convolve(g, 1)
                if not first:
                    y_out(s, sp_, 0)
                    y_out(s, sp_, 1)
                    update(s, sp_, 1)
                if not last:
                    convolve(g, 2)
                    convolve(g, 3)
                if not first:
                    normalise(s)

            over_samples(dve, own, turn, 2 * 67)

        tails_tok = part(0, 4096)

        def odd_out_pe(pe):
            pe.wait_ge(sem("y_normed"), GROUPS)
            pe.wait_ge(sem("conv_done"), 4 * GROUPS)
            for i in range(8):
                if i >= 4:
                    pe.wait_ge(sem("tails_taken"), i - 3)
                for c in range(4):
                    mm = pe.transpose(bank[4 + i % 4][0:27, P * c:P * c + P], tails[:, 4 * i + c, :], ident[:, :])
                mm.then_inc(sem("tails_turned"), 1)
            for s in range(4):
                slot_loaded(pe, s, 19)
            for c in range(KC):
                if c >= 4:
                    pe.wait_ge(sem("h_ready"), 2 * KC + c - 3)
                for k in range(16):
                    mm = pe.matmul(bank[c % 4][:, 0:NT], slot_f[k // 4][:, k % 4, P * c:P * c + P], y_cat[:, k, :],
                                   start=(k == 0), stop=(k == 15))
                mm.then_inc(sem("odd_out"), 1)

        def odd_out_act(act, own):
            for i in range(8):
                act.wait_ge(sem("tails_turned"), i + 1)
                own.step_to(act.copy(tails_tok[0:27, 512 * i:512 * i + 512], bank[4 + i % 4][0:27, :]), sem("tails_taken"), i + 1)
            own.settle()
            act.dma_start(d["conv_prompt"][0, 0], tails_tok[0:3]).then_inc(sem("tails_stored"), 16)
            act.dma_start(d["conv_sample"][0].rearrange("b r c -> (b r) c"), tails_tok[3:27]).then_inc(sem("tails_stored"), 16)

        def odd_out_dve(dve, own):
            for c in range(KC):
                dve.wait_ge(sem("odd_out"), c + 1)
                own.step_to(dve.tensor_tensor(hT[:, c, :], hT[:, c, :], bank[c % 4][:, 0:NT], ALU.add), sem("h_ready"), 2 * KC + c + 1)
            own.settle()

        @block.sync
        def _(sp):
            sp.dma_start(x_tok[:, 0:2, :], d["x_prompt"][0].rearrange("(t p) n -> p t n", p=P)).then_inc(sem("x_loaded"), 32)
            sp.dma_start(x_tok[0:NS, 2, :], d["x_sample"].rearrange("b t n -> (b t) n")).then_inc(sem("x_loaded"), 16)
            even_weights(sp)
            sp.wait_ge(sem("proj_done"), 21)
            expert_piece(sp, 0, 0, 0, 0)
            pages_sp(sp)
            sp.wait_ge(sem("sm_out"), 8)
            expert_piece(sp, 0, 0, 0, 1)
            expert_piece(sp, 0, 0, 0, 2)
            sp.wait_ge(sem("even_out"), 8)
            for q in range(3):
                expert_piece(sp, 0, 1, 1, q)
            experts_sp(sp, 0)
            odd_sp(sp)
            odd_out_sp(sp)
            sp.wait_ge(sem("odd_out"), KC)
            for e in range(2):
                for q in range(3):
                    expert_piece(sp, 1, e, e, q)
            experts_sp(sp, 1)
            for s in ("s00", "s01", "s10", "s11", "ps0", "ps1"):
                sp.wait_ge(sem(s + "_stored"), 64)
            sp.wait_ge(sem("tails_stored"), 32)

        @block.tensor
        def _(pe):
            transpose_x_pe(pe)
            norm_pe(pe, 0)
            even_proj_pe(pe)
            even_turn_pe(pe)
            retention_pe(pe)
            prompt_attn_pe(pe)
            sample_attn_pe(pe)
            even_out_pe(pe)
            norm_pe(pe, 1)
            route_pe(pe, 0)
            experts_pe(pe, 0)
            norm_pe(pe, 2)
            odd_setup_pe(pe)
            odd_turn_pe(pe)
            odd_groups_pe(pe)
            odd_out_pe(pe)
            norm_pe(pe, 3)
            route_pe(pe, 1)
            experts_pe(pe, 1)
            finish_pe(pe, lambda e: e.wait_ge(sem("acc_done"), 2 * DN))

        @block.scalar
        def _(act):
            own = Own(act, sem("act_steps"))
            load_consts(act)
            act.wait_ge(sem("eps_set"), 1)
            norm_act(act, own, 0, lambda e: e.wait_ge(sem("h_ready"), KC))
            even_proj_act(act, own)
            even_turn_act(act, own)
            retention_act(act, own)
            prompt_attn_act(act, own)
            sample_attn_act(act, own)
            norm_act(act, own, 1, lambda e: e.wait_ge(sem("h_ready"), 2 * KC))
            route_act(act, own, 0)
            experts_act(act, 0)
            norm_act(act, own, 2, lambda e: e.wait_ge(sem("acc_done"), 8 * N_EXPERTS))
            odd_setup_act(act, own)
            odd_groups_act(act, own)
            odd_out_act(act, own)
            norm_act(act, own, 3, lambda e: e.wait_ge(sem("h_ready"), 3 * KC))
            act.wait_ge(sem("tails_stored"), 32)
            route_act(act, own, 1)
            experts_act(act, 1)
            finish_act(act, own)

        @block.vector
        def _(dve):
            own = Own(dve, sem("dve_steps"))
            dve.memset(eps[:, :], EPS).then_inc(sem("eps_set"), 1)
            transpose_x_dve(dve, own)
            dve.wait_ge(sem("consts_loaded"), 16 * N_CONSTS)
            norm_dve(dve, own, 0, g_mix[:, 0, :])
            even_rope_dve(dve, own)
            retention_dve(dve, own)
            prompt_attn_dve(dve, own)
            sample_setup_dve(dve, own)
            sample_attn_dve(dve, own)
            even_out_dve(dve, own)
            norm_dve(dve, own, 1, g_ffn[:, 0, :])
            route_dve(dve, own, 0)
            experts_dve(dve, 0)
            norm_dve(dve, own, 2, g_mix[:, 1, :])
            odd_setup_dve(dve, own)
            odd_groups_dve(dve, own)
            odd_out_dve(dve, own)
            norm_dve(dve, own, 3, g_ffn[:, 1, :])
            route_dve(dve, own, 1)
            experts_dve(dve, 1)

        @block.gpsimd
        def _(pool):
            for l in range(2):
                pool.dma_start(wr[:, l, :, 0:4], d["w_router_group"][l].rearrange("(k p) n -> p k n", p=P)).then_inc(sem("wr_loaded"), 16)
                pool.dma_start(wr[:, l, :, 4:20], d["w_router_expert"][l].rearrange("(k p) n -> p k n", p=P)).then_inc(sem("wr_loaded"), 16)
            kv_pool(pool)
            retention_pool(pool)
            pool.wait_ge(sem("ret_s_state"), HEADS)
            pool.dma_start(maskp, d["c_maskp"]).then_inc(sem("maskp_loaded"), 16)
            pool.dma_start(sc_mask[R], d["c_masks"]).then_inc(sem("masks_loaded"), 16)
            pool.dma_start(before[R], d["c_before"]).then_inc(sem("masks_loaded"), 16)
            odd_setup_pool(pool)


N_CONSTS = 13
_CONSTS = shape_constants()
_OUTS = [("y_prompt", (1, SEQ, D_MODEL)), ("y_sample", (8, 8, D_MODEL)),
         ("ret_prompt", (1, 1, 8, 64, 128)), ("ret_sample", (1, 8, 8, 64, 128)),
         ("k_prompt", (1, 1, SEQ, 8, 64)), ("v_prompt", (1, 1, SEQ, 8, 64)),
         ("k_sample", (1, 8, 8, 8, 64)), ("v_sample", (1, 8, 8, 8, 64)),
         ("ssm_prompt", (1, 1, 32, 64, 128)), ("ssm_sample", (1, 8, 32, 64, 128)),
         ("conv_prompt", (1, 1, 3, 4096)), ("conv_sample", (1, 8, 3, 4096))]


def kernel(**inputs):
    import concourse.bacc as _bacc
    from concourse.bass_utils import run_bass_kernel_spmd as _run

    by_part = {"norm_mix": lambda a: a.reshape(2, KC, P).transpose(2, 0, 1),
               "norm_ffn": lambda a: a.reshape(2, KC, P).transpose(2, 0, 1),
               "conv_w": lambda a: a[0].reshape(CONV_W, 32, P).transpose(2, 1, 0),
               "conv_b": lambda a: a[0].reshape(32, P).transpose(1, 0),
               "ssd_norm": lambda a: a[0].reshape(16, P).transpose(1, 0),
               "dt_bias": lambda a: a.reshape(SSM_HEADS, 1), "a_log": lambda a: a.reshape(SSM_HEADS, 1),
               "d_skip": lambda a: a.reshape(16, 2).transpose(1, 0)}
    nc = _bacc.Bacc("TRN2", target_bir_lowering=False, num_devices=1)
    arrays, d = {}, {}
    for name, a in list(inputs.items()) + [("c_" + k, v) for k, v in _CONSTS.items()]:
        a = np.ascontiguousarray(by_part.get(name, lambda x: x)(np.asarray(a)))
        arrays[f"in_{name}"] = a
        d[name] = nc.dram_tensor(f"in_{name}", a.shape, mybir.dt.from_np(a.dtype), kind="ExternalInput").ap()
    for name, shape in _OUTS:
        d[name] = nc.dram_tensor(f"out_{name}", shape, F32, kind="ExternalOutput").ap()
    build(nc, d)
    r = _run(nc, [arrays], core_ids=[0])
    return tuple(r.results[0][f"out_{name}"] for name, _ in _OUTS)
```

```python
from contextlib import ExitStack

import numpy as np

import concourse.bass as bass
from concourse import mybir

F32 = mybir.dt.float32
I32 = mybir.dt.int32
ALU = mybir.AluOpType
ACT = mybir.ActivationFunctionType
AX_X = mybir.AxisListType.X

P = 128
D_MODEL, SEQ, DEC_BATCH, DEC_SEQ, PAST_LEN, PAGE = 1024, 256, 8, 8, 2048, 128
KC = D_MODEL // P
NS = DEC_BATCH * DEC_SEQ
NT = SEQ + NS
NTP = 3 * P
HEADS, HD, DV = 8, 64, 128
N_PAGES = PAST_LEN // PAGE
BLOCK = 256
N_BLOCKS = PAST_LEN // BLOCK
TOPK = 3
QK_SCALE = HD ** -0.5
GROUPS, D_STATE, D_INNER, SSM_HEADS, CONV_W = 8, 128, 2048, 32, 4
N_EXPERTS, EXPERT_FF, MOE_GROUPS = 16, 512, 4
FC = EXPERT_FF // P
EPS = 1e-6
NEG = -1e30
TRI = 2 * P + P + NS
SLOT = 4096
N_SLOTS = 6
CAP = 72
N_PAIRS = 2 * NT
EVEN_COLS = [0, 512, 3072, 3584, 4096, 1024, 1536, 2048, 2560]
RQ, RK, MQ, MK, MV, RV = 0, 512, 1024, 1536, 2048, 2560
QKV_W = 3584


def shape_constants():
    f = np.float32
    tok = np.arange(NTP)
    sample = tok >= SEQ
    t_in = np.where(sample, (tok - SEQ) % DEC_SEQ, tok)
    pos = np.where(sample, PAST_LEN + t_in, tok).astype(f)
    inv = np.power(f(10000.0), -np.arange(HD // 2, dtype=f) * f(2.0) / f(HD)).astype(f)
    ang = pos[:, None] * inv[None, :]
    by_tile = lambda a: np.ascontiguousarray(a.reshape(3, P, -1).transpose(1, 0, 2)).astype(f)
    cos = by_tile(np.concatenate([np.cos(ang), np.cos(ang)], 1))
    sin = by_tile(np.concatenate([-np.sin(ang), np.sin(ang)], 1))
    lg = np.log1p(-np.exp2(-5.0 - np.arange(HEADS)))
    key = np.concatenate([np.repeat(np.arange(P)[:, None], 2 * P, 1),
                          np.repeat(P + np.arange(P)[:, None], P, 1),
                          np.repeat(SEQ + np.arange(P)[:, None], NS, 1)], 1)
    qry = np.concatenate([np.arange(2 * P), P + np.arange(P), SEQ + np.arange(NS)])[None, :].repeat(P, 0)
    same = (key < SEQ) & (qry < SEQ) | (key >= SEQ) & (key < NT) & ((key - SEQ) // 8 == (qry - SEQ) // 8)
    ok = same & (qry >= key)
    dist = np.where(ok, qry - key, 0)
    dmat = np.where(ok[None], np.exp(dist[None] * lg[:, None, None]), 0.0) * HD ** -0.5
    left = np.where(sample, DEC_SEQ - 1 - t_in, SEQ - 1 - t_in)
    kdec = np.where((tok < NT)[:, None], np.exp(left[:, None] * lg[None, :]) * HD ** -0.5, 0.0)
    qdec = np.exp((np.arange(NS) % 8 + 1)[:, None] * lg[None, :])
    stdec = np.exp(DEC_SEQ * lg).reshape(4, 2).T.repeat(HD, 0)
    bmask = (np.arange(NS)[:, None] // 8 == np.arange(8)[None, :])
    q, k = np.arange(P)[:, None], np.arange(2 * P)[None, :]
    maskp = np.concatenate([np.where(k[:, :P] <= q, 0.0, NEG), np.where(k <= q + P, 0.0, NEG)], 1)
    row, own = np.arange(NS) % 8, np.arange(NS)
    masks = np.where((own[None, None, :] // 8 == np.arange(8)[None, :, None])
                     & (own[None, None, :] % 8 <= row[:, None, None]), 0.0, NEG)
    before = np.broadcast_to(np.arange(8)[None, :] < np.arange(8)[:, None], (NS, 8, 8))
    out = dict(cos=cos, sin=sin, dmat=dmat, kdec=by_tile(kdec), qdec=qdec, stdec=stdec, bmask=bmask, maskp=maskp,
               masks=masks, before=before, causal=ok, earlier=np.triu(np.ones((P, P)), 1),
               number=np.arange(N_PAIRS // 2)[None, :].repeat(P, 0), ident=np.eye(P), ones=np.ones((P, P)))
    return {k: np.ascontiguousarray(v).astype(f) for k, v in out.items()}


class Own:

    def __init__(self, eng, sem, start=0):
        self.eng, self.sem, self.base, self.n, self.others = eng, sem, start, 0, []

    def __call__(self, ins):
        ins.then_inc(self.sem, 1)
        self.n += 1

    def step_to(self, ins, sem, value):
        ins.then_inc(sem, 1)
        self.others = [(s, v) for s, v in self.others if s is not sem] + [(sem, value)]

    def settle(self):
        for sem, value in self.others:
            self.eng.wait_ge(sem, value)
        self.others = []
        if not (isinstance(self.base, int) and self.base + self.n == 0):
            self.eng.wait_ge(self.sem, self.base + self.n)

    def turn(self, i, start, steps):
        self.before_loop = self.base + self.n
        self.base, self.n, self.steps = self.before_loop + (i - start) * steps, 0, steps

    def end(self, turns):
        assert self.n == self.steps, f"the loop's body takes {self.n} steps"
        self.base, self.n = self.before_loop + turns * self.steps, 0


def build(nc, d):
    with ExitStack() as ctx:
        def sb(name, shape, dt=F32):
            return ctx.enter_context(nc.sbuf_tensor(name, shape, dt))

        sems = {}

        def sem(name):
            if name not in sems:
                sems[name] = ctx.enter_context(nc.semaphore(name))
            return sems[name]

        ring = sb("ring", [P, N_SLOTS, SLOT])
        hT = sb("hT", [P, KC, NT])
        xnT = sb("xnT", [P, KC, NTP])
        catT = sb("catT", [P, 12, NT])
        arena = sb("arena", [P, 17100])
        ident = sb("ident", [P, P])
        ones = sb("ones", [P, P])
        cos, sin = sb("cos", [P, 3, HD]), sb("sin", [P, 3, HD])
        qg, kg = sb("qg", [P, HD]), sb("kg", [P, HD])
        g_mix, g_ffn = sb("g_mix", [P, 2, KC]), sb("g_ffn", [P, 2, KC])
        kdec = sb("kdec", [P, 3, HEADS])
        qdec = sb("qdec", [NS, HEADS])
        stdec = sb("stdec", [P, 4])
        bmask = sb("bmask", [NS, 8])
        small = sb("small", [P, 256])
        eps = sb("eps", [P, 1])
        earlier, number = sb("earlier", [P, P]), sb("number", [P, N_PAIRS // 2])
        most, route_i = sb("most", [P, 1]), sb("route_i", [1, 17], I32)
        wr = sb("wr", [P, 2, KC, MOE_GROUPS + N_EXPERTS])
        cs_dram, e_dram, el_dram = (nc.dram_tensor(n, [SSM_HEADS, w], F32).ap()
                                    for n, w in (("cs_rows_dram", NT), ("e_rows_dram", NS), ("e_last_dram", 8)))
        gate_dram = nc.dram_tensor("gate_rows", [2, N_EXPERTS, NT], F32).ap()
        pages = sb("pages", [1, DEC_BATCH * N_PAGES], I32)
        bank = [ctx.enter_context(nc.psum_tensor(f"bank{i}", [P, 512], F32)) for i in range(8)]

        def part(off, *shape, of=arena):
            n = int(np.prod(shape))
            v = of[:, off:off + n]
            names = "abcd"[:len(shape)]
            return v.rearrange(f"p ({' '.join(names)}) -> p {' '.join(names)}", **dict(zip(names[1:], shape[1:])))

        xn_flat = xnT[:, :, :].rearrange("p a b -> p (a b)")
        cat_flat = catT[:, :, :].rearrange("p a b -> p (a b)")
        slot_k = [ring[:, s, :].rearrange("p (k n) -> p k n", k=KC) for s in range(N_SLOTS)]
        slot_f = [ring[:, s, :].rearrange("p (f n) -> p f n", f=FC) for s in range(N_SLOTS)]

        x_tok = part(0, 3, D_MODEL)
        sq_all = part(14000, KC * NT)
        rs_all = part(16600, NT)
        q_tok = {"rq": part(0, 3, 512), "rk": part(1536, 3, 512), "mq": part(3072, 3, 512),
                 "mk": part(4608, 3, 512), "mv": part(6144, 3, 512), "rv": part(7680, 3, 1024)}
        rqT, rkT, mqT, mkT = (part(10752 + 1280 * i, 4, NT) for i in range(4))
        rope_a, rope_b = part(10752, 3, 512), part(10752 + 1536, 3, 512)
        q_dec = part(14592, 512)
        dmat = part(15872, 2, TRI)
        st = [part(0, 8, DV), part(3072, 8, DV)]
        ret_p = part(4096, 4, DV)
        qdT = part(0, 4, NS, of=xn_flat)
        sc_sb = part(256, 2, TRI, of=xn_flat)
        rv_bd = part(1152, 8, DV, of=xn_flat)
        ro_sq = part(2176, NT, of=xn_flat)
        ro_rs = part(2496, NT, of=xn_flat)
        pm_s = part(0, 2, 3 * P, of=xn_flat)
        pm_T = part(768, 2, 3 * P, of=xn_flat)
        maskp = part(1536, 3 * P, of=xn_flat)

        def causal_parts(t):
            return t[:, 0:3 * P], t[0:NS, 3 * P:TRI]

        block = ctx.enter_context(nc.Block())

        def load_slot(sp, s, src, cols=None):
            k = src.shape[0] // P
            dst = ring[:, s, 0:k * src.shape[1]].rearrange("p (k n) -> p k n", k=k)
            sp.dma_start(dst, src.rearrange("(k p) n -> p k n", p=P)).then_inc(sem(f"slot{s}_loaded"), 16)

        def slot_loaded(pe, s, use):
            pe.wait_ge(sem(f"slot{s}_loaded"), 16 * use)

        def even_weights(sp):
            for n, c in enumerate(EVEN_COLS):
                if n >= N_SLOTS:
                    sp.wait_ge(sem("proj_done"), 3 * (n - N_SLOTS + 1))
                load_slot(sp, n % N_SLOTS, d["w_in_even"][0][:, c:c + 512])
            for n in range(3):
                s = 3 + n
                sp.wait_ge(sem("proj_done"), 3 * (s + 1))
                load_slot(sp, s, d["w_out_even"][0][512 * n:512 * n + 512, :])

        def norm_act(act, own, k, ready):
            ready(act)
            own.step_to(act.activation(sq_all, hT[:, :, :].rearrange("p a b -> p (a b)"), ACT.Square), sem("norm_sq"), k + 1)
            act.wait_ge(sem("norm_sum"), k + 1)
            own.step_to(act.activation(rs_all, bank[0][:, 0:NT], ACT.Sqrt, bias=eps[:, :], scale=1.0 / D_MODEL),
                       sem("norm_root"), k + 1)

        def norm_pe(pe, k):
            pe.wait_ge(sem("norm_sq"), k + 1)
            for c in range(KC):
                mm = pe.matmul(bank[0][:, 0:NT], ones[:, :], sq_all[:, NT * c:NT * c + NT], start=(c == 0), stop=(c == KC - 1))
            mm.then_inc(sem("norm_sum"), 1)

        def norm_dve(dve, own, k, gain):
            own(dve.memset(xnT[:, :, NT:NTP], 0.0))
            dve.wait_ge(sem("norm_root"), k + 1)
            own(dve.reciprocal(rs_all, rs_all))
            own.settle()
            for c in range(KC):
                ins = dve.scalar_tensor_tensor(out=xnT[:, c, 0:NT], in0=hT[:, c, :], scalar=gain[:, c:c + 1],
                                               in1=rs_all, op0=ALU.mult, op1=ALU.mult)
                if c < KC - 1:
                    own(ins)
            own.step_to(ins, sem("xn_ready"), k + 1)

        def transpose_x_pe(pe):
            pe.wait_ge(sem("x_loaded"), 48)
            pe.wait_ge(sem("consts_loaded"), 16 * N_CONSTS)
            for c in range(KC):
                for t, n in ((0, P), (1, P), (2, NS)):
                    mm = pe.transpose(bank[c][:, P * t:P * t + n], x_tok[0:n, t, P * c:P * c + P], ident[0:n, 0:n])
                mm.then_inc(sem("x_turned"), 1)

        def transpose_x_dve(dve, own):
            for c in range(KC):
                dve.wait_ge(sem("x_turned"), c + 1)
                own.step_to(dve.tensor_copy(hT[:, c, :], bank[c][:, 0:NT]), sem("h_ready"), c + 1)
            own.settle()

        PROJ_BANKS = 4

        def even_proj_pe(pe):
            pe.wait_ge(sem("xn_ready"), 1)
            idx = 0
            for n in range(7):
                slot_loaded(pe, n % N_SLOTS, n // N_SLOTS + 1)
                for t in range(3):
                    if idx >= PROJ_BANKS:
                        pe.wait_ge(sem("proj_taken"), idx - PROJ_BANKS + 1)
                    b = bank[1 + idx % PROJ_BANKS]
                    for k in range(KC):
                        mm = pe.matmul(b[:, :], xnT[:, k, P * t:P * t + P], slot_k[n % N_SLOTS][:, k, :],
                                       start=(k == 0), stop=(k == KC - 1))
                    mm.then_inc(sem("proj_done"), 1)
                    idx += 1
            for c in range(8):
                n = 7 + c // 4
                slot_loaded(pe, n % N_SLOTS, n // N_SLOTS + 1)
                pe.wait_ge(sem("proj_taken"), idx - PROJ_BANKS + 1)
                b = bank[1 + idx % PROJ_BANKS]
                for k in range(KC):
                    mm = pe.matmul(b[:, 0:NT], slot_k[n % N_SLOTS][:, k, P * (c % 4):P * (c % 4) + P], xnT[:, k, 0:NT],
                                   start=(k == 0), stop=(k == KC - 1))
                mm.then_inc(sem("proj_done"), 1)
                idx += 1

        def even_proj_act(act, own):
            dests = [(q_tok[x], 0) for x in ("rq", "rk", "mq", "mk", "mv", "rv")] + [(q_tok["rv"], 512)]
            roots = {2: 0, 3: 1}
            idx = 0
            for n, (dst, c0) in enumerate(dests):
                for t in range(3):
                    act.wait_ge(sem("proj_done"), idx + 1)
                    own.step_to(act.copy(dst[:, t, c0:c0 + 512], bank[1 + idx % PROJ_BANKS][:, :]), sem("proj_taken"), idx + 1)
                    idx += 1
            for i in range(2):
                act.wait_ge(sem("qk_sums"), i + 1)
                own.step_to(act.activation(small[:, 24 * i:24 * i + 24], small[:, 24 * i:24 * i + 24], ACT.Sqrt,
                                          bias=eps[:, :], scale=1.0 / HD), sem("qk_roots"), i + 1)
            for c in range(8):
                act.wait_ge(sem("proj_done"), idx + 1)
                own.step_to(act.activation(catT[:, c, :], bank[1 + idx % PROJ_BANKS][:, 0:NT], ACT.Silu), sem("proj_taken"), idx + 1)
                idx += 1

        def heads(x):
            return x.rearrange("p t (h e) -> p t h e", h=HEADS)

        def even_rope_dve(dve, own):
            H2 = HD // 2
            over = lambda table: table.unsqueeze(2).to_broadcast([P, 3, HEADS, table.shape[2]])

            def rope(x, k):
                xh, a, b = heads(x), heads(rope_a), heads(rope_b)
                own.settle()
                own(dve.tensor_tensor(a, xh, over(cos[:, :, :]), ALU.mult))
                own(dve.tensor_tensor(b[:, :, :, 0:H2], xh[:, :, :, H2:HD], over(sin[:, :, 0:H2]), ALU.mult))
                own(dve.tensor_tensor(b[:, :, :, H2:HD], xh[:, :, :, 0:H2], over(sin[:, :, H2:HD]), ALU.mult))
                own.settle()
                own.step_to(dve.tensor_tensor(x, rope_a, rope_b, ALU.add), sem("roped"), k)

            def head_sums(x, i):
                own.settle()
                own(dve.tensor_tensor(rope_a, x, x, ALU.mult))
                own.settle()
                own.step_to(dve.tensor_reduce(small[:, 24 * i:24 * i + 24].rearrange("p (t h) -> p t h", t=3),
                                             heads(rope_a), AX_X, ALU.add), sem("qk_sums"), i + 1)
                own.settle()

            def qk_norm(x, i, gain):
                dve.wait_ge(sem("qk_roots"), i + 1)
                r = small[:, 24 * i:24 * i + 24]
                own(dve.reciprocal(r, r))
                own.settle()
                own(dve.tensor_tensor(heads(x), heads(x), r.rearrange("p (t h) -> p t h", t=3).unsqueeze(3)
                                      .to_broadcast([P, 3, HEADS, HD]), ALU.mult))
                own.settle()
                own(dve.tensor_tensor(heads(x), heads(x), gain[:, :].unsqueeze(1).unsqueeze(1)
                                      .to_broadcast([P, 3, HEADS, HD]), ALU.mult))

            dve.wait_ge(sem("proj_taken"), 3)
            rope(q_tok["rq"], 1)
            dve.wait_ge(sem("proj_taken"), 6)
            rope(q_tok["rk"], 2)
            dve.wait_ge(sem("proj_taken"), 9)
            head_sums(q_tok["mq"], 0)
            dve.wait_ge(sem("proj_taken"), 12)
            head_sums(q_tok["mk"], 1)
            qk_norm(q_tok["mq"], 0, qg)
            rope(q_tok["mq"], 3)
            qk_norm(q_tok["mk"], 1, kg)
            rope(q_tok["mk"], 4)
            own.step_to(dve.tensor_tensor(q_dec[0:NS, :].rearrange("p (h e) -> p h e", h=HEADS),
                                         heads(q_tok["rq"])[0:NS, 2, :, :],
                                         qdec[:, :].unsqueeze(2).to_broadcast([NS, HEADS, HD]), ALU.mult), sem("roped"), 5)
            own.settle()

        TURNS = [("rq", j) for j in range(4)] + [("rk", j) for j in range(4)] + [("mq", j) for j in range(4)] \
            + [("dec", 0)] + [("mk", j) for j in range(4)]
        TURN_OF = {"rq": (1, rqT), "rk": (2, rkT), "mq": (3, mqT), "mk": (4, mkT)}

        def even_turn_pe(pe):
            for r, (x, j) in enumerate(TURNS):
                if r >= 2:
                    pe.wait_ge(sem("turn_taken"), r - 1)
                b = bank[5 + r % 2]
                if x == "dec":
                    pe.wait_ge(sem("roped"), 5)
                    for jj in range(4):
                        mm = pe.transpose(b[:, NS * jj:NS * jj + NS], q_dec[0:NS, P * jj:P * jj + P], ident[0:NS, 0:NS])
                else:
                    pe.wait_ge(sem("roped"), 5)
                    for t, n in ((0, P), (1, P), (2, NS)):
                        mm = pe.transpose(b[:, P * t:P * t + n], q_tok[x][0:n, t, P * j:P * j + P], ident[0:n, 0:n])
                mm.then_inc(sem("turned"), 1)

        def even_turn_act(act, own):
            act.wait_ge(sem("proj_done"), 29)
            for r, (x, j) in enumerate(TURNS):
                act.wait_ge(sem("turned"), r + 1)
                b = bank[5 + r % 2]
                if x == "dec":
                    ins = act.copy(qdT, b[:, 0:4 * NS].rearrange("p (j t) -> p j t", j=4))
                else:
                    if x == "mk" and j == 0:
                        act.wait_ge(sem("turned"), 13)
                    ins = act.copy(TURN_OF[x][1][:, j, :], b[:, 0:NT])
                own.step_to(ins, sem("turn_taken"), r + 1)

        def rows(h):
            return slice(HD * (h % 2), HD * (h % 2) + HD)

        def retention_pe(pe):
            rv, rk = q_tok["rv"], q_tok["rk"]

            def scores(h):
                if h >= 2:
                    pe.wait_ge(sem("ret_scaled"), h - 1)
                b, r, j = bank[h % 2], rows(h), h // 2
                pe.matmul(b[:, 0:2 * P], rkT[r, j, 0:P], rqT[r, j, 0:2 * P], start=True, stop=True)
                pe.matmul(b[:, 2 * P:3 * P], rkT[r, j, P:2 * P], rqT[r, j, P:2 * P], start=True, stop=True)
                pe.matmul(b[0:NS, 3 * P:TRI], rkT[r, j, 2 * P:NT], rqT[r, j, 2 * P:NT], start=True, stop=True)\
                    .then_inc(sem("ret_scores"), 1)

            def outputs(h):
                pe.wait_ge(sem("ret_scaled"), h + 1)
                if h >= 2:
                    pe.wait_ge(sem("ret_out"), h - 1)
                if h % 2 == 0:
                    pe.wait_ge(sem(f"st{h // 2 % 2}_loaded"), 16 * (h // 4 + 1))
                b, s, v = bank[2 + h % 2], sc_sb[:, h % 2, :], slice(DV * h, DV * h + DV)
                pe.matmul(b[:, 0:2 * P], rv[:, 0, v], s[:, 0:2 * P], start=True, stop=False)
                pe.matmul(b[:, P:2 * P], rv[:, 1, v], s[:, 2 * P:3 * P], start=False, stop=True)
                mm = pe.matmul(b[:, 2 * P:NT], rv[0:NS, 2, v], s[0:NS, 3 * P:TRI], start=True, stop=False)
                if h % 2 == 1:
                    mm.then_inc(sem("ret_own_done"), 1)
                    pe.wait_ge(sem("ret_own_done"), h // 2 + 1)
                for n in range(DEC_BATCH):
                    at = slice(2 * P + 8 * n, 2 * P + 8 * n + 8)
                    mm = pe.matmul(b[:, at], st[h // 2 % 2][rows(h), n, :], qdT[rows(h), h // 2, 8 * n:8 * n + 8],
                                   start=False, stop=(n == DEC_BATCH - 1))
                mm.then_inc(sem("ret_o"), 1)

            def states(h):
                if h == 0:
                    pe.wait_ge(sem("k_decayed"), 1)
                kd = slice(HD * h, HD * h + HD)
                if h % 2 == 0 and h >= 2:
                    pe.wait_ge(sem("ret_p_taken"), h // 2)
                    pe.wait_ge(sem("st_updated"), h // 2)
                pe.matmul(bank[5][rows(h), 0:DV], rk[:, 0, kd], rv[:, 0, DV * h:DV * h + DV], start=True, stop=False)
                pe.matmul(bank[5][rows(h), 0:DV], rk[:, 1, kd], rv[:, 1, DV * h:DV * h + DV], start=False, stop=True)\
                    .then_inc(sem("ret_p_state"), 1)
                pe.wait_ge(sem("rv_spread"), h + 1)
                for half in range(2):
                    mm = pe.matmul(bank[6 + half][rows(h), :], rk[0:NS, 2, kd],
                                   rv_bd[0:NS, 4 * half:4 * half + 4, :], start=True, stop=True)
                mm.then_inc(sem("ret_s_state"), 1)

            def sums(h):
                pe.wait_ge(sem("ret_sq"), h + 1)
                if h >= 1:
                    pe.wait_ge(sem("ret_root"), h)
                pe.matmul(bank[4][:, 0:NT], ones[:, :], ro_sq, start=True, stop=True).then_inc(sem("ret_sum"), 1)

            pe.wait_ge(sem("turn_taken"), len(TURNS))
            scores(0)
            for h in range(HEADS):
                if h + 1 < HEADS:
                    scores(h + 1)
                if h:
                    sums(h - 1)
                outputs(h)
                states(h)
            sums(HEADS - 1)

        def retention_dve(dve, own):
            rk, rv = q_tok["rk"], q_tok["rv"]
            dve.wait_ge(sem("turned"), 8)
            own.step_to(dve.tensor_tensor(heads(rk), heads(rk), kdec[:, :, :].unsqueeze(3).to_broadcast([P, 3, HEADS, HD]),
                                         ALU.mult), sem("k_decayed"), 1)

            def scale(h):
                dve.wait_ge(sem("ret_scores"), h + 1)
                dve.wait_ge(sem(f"dmat{h % 2}_loaded"), 16 * (h // 2 + 1))
                if h >= 2:
                    dve.wait_ge(sem("ret_o"), h - 1)
                (bp, bs), (dp, ds), (sp_, ss) = (causal_parts(x) for x in (bank[h % 2], dmat[:, h % 2, :], sc_sb[:, h % 2, :]))
                own(dve.tensor_tensor(sp_, bp, dp, ALU.mult))
                own.step_to(dve.tensor_tensor(ss, bs, ds, ALU.mult), sem("ret_scaled"), h + 1)

            def spread(h):
                if h:
                    dve.wait_ge(sem("ret_s_state"), h)
                own.step_to(dve.tensor_tensor(rv_bd[0:NS, :, :],
                                             rv[0:NS, 2, DV * h:DV * h + DV].unsqueeze(1).to_broadcast([NS, 8, DV]),
                                             bmask[:, :].unsqueeze(2).to_broadcast([NS, 8, DV]), ALU.mult),
                           sem("rv_spread"), h + 1)

            def update(p):
                dve.wait_ge(sem("ret_s_state"), 2 * p + 2)
                for half in range(2):
                    s = st[p % 2][:, 4 * half:4 * half + 4, :].rearrange("p a b -> p (a b)")
                    ins = dve.scalar_tensor_tensor(out=s, in0=s, scalar=stdec[:, p:p + 1], in1=bank[6 + half][:, :],
                                                   op0=ALU.mult, op1=ALU.add)
                    if half == 0:
                        own(ins)
                own.step_to(ins, sem("st_updated"), p + 1)

            def out(h):
                dve.wait_ge(sem("ret_root"), h + 1)
                own(dve.reciprocal(ro_rs, ro_rs))
                own.settle()
                own(dve.tensor_tensor(ro_sq, bank[2 + h % 2][:, 0:NT], ro_rs, ALU.mult))
                own.settle()
                own.step_to(dve.tensor_tensor(catT[:, h, :], catT[:, h, :], ro_sq, ALU.mult), sem("ret_out"), h + 1)

            for h in range(HEADS):
                if h == 0:
                    dve.wait_ge(sem("proj_done"), 29)
                scale(h)
                spread(h)
                if h >= 2 and h % 2 == 0:
                    update(h // 2 - 1)
                if h:
                    if h == 1:
                        dve.wait_ge(sem("proj_taken"), 29)
                    out(h - 1)
            update(3)
            out(HEADS - 1)
            own.settle()

        def retention_act(act, own):
            for h in range(HEADS):
                act.wait_ge(sem("ret_o"), h + 1)
                if h:
                    act.wait_ge(sem("ret_out"), h)
                own.step_to(act.activation(ro_sq, bank[2 + h % 2][:, 0:NT], ACT.Square), sem("ret_sq"), h + 1)
                if h % 2 == 1:
                    act.wait_ge(sem("ret_p_state"), h + 1)
                    own.step_to(act.copy(ret_p[:, h // 2, :], bank[5][:, 0:DV]), sem("ret_p_taken"), h // 2 + 1)
                act.wait_ge(sem("ret_sum"), h + 1)
                own.step_to(act.activation(ro_rs, bank[4][:, 0:NT], ACT.Sqrt, bias=eps[:, :], scale=1.0 / DV),
                           sem("ret_root"), h + 1)

        def retention_pool(pool):
            def load_state(p):
                if p < 2:
                    pool.wait_ge(sem("turned"), [13, 13][p])
                    pool.wait_ge(sem("turn_taken"), 12)
                else:
                    pool.wait_ge(sem(f"st{p % 2}_stored"), 16)
                pool.dma_start(st[p % 2], d["state_ret"][0][:, 2 * p:2 * p + 2].rearrange("b h k v -> (h k) b v"))\
                    .then_inc(sem(f"st{p % 2}_loaded"), 16)

            load_state(0)
            load_state(1)
            for h in range(HEADS):
                if h >= 2:
                    pool.wait_ge(sem("ret_scaled"), h - 1)
                pool.dma_start(dmat[:, h % 2, :], d["c_dmat"][h]).then_inc(sem(f"dmat{h % 2}_loaded"), 16)
                if h >= 3 and h % 2 == 1:
                    store_state(pool, h // 2 - 1)
                    if h // 2 + 1 < 4:
                        load_state(h // 2 + 1)
            store_state(pool, 3)
            pool.wait_ge(sem("ret_p_taken"), 4)
            pool.dma_start(d["ret_prompt"][0, 0].rearrange("(j h) k v -> (h k) j v", h=2), ret_p)\
                .then_inc(sem("stored"), 16)

        def store_state(pool, p):
            pool.wait_ge(sem("st_updated"), p + 1)
            pool.dma_start(d["ret_sample"][0][:, 2 * p:2 * p + 2].rearrange("b h k v -> (h k) b v"), st[p % 2])\
                .then_inc(sem(f"st{p % 2}_stored"), 16)

        def kv_pool(pool):
            for name, ready, n in (("k", "roped", 4), ("v", "proj_taken", 15)):
                pool.wait_ge(sem(ready), n)
                x = q_tok["m" + name]
                pool.dma_start(d[name + "_prompt"][0, 0].rearrange("(t p) h e -> p t (h e)", p=P), x[:, 0:2, :])\
                    .then_inc(sem("stored"), 16)
                pool.dma_start(d[name + "_sample"][0].rearrange("b t h e -> (b t) (h e)"), x[0:NS, 2, :])\
                    .then_inc(sem("stored"), 16)

        def prompt_attn_pe(pe):
            mv = q_tok["mv"]

            def scores(h):
                if h < 2:
                    pe.wait_ge(sem("ret_scaled"), HEADS)
                else:
                    pe.wait_ge(sem("pm_masked"), h - 1)
                b, r, j = bank[h % 2], rows(h), h // 2
                pe.matmul(b[:, 0:P], mqT[r, j, 0:P], mkT[r, j, 0:P], start=True, stop=True)
                pe.matmul(b[:, P:3 * P], mqT[r, j, P:2 * P], mkT[r, j, 0:2 * P], start=True, stop=True)\
                    .then_inc(sem("pm_scores"), 1)

            scores(0)
            scores(1)
            for h in range(HEADS):
                pe.wait_ge(sem("pm_probs"), h + 1)
                if h < 2:
                    pe.wait_ge(sem("ret_out"), HEADS)
                if h >= 2:
                    pe.wait_ge(sem("pm_T_taken"), h - 1)
                b = bank[2 + h % 2]
                for i in range(3):
                    mm = pe.transpose(b[:, P * i:P * i + P], pm_s[:, h % 2, P * i:P * i + P], ident[:, :])
                mm.then_inc(sem("pm_T"), 1)
                if h + 2 < HEADS:
                    scores(h + 2)
                pe.wait_ge(sem("pm_T_taken"), h + 1)
                if h in (0, 2):
                    pe.wait_ge(sem("ret_root"), HEADS)
                    pe.wait_ge(sem("ret_p_taken"), 4)
                if h >= 4 and h % 2 == 0:
                    pe.wait_ge(sem("pm_out"), h // 2 - 1)
                o, v, pT = bank[4 + h // 2 % 2], slice(HD * h, HD * h + HD), pm_T[:, h % 2, :]
                pe.matmul(o[rows(h), 0:2 * P], mv[:, 0, v], pT[:, 0:2 * P], start=True, stop=False)
                pe.matmul(o[rows(h), P:2 * P], mv[:, 1, v], pT[:, 2 * P:3 * P], start=False, stop=True)\
                    .then_inc(sem("pm_o"), 1)

        def prompt_attn_dve(dve, own):
            def mask(h):
                dve.wait_ge(sem("pm_scores"), h + 1)
                if h == 0:
                    dve.wait_ge(sem("ret_o"), HEADS)
                    dve.wait_ge(sem("ret_s_state"), HEADS)
                    dve.wait_ge(sem("maskp_loaded"), 16)
                if h >= 2:
                    dve.wait_ge(sem("pm_T"), h - 1)
                s, m = pm_s[:, h % 2, :], small[:, 64 + 8 * (h % 2):72 + 8 * (h % 2)]
                own.step_to(dve.tensor_tensor(s, bank[h % 2][:, 0:3 * P], maskp, ALU.add), sem("pm_masked"), h + 1)
                own.settle()
                own(dve.tensor_reduce(m[:, 0:1], s[:, 0:P], AX_X, ALU.max))
                own(dve.tensor_reduce(m[:, 1:2], s[:, P:3 * P], AX_X, ALU.max))
                own.settle()
                own.step_to(dve.tensor_scalar(m[:, 2:4], m[:, 0:2], -QK_SCALE, None, ALU.mult), sem("pm_max"), h + 1)

            def probs(h):
                dve.wait_ge(sem("pm_exp"), h + 1)
                s, m = pm_s[:, h % 2, :], small[:, 64 + 8 * (h % 2):72 + 8 * (h % 2)]
                own(dve.reciprocal(m[:, 6:8], m[:, 4:6]))
                own.settle()
                own(dve.tensor_scalar(s[:, 0:P], s[:, 0:P], m[:, 6:7], None, ALU.mult))
                own.step_to(dve.tensor_scalar(s[:, P:3 * P], s[:, P:3 * P], m[:, 7:8], None, ALU.mult), sem("pm_probs"), h + 1)

            mask(0)
            for h in range(HEADS):
                if h + 1 < HEADS:
                    mask(h + 1)
                probs(h)
            own.settle()

        def prompt_attn_act(act, own):
            def exps(h):
                act.wait_ge(sem("pm_max"), h + 1)
                s, m = pm_s[:, h % 2, :], small[:, 64 + 8 * (h % 2):72 + 8 * (h % 2)]
                own(act.activation(s[:, 0:P], s[:, 0:P], ACT.Exp, bias=m[:, 2:3], scale=QK_SCALE, accum_out=m[:, 4:5]))
                own.step_to(act.activation(s[:, P:3 * P], s[:, P:3 * P], ACT.Exp, bias=m[:, 3:4], scale=QK_SCALE,
                                          accum_out=m[:, 5:6]), sem("pm_exp"), h + 1)

            exps(0)
            for h in range(HEADS):
                if h + 1 < HEADS:
                    exps(h + 1)
                act.wait_ge(sem("pm_T"), h + 1)
                if h >= 2:
                    act.wait_ge(sem("pm_o"), h - 1)
                own.step_to(act.copy(pm_T[:, h % 2, :], bank[2 + h % 2][:, 0:3 * P]), sem("pm_T_taken"), h + 1)
                if h % 2 == 1:
                    act.wait_ge(sem("pm_o"), h + 1)
                    own.step_to(act.copy(catT[:, 8 + h // 2, 0:SEQ], bank[4 + h // 2 % 2][:, 0:SEQ]), sem("pm_out"), h // 2 + 1)

        def load_consts(act):
            loads = [(ident[:, :], d["c_ident"]), (ones[:, :], d["c_ones"]), (cos[:, :, :], d["c_cos"]),
                     (sin[:, :, :], d["c_sin"]), (kdec[:, :, :], d["c_kdec"]), (qdec[:, :], d["c_qdec"]),
                     (stdec[:, :], d["c_stdec"]), (bmask[:, :], d["c_bmask"]),
                     (g_mix[:, :, :], d["norm_mix"]), (g_ffn[:, :, :], d["norm_ffn"]),
                     (qg[:, :], d["q_norm"].to_broadcast([P, HD])), (kg[:, :], d["k_norm"].to_broadcast([P, HD])),
                     (earlier[:, :], d["c_earlier"]), (number[:, :], d["c_number"]),
                     (pages[:, :], d["page_table"].rearrange("b n -> (b n)").rearrange("(a n) -> a n", a=1))]
            assert len(loads) == N_CONSTS
            for dst, src in loads:
                act.dma_start(dst, src).then_inc(sem("consts_loaded"), 16)

        free1, free2 = ring[:, 1, :], ring[:, 2, :]
        k_pg = part(0, 2, 4, 512)
        v_pg = part(4096, 4, 4, 512)
        kT = part(12288, 2, 4, 512)
        own_kT = part(16384, 4, NS)
        own_v = part(1280, 512, of=free1)
        o_rows = part(1800, 512, of=free1)
        q_diag = part(0, 8, 4, NS, of=xn_flat)
        pT = part(2048, N_PAGES, NS, of=xn_flat)
        sc_mask = part(0, 8, NS, of=free1)
        q_now = part(512, 4, NS, of=free1)
        s_own = part(768, 2, NS, of=free1)
        pT_own = part(896, NS, of=free1)
        before = part(960, 8, 8, of=free1)
        rank_a, rank_b = part(1024, 8, 8, of=free1), part(1088, 8, 8, of=free1)
        blk_sum = part(1152, 2, 8, of=free1)
        rank, blk_off = part(1168, 8, of=free1), part(1176, 8, of=free1)
        blk_max = part(1184, 16, of=free1)
        exp_off = part(1200, 2, 16, of=free1)
        exp_sum = part(1232, 2, 16, of=free1)
        probs = part(0, 2, PAST_LEN, of=free2)
        R = slice(0, NS)

        def sample_setup_dve(dve, own):
            dve.wait_ge(sem("pm_o"), HEADS)
            dve.wait_ge(sem("pm_T"), HEADS)
            own(dve.memset(q_diag, 0.0))
            own(dve.tensor_copy(own_kT, mkT[:, :, 2 * P:NT]))
            own(dve.tensor_copy(own_v[R, :], q_tok["mv"][R, 2, :]))
            own.settle()
            for h in range(HEADS):
                ins = dve.tensor_copy(q_diag[rows(h), :, h // 2, 8 * h:8 * h + 8],
                                      mqT[rows(h), h // 2, 2 * P:NT].rearrange("p (b t) -> p b t", t=DEC_SEQ))
                if h < HEADS - 1:
                    own(ins)
            own.step_to(ins, sem("sm_ready"), 1)
            own.settle()

        def pages_sp(sp):
            def load(cache, dst, b, q, s):
                for k in range(4):
                    page = sp.value_load(pages[0:1, bass.ds(16 * b + 4 * q + k, 1)], min_val=0, max_val=d["cache_k"].shape[1] - 1)
                    sp.dma_start(dst[:, k, :], d[cache][0][bass.ds(page, 1)].rearrange("a s h e -> s (a h e)"))\
                        .then_inc(sem(s), 16)

            def keys(b, q):
                if not (isinstance(b, int) and 4 * b + q < 2):
                    sp.wait_ge(sem("kt_turned"), 16 * b + 4 * q - 4)
                load("cache_k", k_pg[:, q % 2], b, q, f"k{q % 2}_loaded")

            def values(b):
                if not (isinstance(b, int) and b == 0):
                    sp.wait_ge(sem("sm_o"), b)
                for q in range(4):
                    load("cache_v", v_pg[:, q], b, q, "v_loaded")

            sp.wait_ge(sem("consts_loaded"), 16 * N_CONSTS)
            sp.wait_ge(sem("sm_ready"), 1)
            sp.wait_ge(sem("stored"), 80)
            sp.wait_ge(sem("st0_stored"), 32)
            sp.wait_ge(sem("st1_stored"), 32)
            keys(0, 0)
            keys(0, 1)

            def turn(b, first=False, last=False):
                keys(b, 2)
                keys(b, 3)
                if not first:
                    values(b - 1)
                if not last:
                    keys(b + 1, 0)
                    keys(b + 1, 1)

            turn(0, first=True)
            turn(1)
            with sp.Fori(2, DEC_BATCH - 1) as b:
                turn(b)
            turn(DEC_BATCH - 1, last=True)
            values(DEC_BATCH - 1)

        def over_samples(eng, own, turn, steps):
            turn(0, 0, first=True)
            turn(1, 1)
            with eng.Fori(1, DEC_BATCH // 2) as i:
                if own:
                    own.turn(i, 1, steps)
                turn(2 * i, 0)
                turn(2 * i + 1, 1)
                if own:
                    own.end(DEC_BATCH // 2 - 1)
            turn(DEC_BATCH, 0, last=True)

        def wait_pos(eng, s, value):
            if not (isinstance(value, int) and value <= 0):
                eng.wait_ge(sem(s), value)

        def sample_attn_pe(pe):
            def turn_keys(b, q):
                pe.wait_ge(sem(f"k{q % 2}_loaded"), 64 * (2 * b + q // 2 + 1))
                for j in range(4):
                    wait_pos(pe, ["kt_taken_a", "kt_taken_d"][j % 2], 8 * b + 2 * q + j // 2)
                    for k in range(4):
                        mm = pe.transpose(bank[j % 2][:, P * k:P * k + P], k_pg[:, q % 2, k, P * j:P * j + P], ident[:, :])
                    mm.then_inc(sem("kt_turned"), 1)

            def scores(b, q):
                pe.wait_ge(sem("kt_taken_a"), 8 * b + 2 * q + 2)
                pe.wait_ge(sem("kt_taken_d"), 8 * b + 2 * q + 2)
                wait_pos(pe, "s_taken", 4 * b + q - 1)
                if q == 0:
                    pe.wait_ge(sem("q_now_set"), b + 1)
                for j in range(4):
                    mm = pe.matmul(bank[2 + q % 2][R, :], q_now[:, j, :], kT[:, q % 2, j, :], start=(j == 0), stop=(j == 3))
                mm.then_inc(sem("s_done"), 1)

            def own_scores(b):
                wait_pos(pe, "own_taken", b)
                for j in range(4):
                    mm = pe.matmul(bank[4][R, 0:NS], q_now[:, j, :], own_kT[:, j, :], start=(j == 0), stop=(j == 3))
                mm.then_inc(sem("own_done"), 1)

            def values(b, par):
                pe.wait_ge(sem("sm_ready"), 1)
                pe.wait_ge(sem("sm_p"), b + 1)
                wait_pos(pe, "sm_out", b)
                for pg in range(N_PAGES):
                    pe.transpose(bank[5 + pg // 8][:, NS * (pg % 8):NS * (pg % 8) + NS], probs[R, par, PAGE * pg:PAGE * pg + PAGE],
                                 ident[R, R])
                pe.transpose(bank[7][R, 0:NS], s_own[R, par, :], ident[R, R]).then_inc(sem("p_turned"), 1)
                pe.wait_ge(sem("p_taken"), b + 1)
                pe.wait_ge(sem("v_loaded"), 256 * (b + 1))
                for pg in range(N_PAGES):
                    pe.matmul(bank[7][R, :], pT[:, pg, :], v_pg[:, pg // 4, pg % 4, :], start=(pg == 0), stop=False)
                mm = pe.matmul(bank[7][R, :], pT_own[R, :], own_v[R, :], start=False, stop=True)
                mm.then_inc(sem("sm_o"), 1)

            def turn_outputs(b):
                for j in range(4):
                    mm = pe.transpose(bank[5][:, NS * j:NS * j + NS], o_rows[R, P * j:P * j + P], ident[R, R])
                mm.then_inc(sem("o_turned"), 1)

            def turn(b, par, first=False, last=False):
                if not last:
                    turn_keys(b, 0)
                third = not (isinstance(b, int) and b < 2)
                if third:
                    pe.wait_ge(sem("o_taken"), b - 1)
                if not last:
                    turn_keys(b, 1)
                if third:
                    turn_outputs(b - 2)
                if not last:
                    scores(b, 0)
                    turn_keys(b, 2)
                    scores(b, 1)
                    turn_keys(b, 3)
                    scores(b, 2)
                    scores(b, 3)
                    own_scores(b)
                if not first:
                    values(b - 1, 1 - par)

            pe.wait_ge(sem("sm_ready"), 1)
            pe.wait_ge(sem("pm_out"), 4)
            over_samples(pe, None, turn, 0)
            pe.wait_ge(sem("o_taken"), DEC_BATCH)
            turn_outputs(DEC_BATCH - 1)

        def sample_attn_act(act, own):
            def keys(b, q):
                wait_pos(act, "s_done", 4 * b + q - 1)
                for j in (0, 2):
                    act.wait_ge(sem("kt_turned"), 16 * b + 4 * q + j + 1)
                    act.copy(kT[:, q % 2, j, :], bank[0][:, :]).then_inc(sem("kt_taken_a"), 1)

            def scores(b, q, par):
                act.wait_ge(sem("s_done"), 4 * b + q + 1)
                if q == 0:
                    wait_pos(act, "p_turned", b - 1)
                for half in range(2):
                    n = 2 * q + half
                    ins = act.activation(probs[R, par, BLOCK * n:BLOCK * n + BLOCK],
                                         bank[2 + q % 2][R, BLOCK * half:BLOCK * half + BLOCK], ACT.Identity,
                                         accum_out=blk_sum[R, par, n:n + 1])
                    if half == 0:
                        own(ins)
                ins.then_inc(sem("s_taken"), 1)

            def exps(b, par):
                act.wait_ge(sem("sm_max"), b + 1)
                for n in range(N_BLOCKS):
                    p = probs[R, par, BLOCK * n:BLOCK * n + BLOCK]
                    own(act.activation(p, p, ACT.Exp, bias=exp_off[R, par, n:n + 1], scale=QK_SCALE,
                                       accum_out=exp_sum[R, par, n:n + 1]))
                act.activation(s_own[R, par, :], s_own[R, par, :], ACT.Exp, bias=exp_off[R, par, 8:9], scale=QK_SCALE,
                               accum_out=exp_sum[R, par, 8:9]).then_inc(sem("sm_exp"), 1)

            def turned(b):
                act.wait_ge(sem("p_turned"), b + 1)
                for half in range(2):
                    own(act.copy(pT[:, 8 * half:8 * half + 8, :], bank[5 + half][:, :].rearrange("p (a r) -> p a r", a=8)))
                act.copy(pT_own[R, :], bank[7][R, 0:NS]).then_inc(sem("p_taken"), 1)
                act.wait_ge(sem("sm_o"), b + 1)
                act.copy(o_rows[R, :], bank[7][R, :]).then_inc(sem("o_taken"), 1)

            def turn(b, par, first=False, last=False):
                if not last:
                    keys(b, 0)
                    keys(b, 1)
                    scores(b, 0, par)
                if not first:
                    exps(b - 1, 1 - par)
                if not last:
                    keys(b, 2)
                    scores(b, 1, par)
                    keys(b, 3)
                    scores(b, 2, par)
                    scores(b, 3, par)
                if not first:
                    turned(b - 1)

            act.wait_ge(sem("sm_ready"), 1)
            over_samples(act, own, turn, 2 * (4 + 8 + 2))

        def sample_attn_dve(dve, own):
            def set_queries(b):
                wait_pos(dve, "own_done", b)
                dve.tensor_scalar(q_now, q_diag[:, bass.ds(b, 1), :, :].rearrange("p a j r -> p (a j) r"), 1.0, None,
                                  ALU.mult).then_inc(sem("q_now_set"), 1)

            def keys(b, q):
                wait_pos(dve, "s_done", 4 * b + q - 1)
                for j in (1, 3):
                    dve.wait_ge(sem("kt_turned"), 16 * b + 4 * q + j + 1)
                    dve.tensor_copy(kT[:, q % 2, j, :], bank[1][:, :]).then_inc(sem("kt_taken_d"), 1)

            def maxima(b, par):
                dve.wait_ge(sem("own_done"), b + 1)
                dve.tensor_tensor(s_own[R, par, :], bank[4][R, 0:NS],
                                  sc_mask[R, bass.ds(b, 1), :].rearrange("p a n -> p (a n)"), ALU.add).then_inc(sem("own_taken"), 1)
                dve.wait_ge(sem("s_taken"), 4 * b + 4)
                own(dve.tensor_reduce(blk_max[R, 0:8], probs[R, par, :].rearrange("p (n k) -> p n k", k=BLOCK), AX_X, ALU.max))
                g = blk_sum[R, par, :]
                theirs, mine = g.unsqueeze(1).to_broadcast([NS, 8, 8]), g.unsqueeze(2).to_broadcast([NS, 8, 8])
                own(dve.tensor_tensor(rank_a[R], theirs, mine, ALU.is_gt))
                own(dve.tensor_tensor(rank_b[R], theirs, mine, ALU.is_equal))
                own.settle()
                own(dve.tensor_tensor(rank_b[R], rank_b[R], before[R], ALU.mult))
                own.settle()
                own(dve.tensor_tensor(rank_a[R], rank_a[R], rank_b[R], ALU.add))
                dve.wait_ge(sem("own_taken"), b + 1)
                own(dve.tensor_reduce(blk_max[R, 8:9], s_own[R, par, :], AX_X, ALU.max))
                own.settle()
                own(dve.tensor_reduce(rank[R, :], rank_a[R], AX_X, ALU.add))
                own.settle()
                own(dve.tensor_scalar(blk_off[R, :], rank[R, :], float(TOPK), NEG, ALU.is_ge, ALU.mult))
                own.settle()
                own(dve.tensor_tensor(blk_max[R, 0:8], blk_max[R, 0:8], blk_off[R, :], ALU.add))
                own.settle()
                own(dve.tensor_reduce(blk_max[R, 9:10], blk_max[R, 0:9], AX_X, ALU.max))
                own.settle()
                own(dve.tensor_scalar(exp_off[R, par, 8:9], blk_max[R, 9:10], -QK_SCALE, None, ALU.mult))
                own.settle()
                dve.tensor_scalar(exp_off[R, par, 0:8], blk_off[R, :], QK_SCALE, exp_off[R, par, 8:9], ALU.mult, ALU.add)\
                    .then_inc(sem("sm_max"), 1)

            def normalise(b, par):
                dve.wait_ge(sem("sm_exp"), b + 1)
                own(dve.tensor_reduce(exp_sum[R, par, 9:10], exp_sum[R, par, 0:9], AX_X, ALU.add))
                own.settle()
                own(dve.reciprocal(exp_sum[R, par, 10:11], exp_sum[R, par, 9:10]))
                own.settle()
                own(dve.tensor_scalar(probs[R, par, :], probs[R, par, :], exp_sum[R, par, 10:11], None, ALU.mult))
                dve.tensor_scalar(s_own[R, par, :], s_own[R, par, :], exp_sum[R, par, 10:11], None, ALU.mult)\
                    .then_inc(sem("sm_p"), 1)

            def outputs(b):
                dve.wait_ge(sem("o_turned"), b + 1)
                o = bank[5][:, 0:320].rearrange("p (j w) -> p j w", w=NS + 16)
                for g in range(2):
                    r = slice(HD * g, HD * g + HD)
                    ins = dve.tensor_scalar(catT[r, 8:12, bass.ds(SEQ + DEC_SEQ * b, DEC_SEQ)], o[r, :, DEC_SEQ * g:DEC_SEQ * g + DEC_SEQ], 1.0, None, ALU.mult)
                    if g == 0:
                        own(ins)
                ins.then_inc(sem("sm_out"), 1)

            def turn(b, par, first=False, last=False):
                if not last:
                    set_queries(b)
                    keys(b, 0)
                    keys(b, 1)
                if not (isinstance(b, int) and b < 2):
                    outputs(b - 2)
                if not first:
                    maxima(b - 1, 1 - par)
                if not last:
                    keys(b, 2)
                    keys(b, 3)
                if not first:
                    normalise(b - 1, 1 - par)

            dve.wait_ge(sem("masks_loaded"), 32)
            over_samples(dve, own, turn, 2 * 15)
            outputs(DEC_BATCH - 1)
            dve.wait_ge(sem("sm_out"), 8)

        def even_out_pe(pe):
            pe.wait_ge(sem("sm_out"), DEC_BATCH)
            for s in (3, 4, 5):
                slot_loaded(pe, s, 2)
            for c in range(KC):
                if c >= 4:
                    pe.wait_ge(sem("h_ready"), KC + c - 3)
                for k in range(12):
                    mm = pe.matmul(bank[c % 4][:, 0:NT], slot_f[3 + k // 4][:, k % 4, P * c:P * c + P], catT[:, k, :],
                                   start=(k == 0), stop=(k == 11))
                mm.then_inc(sem("even_out"), 1)

        def even_out_dve(dve, own):
            for c in range(KC):
                dve.wait_ge(sem("even_out"), c + 1)
                own.step_to(dve.tensor_tensor(hT[:, c, :], hT[:, c, :], bank[c % 4][:, 0:NT], ALU.add), sem("h_ready"), KC + c + 1)
            own.settle()

        gates = part(0, N_EXPERTS, NT)
        hid = part(5120, 2, FC, NT)
        sil = part(7680, 2, NT)
        gu = part(8320, 2, NT)
        logit = part(16200, 3, 20)
        ra, rb, rc, rd, re_, rf = (part(16300 + 12 * i, 3, 4) for i in range(6))
        r16 = part(16400, 3, 16)
        gate_tok = part(16460, 3, 16)
        r1 = [part(16520 + 3 * i, 3, 1) for i in range(10)]
        gate_T = part(16600, NT)
        chosen, place = part(16920, 3, 16), part(16970, 3, 16)
        counts, firsts, running = part(17020, 16), part(17040, 2, 16), part(17080, 16)

        GATHER, PUT, SLOTWISE, MOVES = 6, 6 + 2 * KC, 6 + 2 * KC + N_PAIRS // P, 6 + 2 * KC + 3 * (N_PAIRS // P)

        def moved_in(i):
            return bank[3 + i % 2]

        def to_bank(pe, l, i):
            if i >= 2:
                pe.wait_ge(sem("moved_taken"), MOVES * l + i - 1)

        def route_pe(pe, l):
            pe.wait_ge(sem("xn_ready"), 2 + 2 * l)
            pe.wait_ge(sem("wr_loaded"), 64)
            for t in range(3):
                for k in range(KC):
                    mm = pe.matmul(bank[0][:, 20 * t:20 * t + 20], xnT[:, k, P * t:P * t + P], wr[:, l, k, :],
                                   start=(k == 0), stop=(k == KC - 1))
            mm.then_inc(sem("routed"), 1)
            for i, (t, half) in enumerate((t, half) for t in range(3) for half in range(2)):
                n = P if t < 2 else NS
                to_bank(pe, l, i)
                for c in range(4):
                    mm = pe.transpose(moved_in(i)[0:n, P * c:P * c + P], xnT[:, 4 * half + c, P * t:P * t + n], ident[:, :])
                mm.then_inc(sem("moved"), 1)
            pe.wait_ge(sem("route_step"), 4 * l + 3)
            for t in range(4):
                for u in range(min(t + 1, 3)):
                    mm = pe.matmul(bank[1][:, 16 * t:16 * t + 16], earlier[:, :] if u == t else ones[:, :], chosen[:, u, :],
                                   start=(u == 0), stop=(u == min(t, 2)))
            mm.then_inc(sem("routed"), 1)

        def gate_rows_pe(pe, l):
            pe.wait_ge(sem("route_step"), 4 * l + 4)
            for t, n in ((0, P), (1, P), (2, NS)):
                mm = pe.transpose(bank[0][0:16, P * t:P * t + n], gate_tok[0:n, t, :], ident[0:n, 0:n])
            mm.then_inc(sem("gate_turned"), 1)

        def route_act(act, own, l):
            for i in range(2):
                act.wait_ge(sem("route_step"), 4 * l + i + 1)
                own.step_to(act.activation(ra, ra, ACT.Exp), sem("route_exp"), 2 * l + i + 1)
            for i in range(6):
                t, n = i // 2, (P if i < 4 else NS)
                act.wait_ge(sem("moved"), MOVES * l + i + 1)
                own.step_to(act.copy(xn_tok[0:n, t, 512 * (i % 2):512 * (i % 2) + 512], moved_in(i)[0:n, :]),
                            sem("moved_taken"), MOVES * l + i + 1)
            own.settle()

        def gate_rows_act(act, l):
            act.wait_ge(sem("gate_turned"), l + 1)
            act.copy(gate_T[0:16, :], bank[0][0:16, 0:NT]).then_inc(sem("gate_row"), 1)
            act.wait_ge(sem("gate_row"), l + 1)
            act.dma_start(gate_dram[l], gate_T[0:16, :]).then_inc(sem("gate_out"), 16)
            act.wait_ge(sem("gate_out"), 16 * (l + 1))
            act.dma_start(gates, gate_dram[l].rearrange("e n -> (e n)").rearrange("(a m) -> a m", a=1)
                          .to_broadcast([P, N_EXPERTS * NT]).rearrange("p (e n) -> p e n", e=N_EXPERTS))\
                .then_inc(sem("gates_loaded"), 16)

        def route_dve(dve, own, l):
            def step(ins):
                own(ins)
                own.settle()

            wide = lambda x, n=4: x.to_broadcast([P, 3, n])

            def first_hot(eq, rem):
                step(dve.tensor_scalar(rem, eq[:, :, 0:1], -1.0, 1.0, ALU.mult, ALU.add))
                for i in range(1, 4):
                    step(dve.tensor_tensor(eq[:, :, i:i + 1], eq[:, :, i:i + 1], rem, ALU.mult))
                    if i < 3:
                        step(dve.tensor_tensor(rem, rem, eq[:, :, i:i + 1], ALU.subtract))

            def shifted_exp(x, m, i):
                step(dve.tensor_reduce(m, x, AX_X, ALU.max))
                own.step_to(dve.tensor_tensor(ra, x, wide(m), ALU.subtract), sem("route_step"), 4 * l + i + 1)

            def exp_sum_of(m, i):
                dve.wait_ge(sem("route_exp"), 2 * l + i + 1)
                step(dve.tensor_reduce(m, ra, AX_X, ALU.add))
                step(dve.reciprocal(m, m))

            dve.wait_ge(sem("routed"), 2 * l + 1)
            step(dve.tensor_copy(logit, bank[0][:, 0:60].rearrange("p (t n) -> p t n", t=3)))
            lg, le = logit[:, :, 0:4], logit[:, :, 4:20].rearrange("p t (g e) -> p t g e", g=4)
            mg, wg, rem, m2, v, v2, ts = r1[:7]
            step(dve.tensor_reduce(mg, lg, AX_X, ALU.max))
            step(dve.tensor_tensor(rb, lg, wide(mg), ALU.is_equal))
            shifted_exp(lg, wg, 0)
            first_hot(rb, rem)
            exp_sum_of(wg, 0)
            step(dve.tensor_tensor(r16.rearrange("p t (g e) -> p t g e", g=4), le,
                                   rb.unsqueeze(3).to_broadcast([P, 3, 4, 4]), ALU.mult))
            step(dve.tensor_reduce(rc, r16.rearrange("p t (g e) -> p t e g", g=4), AX_X, ALU.add))
            shifted_exp(rc, m2, 1)
            exp_sum_of(m2, 1)
            step(dve.tensor_tensor(rc, ra, wide(m2), ALU.mult))
            step(dve.tensor_reduce(v, rc, AX_X, ALU.max))
            step(dve.tensor_tensor(rd, rc, wide(v), ALU.is_equal))
            first_hot(rd, rem)
            step(dve.scalar_tensor_tensor(out=re_, in0=rd, scalar=-2.0, in1=rc, op0=ALU.mult, op1=ALU.add))
            step(dve.tensor_reduce(v2, re_, AX_X, ALU.max))
            step(dve.tensor_tensor(rf, re_, wide(v2), ALU.is_equal))
            first_hot(rf, rem)
            step(dve.tensor_tensor(rd, rd, rf, ALU.add))
            step(dve.tensor_tensor(chosen.rearrange("p t (g e) -> p t g e", g=4), rb.unsqueeze(3).to_broadcast([P, 3, 4, 4]),
                                   rd.unsqueeze(2).to_broadcast([P, 3, 4, 4]), ALU.mult))
            own.step_to(dve.memset(chosen[NS:P, 2, :], 0.0), sem("route_step"), 4 * l + 3)
            step(dve.tensor_tensor(rc, rc, rd, ALU.mult))
            step(dve.tensor_reduce(ts, rc, AX_X, ALU.add))
            step(dve.reciprocal(ts, ts))
            step(dve.tensor_tensor(ts, ts, wg, ALU.mult))
            step(dve.tensor_tensor(rc, rc, wide(ts), ALU.mult))
            step(dve.tensor_tensor(gate_tok.rearrange("p t (g e) -> p t g e", g=4), rb.unsqueeze(3).to_broadcast([P, 3, 4, 4]),
                                   rc.unsqueeze(2).to_broadcast([P, 3, 4, 4]), ALU.mult))
            dve.wait_ge(sem("routed"), 2 * l + 2)
            step(dve.tensor_copy(counts, bank[1][:, 48:64]))
            own(dve.tensor_reduce(most[:, 0:1], counts, AX_X, ALU.max))
            a, b = counts, running
            for shift in (1, 2, 4, 8):
                own(dve.tensor_copy(b[:, 0:shift], a[:, 0:shift]))
                step(dve.tensor_tensor(b[:, shift:16], a[:, shift:16], a[:, 0:16 - shift], ALU.add))
                a, b = b, firsts[:, [1, 2, 4, 8].index(shift) % 2, :]
            first = firsts[:, 1, :]
            step(dve.tensor_tensor(first, a, counts, ALU.subtract))
            own(dve.scalar_tensor_tensor(out=place, in0=bank[1][:, 0:48].rearrange("p (t e) -> p t e", t=3), scalar=1.0,
                                         in1=first.unsqueeze(1).to_broadcast([P, 3, 16]), op0=ALU.add, op1=ALU.add))
            own(dve.tensor_copy(route_i[:, 0:1], most[0:1, 0:1]))
            own.step_to(dve.tensor_copy(route_i[:, 1:17], first[0:1, :]), sem("route_step"), 4 * l + 4)
            own.settle()
            step(dve.tensor_tensor(place, place, chosen, ALU.mult))
            step(dve.tensor_scalar(place, place, -1.0, None, ALU.add))

        def over_experts(eng, own, turn, steps):
            turn(0, 0, 0, first=True)
            turn(1, 1, 0)
            with eng.Fori(1, N_EXPERTS // 2) as i:
                if own:
                    own.turn(i, 1, steps)
                turn(2 * i, 0, i)
                turn(2 * i + 1, 1, i)
                if own:
                    own.end(N_EXPERTS // 2 - 1)
            turn(N_EXPERTS, 0, N_EXPERTS // 2, last=True)

        def slots_before(l, s):
            return 2 if l == 0 else 19 if s < 4 else 10

        UP, DN = FC * N_EXPERTS, KC * N_EXPERTS

        def experts_pe(pe, l):
            def gate_up(e, par, half, f):
                if f == 0:
                    for q in range(2):
                        slot_loaded(pe, 3 * par + q, slots_before(l, 3 * par + q) + half + 1)
                wait_pos(pe, "sil_done", 4 * e + f - 1 + UP * l)
                for q, b in ((0, bank[1 + f % 2]), (1, bank[3 + f % 2])):
                    if q == 1:
                        wait_pos(pe, "hid_done", 4 * e + f - 1 + UP * l)
                    for k in range(KC):
                        mm = pe.matmul(b[:, 0:NT], slot_k[3 * par + q][:, k, P * f:P * f + P], xnT[:, k, 0:NT],
                                       start=(k == 0), stop=(k == KC - 1))
                mm.then_inc(sem("gu_ready"), 1)

            def down(e, par, half):
                slot_loaded(pe, 3 * par + 2, slots_before(l, 3 * par + 2) + half + 1)
                pe.wait_ge(sem("hid_done"), 4 * e + 4 + UP * l)
                for c in range(KC):
                    wait_pos(pe, "acc_done", 8 * e + c - 3 + DN * l)
                    for f in range(FC):
                        mm = pe.matmul(bank[(5 + c % 4) % 8][:, 0:NT], slot_f[3 * par + 2][:, f, P * c:P * c + P],
                                       hid[:, par, f, :], start=(f == 0), stop=(f == FC - 1))
                    mm.then_inc(sem("down_done"), 1)

            def turn(e, par, half, first=False, last=False):
                if not last:
                    gate_up(e, par, half, 0)
                if not first:
                    down(e - 1, 1 - par, half if par else half - 1)
                if not last:
                    for f in range(1, FC):
                        gate_up(e, par, half, f)

            pe.wait_ge(sem("moved_taken"), MOVES * l + GATHER)
            over_experts(pe, None, turn, 0)

        def experts_act(act, l):
            def turn(e, par, half, first=False, last=False):
                if not last:
                    for f in range(FC):
                        act.wait_ge(sem("gu_ready"), 4 * e + f + 1 + UP * l)
                        wait_pos(act, "hid_done", 4 * e + f - 1 + UP * l)
                        act.activation(sil[:, f % 2, :], bank[1 + f % 2][:, 0:NT], ACT.Silu).then_inc(sem("sil_done"), 1)

            over_experts(act, None, turn, 0)

        def experts_dve(dve, l):
            def hidden(e, par, f):
                dve.wait_ge(sem("sil_done"), 4 * e + f + 1 + UP * l)
                wait_pos(dve, "hid_done", 4 * e + f - 1 + UP * l)
                dve.tensor_tensor(gu[:, f % 2, :], sil[:, f % 2, :], bank[3 + f % 2][:, 0:NT], ALU.mult)\
                    .then_inc(sem("gu_done"), 1)
                dve.wait_ge(sem("gu_done"), 4 * e + f + 1 + UP * l)
                wait_pos(dve, "down_done", 8 * e - 8 + DN * l)
                dve.tensor_tensor(hid[:, par, f, :], gu[:, f % 2, :],
                                  gates[:, bass.ds(e, 1), :].rearrange("p a n -> p (a n)"), ALU.mult).then_inc(sem("hid_done"), 1)

            def turn(e, par, half, first=False, last=False):
                if not last:
                    hidden(e, par, 0)
                if not first:
                    for c in range(KC):
                        dve.wait_ge(sem("down_done"), 8 * (e - 1) + c + 1 + DN * l)
                        dve.tensor_tensor(hT[:, c, :], hT[:, c, :], bank[(5 + c % 4) % 8][:, 0:NT], ALU.add)\
                            .then_inc(sem("acc_done"), 1)
                if not last:
                    for f in range(1, FC):
                        hidden(e, par, f)

            dve.wait_ge(sem("gates_loaded"), 16 * (l + 1))
            over_experts(dve, None, turn, 0)
            dve.wait_ge(sem("acc_done"), 8 * N_EXPERTS + DN * l)

        N_ST = N_PAIRS // P
        xn_tok = part(0, 3, D_MODEL)
        pick, pick_g = part(3072, 3, N_PAIRS), part(4992, 3, N_PAIRS)
        y_s = part(0, KC, N_PAIRS + CAP)
        x_s = part(7000, KC, N_PAIRS + CAP)
        y_slot = part(7000, N_ST, D_MODEL)
        low_g = part(12700, 2, 3, N_PAIRS // 2)
        put = part(12700, N_ST, NT)
        hid_c = part(14300, 2, FC, CAP)
        sil_c = part(14880, 2, CAP)
        x_in = part(15030, 2, KC, CAP)
        HALF = N_PAIRS // 2
        TILES = ((0, P), (1, P), (2, NS))

        def few_pe(pe, l):
            U, E = UP * l, N_EXPERTS * l

            def gate_up(e, par, half, f):
                if f == 0:
                    for q in range(2):
                        slot_loaded(pe, 3 * par + q, slots_before(l, 3 * par + q) + half + 1)
                    pe.wait_ge(sem("x_in_set"), e + 1 + E)
                wait_pos(pe, "hid_done", 4 * e + f - 1 + U)
                b = bank[1 + f % 2]
                for q in range(2):
                    for k in range(KC):
                        mm = pe.matmul(b[:, CAP * q:CAP * q + CAP], slot_k[3 * par + q][:, k, P * f:P * f + P], x_in[:, par, k, :],
                                       start=(k == 0), stop=(k == KC - 1))
                mm.then_inc(sem("gu_ready"), 1)

            def down(e, par, half):
                slot_loaded(pe, 3 * par + 2, slots_before(l, 3 * par + 2) + half + 1)
                pe.wait_ge(sem("hid_done"), 4 * e + 4 + U)
                wait_pos(pe, "y_set", e + E)
                for c in range(KC):
                    for f in range(FC):
                        mm = pe.matmul(bank[5 + c // 4][:, CAP * (c % 4):CAP * (c % 4) + CAP], slot_f[3 * par + 2][:, f, P * c:P * c + P],
                                       hid_c[:, par, f, :], start=(f == 0), stop=(f == FC - 1))
                    mm.then_inc(sem("down_done"), 1)

            def turn(e, par, half, first=False, last=False):
                if not last:
                    gate_up(e, par, half, 0)
                    gate_up(e, par, half, 1)
                if not first:
                    down(e - 1, 1 - par, half if par else half - 1)
                if not last:
                    gate_up(e, par, half, 2)
                    gate_up(e, par, half, 3)

            pe.wait_ge(sem("moved_taken"), MOVES * l + GATHER)
            pe.wait_ge(sem("pick_set"), 4 * l + 1)
            for i in range(2 * KC):
                half, k = i // KC, i % KC
                if i == KC:
                    pe.wait_ge(sem("pick_set"), 4 * l + 2)
                to_bank(pe, l, GATHER + i)
                for t, n in TILES:
                    mm = pe.matmul(moved_in(GATHER + i)[:, 0:HALF], xn_tok[0:n, t, P * k:P * k + P],
                                   pick[0:n, t, HALF * half:HALF * half + HALF], start=(t == 0), stop=(t == 2))
                mm.then_inc(sem("moved"), 1)
            pe.wait_ge(sem("pick_set"), 4 * l + 4)
            for s in range(N_ST):
                to_bank(pe, l, PUT + s)
                for t, n in TILES:
                    mm = pe.transpose(moved_in(PUT + s)[:, P * t:P * t + n], pick_g[0:n, t, P * s:P * s + P], ident[0:n, 0:n])
                mm.then_inc(sem("moved"), 1)
            over_experts(pe, None, turn, 0)
            pe.wait_ge(sem("y_set"), N_EXPERTS + E)
            for i in range(2 * N_ST):
                to_bank(pe, l, SLOTWISE + i)
                for c in range(4):
                    mm = pe.transpose(moved_in(SLOTWISE + i)[:, P * c:P * c + P], y_s[:, 4 * (i % 2) + c, P * (i // 2):P * (i // 2) + P],
                                      ident[:, :])
                mm.then_inc(sem("moved"), 1)
            pe.wait_ge(sem("moved_taken"), MOVES * l + MOVES)
            for c in range(KC):
                if c >= 4:
                    pe.wait_ge(sem("acc_done"), DN * l + DN - KC + c - 3)
                for s in range(N_ST):
                    mm = pe.matmul(bank[[0, 7, 1, 2][c % 4]][:, 0:NT], y_slot[:, s, P * c:P * c + P], put[:, s, :],
                                   start=(s == 0), stop=(s == N_ST - 1))
                mm.then_inc(sem("put_back"), 1)
            pe.sem_inc(sem("gate_turned"), 1)

        def few_act(act, l):
            U = UP * l

            def take(i, dst, src):
                act.wait_ge(sem("moved"), MOVES * l + i + 1)
                act.copy(dst, src).then_inc(sem("moved_taken"), 1)

            def turn(e, par, half, first=False, last=False):
                if not last:
                    for f in range(FC):
                        act.wait_ge(sem("gu_ready"), 4 * e + f + 1 + U)
                        wait_pos(act, "hid_done", 4 * e + f - 1 + U)
                        act.activation(sil_c[:, f % 2, :], bank[1 + f % 2][:, 0:CAP], ACT.Silu).then_inc(sem("sil_done"), 1)

            for i in range(2 * KC):
                take(GATHER + i, x_s[:, i % KC, HALF * (i // KC):HALF * (i // KC) + HALF], moved_in(GATHER + i)[:, 0:HALF])
            for s in range(N_ST):
                take(PUT + s, put[:, s, :], moved_in(PUT + s)[:, 0:NT])
            over_experts(act, None, turn, 0)
            for i in range(2 * N_ST):
                take(SLOTWISE + i, y_slot[:, i // 2, 512 * (i % 2):512 * (i % 2) + 512], moved_in(SLOTWISE + i)[:, :])
            act.sem_inc(sem("gate_row"), 1)
            act.sem_inc(sem("gate_out"), 16)
            act.sem_inc(sem("gates_loaded"), 16)

        def few_dve(dve, own, l):
            U, E = UP * l, N_EXPERTS * l
            hi, lo = [[r1[0], r1[1]], [r1[2], r1[3]]]
            g_hi, g_lo = r1[4:6]

            def step(ins):
                own(ins)
                own.settle()

            def first_slot(e):
                return dve.value_load(route_i[0:1, bass.ds(e + 1, 1)], min_val=0, max_val=N_PAIRS)

            def set_x(e, par):
                dve.tensor_scalar(x_in[:, par], x_s[:, :, bass.ds(first_slot(e), CAP)], 1.0, None, ALU.mult)\
                    .then_inc(sem("x_in_set"), 1)

            def hidden(e, par, f):
                dve.wait_ge(sem("sil_done"), 4 * e + f + 1 + U)
                wait_pos(dve, "down_done", 8 * e - 8 + DN * l)
                dve.tensor_tensor(hid_c[:, par, f, :], sil_c[:, f % 2, :], bank[1 + f % 2][:, CAP:2 * CAP], ALU.mult)\
                    .then_inc(sem("hid_done"), 1)

            def take_y(e):
                at = first_slot(e)
                dve.wait_ge(sem("down_done"), 8 * e + 8 + DN * l)
                for h in range(2):
                    ins = dve.tensor_scalar(y_s[:, 4 * h:4 * h + 4, bass.ds(at, CAP)],
                                            bank[5 + h][:, 0:4 * CAP].rearrange("p (k c) -> p k c", k=4), 1.0, None, ALU.mult)
                ins.then_inc(sem("y_set"), 1)

            def turn(e, par, half, first=False, last=False, ahead=True):
                if not last:
                    hidden(e, par, 0)
                    hidden(e, par, 1)
                    if ahead:
                        set_x(e + 1, 1 - par)
                if not first:
                    take_y(e - 1)
                if not last:
                    hidden(e, par, 2)
                    hidden(e, par, 3)

            own(dve.tensor_reduce(hi[0], place, AX_X, ALU.max))
            step(dve.tensor_reduce(lo[0], place, AX_X, ALU.add))
            own(dve.memset(x_s[:, :, N_PAIRS:N_PAIRS + CAP], 0.0))
            own(dve.tensor_scalar(hi[1], hi[0], -float(HALF), None, ALU.add))
            step(dve.scalar_tensor_tensor(out=lo[0], in0=lo[0], scalar=float(N_EXPERTS - 2), in1=hi[0], op0=ALU.add, op1=ALU.subtract))
            step(dve.tensor_scalar(lo[1], lo[0], -float(HALF), None, ALU.add))
            halves = [(t, n, h, slice(HALF * h, HALF * h + HALF)) for h in range(2) for t, n in TILES]
            for t, n, h, r in halves:
                own(dve.tensor_scalar(pick[0:n, t, r], number[0:n, :], hi[h][0:n, t, :], None, ALU.is_equal))
            own.settle()
            for t, n, h, r in halves:
                ins = dve.scalar_tensor_tensor(out=pick[0:n, t, r], in0=number[0:n, :], scalar=lo[h][0:n, t, :], in1=pick[0:n, t, r],
                                               op0=ALU.is_equal, op1=ALU.add)
                if t < 2:
                    own(ins)
                else:
                    own.step_to(ins, sem("pick_set"), 4 * l + h + 1)
            for at, g in ((hi[0], g_hi), (lo[0], g_lo)):
                step(dve.tensor_tensor(r16, place, at.to_broadcast([P, 3, 16]), ALU.is_equal))
                step(dve.tensor_tensor(r16, r16, gate_tok, ALU.mult))
                step(dve.tensor_reduce(g, r16, AX_X, ALU.add))
            for t, n, h, r in halves:
                own(dve.tensor_scalar(pick_g[0:n, t, r], number[0:n, :], hi[h][0:n, t, :], g_hi[0:n, t, :], ALU.is_equal, ALU.mult))
                own(dve.tensor_scalar(low_g[0:n, h, t, :], number[0:n, :], lo[h][0:n, t, :], g_lo[0:n, t, :], ALU.is_equal, ALU.mult))
            own.settle()
            for t, n, h, r in halves:
                ins = dve.tensor_tensor(pick_g[0:n, t, r], pick_g[0:n, t, r], low_g[0:n, h, t, :], ALU.add)
                if t < 2:
                    own(ins)
                else:
                    own.step_to(ins, sem("pick_set"), 4 * l + 3 + h)
            dve.wait_ge(sem("moved_taken"), MOVES * l + PUT)
            set_x(0, 0)
            dve.wait_ge(sem("moved"), MOVES * l + SLOTWISE)
            turn(0, 0, 0, first=True)
            turn(1, 1, 0)
            with dve.Fori(1, N_EXPERTS // 2 - 1) as i:
                turn(2 * i, 0, i)
                turn(2 * i + 1, 1, i)
            turn(N_EXPERTS - 2, 0, N_EXPERTS // 2 - 1)
            turn(N_EXPERTS - 1, 1, N_EXPERTS // 2 - 1, ahead=False)
            turn(N_EXPERTS, 0, N_EXPERTS // 2, last=True, ahead=False)
            dve.sem_inc(sem("acc_done"), DN - KC)
            for c in range(KC):
                dve.wait_ge(sem("put_back"), KC * l + c + 1)
                dve.tensor_tensor(hT[:, c, :], hT[:, c, :], bank[[0, 7, 1, 2][c % 4]][:, 0:NT], ALU.add).then_inc(sem("acc_done"), 1)
            dve.wait_ge(sem("acc_done"), DN * l + DN)
            dve.sem_inc(sem("gu_done"), UP)

        def moe_pe(pe, l):
            route_pe(pe, l)
            pe.wait_ge(sem("route_step"), 4 * l + 4)
            n = pe.value_load(route_i[0:1, 0:1], min_val=0, max_val=NT)
            with pe.If(n <= CAP):
                few_pe(pe, l)
            with pe.Else():
                gate_rows_pe(pe, l)
                experts_pe(pe, l)
                pe.sem_inc(sem("moved"), MOVES - GATHER)
                pe.sem_inc(sem("put_back"), KC)

        def moe_act(act, own, l):
            route_act(act, own, l)
            act.wait_ge(sem("route_step"), 4 * l + 4)
            n = act.value_load(route_i[0:1, 0:1], min_val=0, max_val=NT)
            with act.If(n <= CAP):
                few_act(act, l)
            with act.Else():
                gate_rows_act(act, l)
                experts_act(act, l)
                act.sem_inc(sem("moved_taken"), MOVES - GATHER)

        def moe_dve(dve, own, l):
            route_dve(dve, own, l)
            n = dve.value_load(route_i[0:1, 0:1], min_val=0, max_val=NT)
            with dve.If(n <= CAP):
                before = own.n
                few_dve(dve, own, l)
                few_steps = own.n - before
            with dve.Else():
                experts_dve(dve, l)
                dve.sem_inc(sem("dve_steps"), few_steps)
                dve.sem_inc(sem("pick_set"), 4)
                dve.sem_inc(sem("x_in_set"), N_EXPERTS)
                dve.sem_inc(sem("y_set"), N_EXPERTS)

        def expert_piece(sp, l, e, par, q):
            w = d[["w_expert_gate", "w_expert_up", "w_expert_down"][q]][l][bass.ds(e, 1)].rearrange("a k n -> (a k) n")
            load_slot(sp, 3 * par + q, w)

        def experts_sp(sp, l):
            with sp.Fori(1, N_EXPERTS // 2) as i:
                for par in range(2):
                    e = 2 * i + par
                    sp.wait_ge(sem("gu_ready"), 4 * e - 4 + UP * l)
                    expert_piece(sp, l, e, par, 0)
                    expert_piece(sp, l, e, par, 1)
                    sp.wait_ge(sem("down_done"), 8 * e - 8 + DN * l)
                    expert_piece(sp, l, e, par, 2)

        y_tok = part(0, 3, D_MODEL)

        def finish_pe(pe, ready):
            ready(pe)
            for t, n in ((0, P), (1, P), (2, NS)):
                for half in range(2):
                    b = bank[2 * t + half]
                    for c in range(4):
                        mm = pe.transpose(b[0:n, P * c:P * c + P], hT[:, 4 * half + c, P * t:P * t + n], ident[:, :])
                    mm.then_inc(sem("y_turned"), 1)

        def finish_act(act, own):
            for t, n in ((0, P), (1, P), (2, NS)):
                for half in range(2):
                    act.wait_ge(sem("y_turned"), 2 * t + half + 1)
                    own(act.copy(y_tok[0:n, t, 512 * half:512 * half + 512], bank[2 * t + half][0:n, :]))
                own.settle()
                dst = d["y_prompt"][0][P * t:P * t + P, :] if t < 2 else d["y_sample"].rearrange("b t n -> (b t) n")
                act.dma_start(dst, y_tok[0:n, t, :]).then_inc(sem("y_stored"), 16)
            act.wait_ge(sem("y_stored"), 48)

        half1, half3 = ring[:, 1, SLOT // 2:], ring[:, 3, SLOT // 2:]
        slots45 = ring[:, 4:6, :].rearrange("p a b -> p (a b)")
        RAW = 3 + SEQ + DEC_BATCH * (3 + DEC_SEQ)
        raw = part(0, 4, RAW)
        conv = part(1400, 2, NT)
        xc = part(2040, 2, 4, NT)
        xdt, xtl = part(4600, 3, 256), part(5368, 3, 256)
        b_tok = part(6136, 3, D_STATE)
        cb = part(7544, TRI)
        cs_rows = part(7992, 2, 4, NT)
        wts = part(10552, 4, TRI)
        y_sb, y_sq, y_rs = part(12344, 2, NT), part(12984, 2, NT), part(13624, NT)
        tails = part(14000, 32, 27)
        p_st = part(14864, 2, 256)
        cin_tok = part(9800, 4096)
        dt_v, dt_e, dt_w, dt_l, dt_m, dt, cs, tail, dtl = (part(10552 + 330 * i, NT) for i in range(9))
        b_diag = part(0, 8, D_STATE, of=half1)
        cin = half1[:, 1024:1792].rearrange("p (c r) -> p c r", c=32)
        stT = half3[:, 0:2048].rearrange("p (c b n) -> p c b n", c=2, b=8)
        causal = part(15504, TRI)
        y_cat = part(0, 16, NT, of=slots45)
        stb = [[part(5120, 8, D_STATE, of=slots45), part(6144, 8, D_STATE, of=slots45)],
               [part(7168, 8, D_STATE, of=slots45), part(0, 8, D_STATE, of=cat_flat)]]
        z_s = part(1024, 2, 2, NT, of=cat_flat)
        e_rows = part(2304, 16, NS, of=cat_flat)
        e_last = part(3328, 16, 8, of=cat_flat)
        tok3 = part(3456, 3, 96, of=cat_flat)
        y_in = part(3744, NS, of=cat_flat)
        w_dt = small[:, :].rearrange("p (k n) -> p k n", k=KC)
        cos_flat, sin_flat = (x[:, :, :].rearrange("p a b -> p (a b)") for x in (cos, sin))
        cw = part(0, 32, CONV_W, of=cos_flat)
        cbias = part(128, 32, of=cos_flat)
        skip, gain = part(0, 16, of=sin_flat), part(16, 16, of=sin_flat)
        dtb, alog, aexp = (sin_flat[0:32, 32 + i:33 + i] for i in range(3))
        H = slice(0, SSM_HEADS)

        def odd_setup_pool(pool):
            pool.wait_ge(sem("sm_ready"), 1)
            for dst, src in ((w_dt, d["w_in_odd"][0][:, 6144:6176].rearrange("(k p) n -> p k n", p=P)), (cw, d["conv_w"]),
                             (cbias, d["conv_b"]), (gain, d["ssd_norm"]), (dtb, d["dt_bias"]), (alog, d["a_log"])):
                pool.dma_start(dst, src).then_inc(sem("odd_consts"), 16)
            for g in range(2):
                pool.dma_start(skip[HD * g:HD * g + HD], d["d_skip"][g:g + 1].to_broadcast([HD, 16])).then_inc(sem("odd_consts"), 16)
            pool.wait_ge(sem("acc_done"), DN)
            pool.dma_start(cin_tok[0:24], d["state_conv"][0].rearrange("b r c -> (b r) c")).then_inc(sem("cin_loaded"), 16)
            pool.wait_ge(sem("xn_ready"), 3)
            pool.dma_start(causal, d["c_causal"]).then_inc(sem("odd_consts"), 16)

        ODD_CONSTS = 16 * 8

        def odd_weights(sp, g, par):
            for s, cols in ((2 * par, ((0, 256, 256), (2048, 256, 256))), (2 * par + 1, ((4096, 128, 128), (5120, 128, 128)))):
                width = cols[0][2] * 2
                dst = ring[:, s, 0:KC * width].rearrange("p (k n) -> p k n", k=KC)
                for i, (base, stride, n) in enumerate(cols):
                    src = d["w_in_odd"][0][:, bass.ds(base + stride * g, n)].rearrange("(k p) n -> p k n", p=P)
                    sp.dma_start(dst[:, :, n * i:n * i + n], src).then_inc(sem(f"slot{s}_loaded"), 16)

        def odd_sp(sp):
            def group_loads(g, par):
                for c in range(2):
                    src = d["state_ssm"][0].rearrange("b (c h) p n -> c (h p) b n", h=2)[bass.ds(2 * g + c, 1)]
                    sp.dma_start(stb[par][c], src.rearrange("a q b n -> (a q) b n")).then_inc(sem(f"s{par}{c}_loaded"), 16)
                if isinstance(g, int) and g == 0:
                    sp.wait_ge(sem("rows_out"), 48)
                wait_pos(sp, "seg_done", g - 1)
                src = cs_dram[bass.ds(4 * g, 4)].rearrange("h n -> (h n)").rearrange("(a m) -> a m", a=1)
                sp.dma_start(cs_rows[:, par], src.to_broadcast([P, 4 * NT]).rearrange("p (h n) -> p h n", h=4))\
                    .then_inc(sem(f"cs{par}_loaded"), 16)

            def group_stores(g, par):
                for c in range(2):
                    sp.wait_ge(sem("st_new"), 2 * g + c + 1)
                    dst = d["ssm_sample"][0].rearrange("b (c h) p n -> c (h p) b n", h=2)[bass.ds(2 * g + c, 1)]
                    sp.dma_start(dst.rearrange("a q b n -> (a q) b n"), stb[par][c]).then_inc(sem(f"s{par}{c}_stored"), 16)
                sp.wait_ge(sem("ps_taken"), g + 1)
                dst = d["ssm_prompt"][0, 0].rearrange("(g c h) p n -> g (h p) c n", h=2, c=2)[bass.ds(g, 1)]
                sp.dma_start(dst.rearrange("a q c n -> (a q) c n"), p_st[:, par].rearrange("p (c n) -> p c n", c=2))\
                    .then_inc(sem(f"ps{par}_stored"), 16)

            def turn(g, par, first=False, last=False):
                early = isinstance(g, int) and g < 2
                if not last:
                    if not early:
                        sp.wait_ge(sem("op_done"), 6 * g - 6)
                        odd_weights(sp, g, par)
                if not early:
                    group_stores(g - 2, par)
                if not last:
                    if not early:
                        for c in range(2):
                            sp.wait_ge(sem(f"s{par}{c}_stored"), 8 * (g - par))
                    group_loads(g, par)
                else:
                    group_stores(7, 1)

            for par, e in ((0, 14), (1, 15)):
                sp.wait_ge(sem("gu_ready"), 4 * e + 4)
                if par == 0:
                    sp.wait_ge(sem("down_done"), 8 * e + 8)
                odd_weights(sp, par, par)
            sp.wait_ge(sem("down_done"), 8 * N_EXPERTS)
            over_samples(sp, None, turn, 0)

        def odd_out_sp(sp):
            for s in range(4):
                if s == 0:
                    sp.wait_ge(sem("op_done"), 48)
                if s == 1:
                    sp.wait_ge(sem("ss_done"), 16)
                if s == 3:
                    sp.wait_ge(sem("yi_done"), 8)
                load_slot(sp, s, d["w_out_odd"][0][512 * s:512 * s + 512, :])

        def odd_setup_pe(pe):
            pe.wait_ge(sem("cin_loaded"), 16)
            pe.wait_ge(sem("acc_done"), 8 * N_EXPERTS)
            for c in range(32):
                mm = pe.transpose(bank[3 + c // 16][:, 24 * (c % 16):24 * (c % 16) + 24], cin_tok[0:24, P * c:P * c + P],
                                  ident[0:24, 0:24])
            mm.then_inc(sem("setup_turned"), 1)
            pe.wait_ge(sem("xn_ready"), 3)
            pe.wait_ge(sem("odd_consts"), ODD_CONSTS + 16)
            for k in range(KC):
                mm = pe.matmul(bank[5][H, 0:NT], w_dt[:, k, :], xnT[:, k, 0:NT], start=(k == 0), stop=(k == KC - 1))
            mm.then_inc(sem("setup_turned"), 1)

        def odd_turn_pe(pe):
            pe.wait_ge(sem("dt_vector"), 4)
            pe.wait_ge(sem("dt_scalar"), 1)
            for i, x in enumerate((cs, dt, dtl)):
                for t, n in ((0, P), (1, P), (2, NS)):
                    mm = pe.transpose(bank[4][0:n, 96 * t + 32 * i:96 * t + 32 * i + 32], x[H, P * t:P * t + n], ident[H, H])
            mm.then_inc(sem("setup_turned"), 1)

        def odd_setup_act(act, own):
            act.wait_ge(sem("setup_turned"), 1)
            act.wait_ge(sem("gu_ready"), 60)
            for i in range(2):
                own(act.copy(cin[:, 16 * i:16 * i + 16, :], bank[3 + i][:, 0:384].rearrange("p (c r) -> p c r", c=16)))
            own.settle()
            act.sem_inc(sem("dt_scalar"), 1)
            act.wait_ge(sem("dt_vector"), 1)
            own(act.activation(dt_e[H], dt_v[H], ACT.Abs))
            own(act.activation(aexp, alog, ACT.Exp))
            own.settle()
            own.step_to(act.activation(dt_e[H], dt_e[H], ACT.Exp, scale=-1.0), sem("dt_scalar"), 2)
            act.wait_ge(sem("dt_vector"), 2)
            own.step_to(act.activation(dt_l[H], dt_w[H], ACT.Ln), sem("dt_scalar"), 3)
            act.wait_ge(sem("dt_vector"), 3)
            own(act.activation(tail[H, 0:SEQ], cs[H, 0:SEQ], ACT.Exp, bias=cs[H, SEQ - 1:SEQ], scale=-1.0))
            own(act.activation(tail[H, SEQ:NT], tail[H, SEQ:NT], ACT.Exp))
            own.step_to(act.activation(dt_e[H, 0:NS], cs[H, SEQ:NT], ACT.Exp), sem("dt_scalar"), 4)
            own.settle()
            act.wait_ge(sem("dt_vector"), 5)
            act.dma_start(cs_dram, cs[H]).then_inc(sem("rows_out"), 16)
            act.dma_start(e_dram, dt_e[H, 0:NS]).then_inc(sem("rows_out"), 16)
            act.dma_start(el_dram, dt_w[H, 0:8]).then_inc(sem("rows_out"), 16)
            act.wait_ge(sem("setup_turned"), 3)
            own(act.copy(tok3[:, 0:2, :], bank[4][:, 0:192].rearrange("p (t n) -> p t n", t=2)))
            own.step_to(act.copy(tok3[R, 2, :], bank[4][R, 192:288]), sem("dt_scalar"), 5)
            own.settle()
            act.wait_ge(sem("rows_out"), 48)
            for g in range(2):
                r = slice(HD * g, HD * g + HD)
                for dst, src, n in ((e_rows, e_dram, NS), (e_last, el_dram, 8)):
                    act.dma_start(dst[r], src.rearrange("(c h) n -> h c n", h=2)[g].unsqueeze(0).to_broadcast([HD, 16, n]))\
                        .then_inc(sem("e_loaded"), 16)

        def odd_setup_dve(dve, own):
            def step(ins):
                own(ins)
                own.settle()

            dve.wait_ge(sem("setup_turned"), 1)
            dve.wait_ge(sem("odd_consts"), ODD_CONSTS + 16)
            own(dve.memset(raw[:, :, 0:3], 0.0))
            dve.wait_ge(sem("setup_turned"), 2)
            own.step_to(dve.tensor_scalar(dt_v[H], bank[5][H, 0:NT], dtb, None, ALU.add), sem("dt_vector"), 1)
            own.settle()
            dve.wait_ge(sem("dt_scalar"), 2)
            own.step_to(dve.tensor_scalar(dt_w[H], dt_e[H], 1.0, None, ALU.add), sem("dt_vector"), 2)
            own.settle()
            step(dve.tensor_scalar(dt_m[H], dt_w[H], 1.0, None, ALU.is_equal))
            step(dve.scalar_tensor_tensor(out=dt[H], in0=dt_w[H], scalar=-1.0, in1=dt_m[H], op0=ALU.add, op1=ALU.add))
            step(dve.reciprocal(dt[H], dt[H]))
            step(dve.tensor_tensor(dt[H], dt[H], dt_e[H], ALU.mult))
            dve.wait_ge(sem("dt_scalar"), 3)
            step(dve.tensor_tensor(dt_l[H], dt_l[H], dt_m[H], ALU.add))
            step(dve.tensor_tensor(dt[H], dt[H], dt_l[H], ALU.mult))
            step(dve.scalar_tensor_tensor(out=dt[H], in0=dt_v[H], scalar=0.0, in1=dt[H], op0=ALU.max, op1=ALU.add))
            step(dve.tensor_scalar(dt_l[H], dt[H], aexp, -1.0, ALU.mult, ALU.mult))
            step(dve.memset(dt_v[H], 1.0))
            step(dve.memset(dt_v[H, SEQ:NT].rearrange("p (b t) -> p b t", t=DEC_SEQ)[:, :, 0:1], 0.0))
            step(dve.tensor_tensor_scan(cs[H], dt_v[H], dt_l[H], 0.0, ALU.mult, ALU.add))
            smp = lambda x: x.rearrange("p (b t) -> p b t", t=DEC_SEQ)
            css = smp(cs[H, SEQ:NT])
            own.step_to(dve.tensor_tensor(smp(tail[H, SEQ:NT]), css[:, :, 7:8].to_broadcast([SSM_HEADS, 8, 8]), css, ALU.subtract),
                       sem("dt_vector"), 3)
            dve.wait_ge(sem("dt_scalar"), 4)
            own.step_to(dve.tensor_tensor(dtl[H], dt[H], tail[H], ALU.mult), sem("dt_vector"), 4)
            own.step_to(dve.tensor_copy(dt_w[H, 0:8].unsqueeze(2), smp(dt_e[H, 0:NS])[:, :, 7:8]), sem("dt_vector"), 5)
            own.settle()
            dve.wait_ge(sem("dt_scalar"), 5)
            dve.wait_ge(sem("e_loaded"), 64)

        def odd_groups_pe(pe):
            def proj(g, par, c):
                if c == 0:
                    pe.wait_ge(sem(f"slot{2 * par}_loaded"), 192 + 16 * (g - par))
                if c == 4:
                    pe.wait_ge(sem(f"slot{2 * par + 1}_loaded"), 192 + 16 * (g - par))
                wait_pos(pe, "op_taken", 6 * g + c - 2)
                w = slot_k[2 * par] if c < 4 else ring[:, 2 * par + 1, 0:2048].rearrange("p (k n) -> p k n", k=KC)
                for k in range(KC):
                    mm = pe.matmul(bank[c % 3][:, 0:NT], w[:, k, P * (c % 4):P * (c % 4) + P], xnT[:, k, 0:NT],
                                   start=(k == 0), stop=(k == KC - 1))
                mm.then_inc(sem("op_done"), 1)

            def turn_state(s, par, c):
                pe.wait_ge(sem(f"s{par}{c}_loaded"), 16 + 8 * (s - par))
                for half in range(2):
                    if c == 0:
                        wait_pos(pe, "st_new", 2 * s)
                    else:
                        pe.wait_ge(sem("stT_taken"), 4 * s + half + 1)
                    for b in range(4):
                        mm = pe.transpose(bank[3 + half][:, P * b:P * b + P], stb[par][c][:, 4 * half + b, :], ident[:, :])
                    mm.then_inc(sem("st_turned"), 1)

            def turn_x(s, par, tiles):
                for t, n in tiles:
                    if t < 2:
                        pe.wait_ge(sem("xc_done"), 4 * s + 4)
                        pe.wait_ge(sem("stT_taken"), 4 * s + 3 + t)
                    for i in range(3):
                        mm = pe.transpose(bank[3 + t % 2][0:n, P * i:P * i + P], xc[:, par, i, P * t:P * t + n], ident[:, :])
                    mm.then_inc(sem("x_turned2"), 1)

            def c_by_b(s, par):
                wait_pos(pe, "y_root", s)
                pe.wait_ge(sem("x_tok_set"), 3 * s + 1)
                pe.wait_ge(sem("b_tok_set"), 3 * s + 1)
                B, C, b = xc[:, par, 2, :], xc[:, par, 3, :], bank[5]
                pe.matmul(b[:, 0:2 * P], B[:, 0:P], C[:, 0:2 * P], start=True, stop=True)
                pe.matmul(b[:, 2 * P:3 * P], B[:, P:2 * P], C[:, P:2 * P], start=True, stop=True)
                pe.matmul(b[R, 3 * P:TRI], B[:, 2 * P:NT], C[:, 2 * P:NT], start=True, stop=True).then_inc(sem("cb_done"), 1)

            def y_start(s, par):
                wait_pos(pe, "y_taken", 2 * s)
                pe.wait_ge(sem("stT_taken"), 4 * s + 4)
                for c in range(2):
                    for n in range(DEC_BATCH):
                        mm = pe.matmul(bank[6 + c][:, NT + 8 * n:NT + 8 * n + 8], stT[:, c, n, :],
                                       xc[:, par, 3, SEQ + 8 * n:SEQ + 8 * n + 8], start=True, stop=True)
                mm.then_inc(sem("yi_done"), 1)

            def new_states(s, c):
                pe.wait_ge(sem("x_tok_set"), 3 * s + 3)
                if c == 0:
                    pe.wait_ge(sem("b_tok_set"), 3 * s + 3)
                else:
                    pe.wait_ge(sem("st_new"), 2 * s + 1)
                for half in range(2):
                    mm = pe.matmul(bank[3 + half][:, :], xtl[R, 2, P * c:P * c + P], b_diag[R, 4 * half:4 * half + 4, :],
                                   start=True, stop=True)
                mm.then_inc(sem("ss_done"), 1)

            def prompt_state(s):
                pe.wait_ge(sem("cb_taken"), s + 1)
                for c in range(2):
                    for t in range(2):
                        mm = pe.matmul(bank[5][:, P * c:P * c + P], xtl[:, t, P * c:P * c + P], b_tok[:, t, :],
                                       start=(t == 0), stop=(t == 1))
                mm.then_inc(sem("ps_done"), 1)

            def y_within(s):
                pe.wait_ge(sem("wts_set"), s + 1)
                for h in range(4):
                    o, x, w = bank[6 + h // 2][HD * (h % 2):HD * (h % 2) + HD, :], slice(HD * h, HD * h + HD), wts[:, h, :]
                    pe.matmul(o[:, 0:2 * P], xdt[:, 0, x], w[:, 0:2 * P], start=True, stop=False)
                    pe.matmul(o[:, P:2 * P], xdt[:, 1, x], w[:, 2 * P:3 * P], start=False, stop=True)
                    mm = pe.matmul(o[:, 2 * P:NT], xdt[R, 2, x], w[R, 3 * P:TRI], start=True, stop=True)
                    if h % 2 == 1:
                        mm.then_inc(sem("y_done"), 1)

            def square_sums(s):
                pe.wait_ge(sem("ps_taken"), s + 1)
                pe.wait_ge(sem("y_sq_set"), 2 * s + 2)
                for c in range(2):
                    mm = pe.matmul(bank[5][:, 0:NT], ones[:, :], y_sq[:, c, :], start=(c == 0), stop=(c == 1))
                mm.then_inc(sem("y_sum"), 1)

            def turn(g, par, first=False, last=False):
                s, sp_ = g - 1, 1 - par
                if not last:
                    proj(g, par, 0)
                if not first:
                    turn_state(s, sp_, 0)
                    turn_state(s, sp_, 1)
                if not last:
                    proj(g, par, 1)
                if not first:
                    turn_x(s, sp_, ((0, P), (1, P)))
                    c_by_b(s, sp_)
                    turn_x(s, sp_, ((2, NS),))
                if not last:
                    proj(g, par, 2)
                if not first:
                    y_start(s, sp_)
                    new_states(s, 0)
                if not last:
                    proj(g, par, 3)
                if not first:
                    prompt_state(s)
                    y_within(s)
                if not last:
                    proj(g, par, 4)
                if not first:
                    new_states(s, 1)
                if not last:
                    proj(g, par, 5)
                if not first:
                    square_sums(s)

            pe.wait_ge(sem("dt_scalar"), 5)
            over_samples(pe, None, turn, 0)

        def odd_groups_act(act, own):
            def take(g, par, c):
                act.wait_ge(sem("op_done"), 6 * g + c + 1)
                b = bank[c % 3]
                if c < 2:
                    wait_pos(act, "yz_set", 2 * g - 2)
                    act.activation(z_s[:, par, c, :], b[:, 0:NT], ACT.Silu).then_inc(sem("op_taken"), 1)
                else:
                    wait_pos(act, "conv_done", 4 * g + c - 5)
                    own(act.copy(raw[:, c - 2, 3:3 + SEQ], b[:, 0:SEQ]))
                    act.copy(raw[:, c - 2, 3 + SEQ:RAW].rearrange("p (b t) -> p b t", b=8)[:, :, 3:11],
                             b[:, SEQ:NT].rearrange("p (b t) -> p b t", b=8)).then_inc(sem("op_taken"), 1)

            def state(s, f):
                act.wait_ge(sem("st_turned"), 4 * s + f + 1)
                if f == 0:
                    wait_pos(act, "yi_done", s)
                act.copy(stT[:, f // 2, 4 * (f % 2):4 * (f % 2) + 4, :], bank[3 + f % 2][:, :].rearrange("p (b n) -> p b n", b=4))\
                    .then_inc(sem("stT_taken"), 1)

            def exps(s):
                act.wait_ge(sem("seg_done"), s + 1)
                own(act.activation(wts[:, :, 0:3 * P], wts[:, :, 0:3 * P], ACT.Exp))
                act.activation(wts[R, :, 3 * P:TRI], wts[R, :, 3 * P:TRI], ACT.Exp).then_inc(sem("wts_exp"), 1)

            def b_to_tok(s, t, n):
                act.wait_ge(sem("x_tok_set"), 3 * s + t + 1)
                wait_pos(act, "ps_done", s)
                act.copy(b_tok[0:n, t, :], bank[3 + t % 2][0:n, 2 * P:3 * P]).then_inc(sem("b_tok_set"), 1)

            def silu(g, par, c):
                act.wait_ge(sem("conv_done"), 4 * g + c + 1)
                act.activation(xc[:, par, c, :], conv[:, c % 2, :], ACT.Silu).then_inc(sem("xc_done"), 1)

            def prompt_state(s, par):
                act.wait_ge(sem("ps_done"), s + 1)
                wait_pos(act, f"ps{par}_stored", 8 * (s - par))
                act.copy(p_st[:, par, :], bank[5][:, 0:256]).then_inc(sem("ps_taken"), 1)

            def squares(s, c):
                act.wait_ge(sem("yz_set"), 2 * s + c + 1)
                if c == 0:
                    wait_pos(act, "y_sum", s)
                act.activation(y_sq[:, c, :], y_sb[:, c, :], ACT.Square).then_inc(sem("y_sq_set"), 1)

            def root(s):
                act.wait_ge(sem("y_sum"), s + 1)
                wait_pos(act, "y_normed", s)
                act.activation(y_rs, bank[5][:, 0:NT], ACT.Sqrt, bias=eps[:, :], scale=1.0 / 256).then_inc(sem("y_root"), 1)

            def turn(g, par, first=False, last=False):
                s, sp_ = g - 1, 1 - par
                if not last:
                    take(g, par, 0)
                if not first:
                    for f in range(4):
                        state(s, f)
                    exps(s)
                if not last:
                    take(g, par, 1)
                if not first:
                    for t, n in ((0, P), (1, P), (2, NS)):
                        b_to_tok(s, t, n)
                if not last:
                    take(g, par, 2)
                    take(g, par, 3)
                if not first:
                    prompt_state(s, sp_)
                if not last:
                    silu(g, par, 0)
                    silu(g, par, 1)
                    take(g, par, 4)
                if not first:
                    squares(s, 0)
                    squares(s, 1)
                if not last:
                    take(g, par, 5)
                    silu(g, par, 2)
                    silu(g, par, 3)
                if not first:
                    root(s)

            over_samples(act, own, turn, 2 * 5)

        def odd_groups_dve(dve, own):
            def segments(s, par):
                dve.wait_ge(sem(f"cs{par}_loaded"), 16 + 8 * (s - par))
                wait_pos(dve, "y_done", 2 * s)
                for h in range(4):
                    for rws, cols, q, t in ((slice(0, P), slice(0, 2 * P), slice(0, 2 * P), 0),
                                            (slice(0, P), slice(2 * P, 3 * P), slice(P, 2 * P), 1),
                                            (R, slice(3 * P, TRI), slice(2 * P, NT), 2)):
                        ins = dve.tensor_scalar(wts[rws, h, cols], cs_rows[rws, par, h, q],
                                                tok3[rws, t, bass.ds(4 * s + h, 1)], 0.0, ALU.subtract, ALU.min)
                        if (h, t) != (3, 2):
                            own(ins)
                ins.then_inc(sem("seg_done"), 1)

            def x_to_tok(s, t, n):
                dve.wait_ge(sem("x_turned2"), 3 * s + t + 1)
                if t == 0:
                    wait_pos(dve, "ss_done", 2 * s)
                b = bank[3 + t % 2][0:n, :]
                x = b[:, 0:256].rearrange("p (h e) -> p h e", h=4)
                for dst, at in ((xdt, 32), (xtl, 64)):
                    ins = dve.tensor_tensor(dst[0:n, t, :].rearrange("p (h e) -> p h e", h=4), x,
                                            tok3[0:n, t, bass.ds(at + 4 * s, 4)].unsqueeze(2).to_broadcast([n, 4, HD]), ALU.mult)
                    if dst is xdt or t == 2:
                        own(ins)
                if t == 2:
                    ins = dve.tensor_tensor(b_diag[R], b[:, 256:384].unsqueeze(1).to_broadcast([NS, 8, D_STATE]),
                                            bmask[:, :].unsqueeze(2).to_broadcast([NS, 8, D_STATE]), ALU.mult)
                ins.then_inc(sem("x_tok_set"), 1)

            def weights(s):
                dve.wait_ge(sem("cb_done"), s + 1)
                (bp, bs), (mp, ms), (cp, cs_) = (causal_parts(x) for x in (bank[5], causal, cb))
                own(dve.tensor_tensor(cp, bp, mp, ALU.mult))
                own.step_to(dve.tensor_tensor(cs_, bs, ms, ALU.mult), sem("cb_taken"), s + 1)
                own.settle()
                dve.wait_ge(sem("wts_exp"), s + 1)
                own(dve.tensor_tensor(wts[:, :, 0:3 * P], wts[:, :, 0:3 * P], cp.unsqueeze(1).to_broadcast([P, 4, 3 * P]), ALU.mult))
                dve.tensor_tensor(wts[R, :, 3 * P:TRI], wts[R, :, 3 * P:TRI], cs_.unsqueeze(1).to_broadcast([NS, 4, NS]),
                                  ALU.mult).then_inc(sem("wts_set"), 1)

            def convolve(g, c):
                ch = (2 * g + c) if c < 2 else (8 * c + g)
                dve.wait_ge(sem("op_taken"), 6 * g + c + 3)
                r = raw[:, c, :]
                rs = r[:, 3 + SEQ:RAW].rearrange("p (b t) -> p b t", b=8)
                dyn = lambda x: x[:, bass.ds(ch, 1)]
                own(dve.tensor_scalar(rs[:, :, 0:3], dyn(cin).rearrange("p a (b t) -> p (a b) t", b=8), 1.0, None, ALU.mult))
                own(dve.tensor_scalar(dyn(tails)[:, :, 0:3].rearrange("p a t -> p (a t)"), r[:, SEQ:SEQ + 3], 1.0, None, ALU.mult))
                own(dve.tensor_scalar(dyn(tails)[:, :, 3:27].rearrange("p a (b t) -> p (a b) t", b=8), rs[:, :, 8:11], 1.0, None, ALU.mult))
                wait_pos(dve, "xc_done", 4 * g + c - 1)
                acc_p, acc_s = conv[:, c % 2, 0:SEQ], conv[:, c % 2, SEQ:NT].rearrange("p (b t) -> p b t", b=8)
                for k in range(CONV_W):
                    w = cw[:, bass.ds(ch, 1), k]
                    own.settle()
                    if k == 0:
                        own(dve.tensor_scalar(acc_p, r[:, 0:SEQ], w, cbias[:, bass.ds(ch, 1)], ALU.mult, ALU.add))
                        own(dve.tensor_scalar(acc_s, rs[:, :, 0:8], w, cbias[:, bass.ds(ch, 1)], ALU.mult, ALU.add))
                    else:
                        own(dve.scalar_tensor_tensor(out=acc_p, in0=r[:, k:k + SEQ], scalar=w, in1=acc_p, op0=ALU.mult, op1=ALU.add))
                        ins = dve.scalar_tensor_tensor(out=acc_s, in0=rs[:, :, k:k + 8], scalar=w, in1=acc_s, op0=ALU.mult, op1=ALU.add)
                        if k < CONV_W - 1:
                            own(ins)
                own.step_to(ins, sem("conv_done"), 4 * g + c + 1)

            def update(s, par, c):
                dve.wait_ge(sem("st_turned"), 4 * s + 4)
                x = stb[par][c]
                own(dve.tensor_tensor(x, x, e_last[:, bass.ds(2 * s + c, 1), :].rearrange("p a b -> p (a b)").unsqueeze(2)
                                      .to_broadcast([P, 8, D_STATE]), ALU.mult))
                dve.wait_ge(sem("ss_done"), 2 * s + c + 1)
                own.settle()
                for half in range(2):
                    xh = x[:, 4 * half:4 * half + 4, :].rearrange("p b n -> p (b n)")
                    ins = dve.tensor_tensor(xh, xh, bank[3 + half][:, :], ALU.add)
                    if half == 0:
                        own(ins)
                ins.then_inc(sem("st_new"), 1)

            def y_out(s, par, c):
                dve.wait_ge(sem("y_done"), 2 * s + c + 1)
                dve.wait_ge(sem("yi_done"), s + 1)
                b, y = bank[6 + c], y_sb[:, c, :]
                own(dve.tensor_tensor(y_in, b[:, NT:NT + NS], e_rows[:, bass.ds(2 * s + c, 1), :].rearrange("p a n -> p (a n)"), ALU.mult))
                own.step_to(dve.scalar_tensor_tensor(out=y, in0=xc[:, par, c, :], scalar=skip[:, bass.ds(2 * s + c, 1)],
                                                    in1=b[:, 0:NT], op0=ALU.mult, op1=ALU.add), sem("y_taken"), 2 * s + c + 1)
                own.settle()
                own(dve.tensor_tensor(y[:, SEQ:NT], y[:, SEQ:NT], y_in, ALU.add))
                own.settle()
                own.step_to(dve.tensor_tensor(y, y, z_s[:, par, c, :], ALU.mult), sem("yz_set"), 2 * s + c + 1)
                own.settle()

            def normalise(s):
                dve.wait_ge(sem("y_root"), s + 1)
                own(dve.reciprocal(y_rs, y_rs))
                own.settle()
                for c in range(2):
                    ins = dve.scalar_tensor_tensor(out=y_cat[:, bass.ds(2 * s + c, 1), :].rearrange("p a n -> p (a n)"),
                                                   in0=y_sb[:, c, :], scalar=gain[:, bass.ds(2 * s + c, 1)], in1=y_rs,
                                                   op0=ALU.mult, op1=ALU.mult)
                    if c == 0:
                        own(ins)
                ins.then_inc(sem("y_normed"), 1)

            def turn(g, par, first=False, last=False):
                s, sp_ = g - 1, 1 - par
                if not first:
                    segments(s, sp_)
                    for t, n in ((0, P), (1, P), (2, NS)):
                        x_to_tok(s, t, n)
                    weights(s)
                    update(s, sp_, 0)
                if not last:
                    convolve(g, 0)
                    convolve(g, 1)
                if not first:
                    y_out(s, sp_, 0)
                    y_out(s, sp_, 1)
                    update(s, sp_, 1)
                if not last:
                    convolve(g, 2)
                    convolve(g, 3)
                if not first:
                    normalise(s)

            over_samples(dve, own, turn, 2 * 67)

        tails_tok = part(0, 4096)

        def odd_out_pe(pe):
            pe.wait_ge(sem("y_normed"), GROUPS)
            pe.wait_ge(sem("conv_done"), 4 * GROUPS)
            for i in range(8):
                if i >= 4:
                    pe.wait_ge(sem("tails_taken"), i - 3)
                for c in range(4):
                    mm = pe.transpose(bank[4 + i % 4][0:27, P * c:P * c + P], tails[:, 4 * i + c, :], ident[:, :])
                mm.then_inc(sem("tails_turned"), 1)
            for s in range(4):
                slot_loaded(pe, s, 19)
            for c in range(KC):
                if c >= 4:
                    pe.wait_ge(sem("h_ready"), 2 * KC + c - 3)
                for k in range(16):
                    mm = pe.matmul(bank[c % 4][:, 0:NT], slot_f[k // 4][:, k % 4, P * c:P * c + P], y_cat[:, k, :],
                                   start=(k == 0), stop=(k == 15))
                mm.then_inc(sem("odd_out"), 1)

        def odd_out_act(act, own):
            for i in range(8):
                act.wait_ge(sem("tails_turned"), i + 1)
                own.step_to(act.copy(tails_tok[0:27, 512 * i:512 * i + 512], bank[4 + i % 4][0:27, :]), sem("tails_taken"), i + 1)
            own.settle()
            act.dma_start(d["conv_prompt"][0, 0], tails_tok[0:3]).then_inc(sem("tails_stored"), 16)
            act.dma_start(d["conv_sample"][0].rearrange("b r c -> (b r) c"), tails_tok[3:27]).then_inc(sem("tails_stored"), 16)

        def odd_out_dve(dve, own):
            for c in range(KC):
                dve.wait_ge(sem("odd_out"), c + 1)
                own.step_to(dve.tensor_tensor(hT[:, c, :], hT[:, c, :], bank[c % 4][:, 0:NT], ALU.add), sem("h_ready"), 2 * KC + c + 1)
            own.settle()

        @block.sync
        def _(sp):
            sp.dma_start(x_tok[:, 0:2, :], d["x_prompt"][0].rearrange("(t p) n -> p t n", p=P)).then_inc(sem("x_loaded"), 32)
            sp.dma_start(x_tok[0:NS, 2, :], d["x_sample"].rearrange("b t n -> (b t) n")).then_inc(sem("x_loaded"), 16)
            sp.wait_ge(sem("consts_loaded"), 16 * N_CONSTS)
            even_weights(sp)
            sp.wait_ge(sem("proj_done"), 21)
            expert_piece(sp, 0, 0, 0, 0)
            pages_sp(sp)
            sp.wait_ge(sem("sm_out"), 8)
            expert_piece(sp, 0, 0, 0, 1)
            expert_piece(sp, 0, 0, 0, 2)
            sp.wait_ge(sem("even_out"), 8)
            for q in range(3):
                expert_piece(sp, 0, 1, 1, q)
            experts_sp(sp, 0)
            odd_sp(sp)
            odd_out_sp(sp)
            sp.wait_ge(sem("odd_out"), KC)
            for e in range(2):
                for q in range(3):
                    expert_piece(sp, 1, e, e, q)
            experts_sp(sp, 1)
            for s in ("s00", "s01", "s10", "s11", "ps0", "ps1"):
                sp.wait_ge(sem(s + "_stored"), 64)
            sp.wait_ge(sem("tails_stored"), 32)

        @block.tensor
        def _(pe):
            transpose_x_pe(pe)
            norm_pe(pe, 0)
            even_proj_pe(pe)
            even_turn_pe(pe)
            retention_pe(pe)
            prompt_attn_pe(pe)
            sample_attn_pe(pe)
            even_out_pe(pe)
            norm_pe(pe, 1)
            moe_pe(pe, 0)
            norm_pe(pe, 2)
            odd_setup_pe(pe)
            odd_turn_pe(pe)
            odd_groups_pe(pe)
            odd_out_pe(pe)
            norm_pe(pe, 3)
            moe_pe(pe, 1)
            finish_pe(pe, lambda e: e.wait_ge(sem("acc_done"), 2 * DN))

        @block.scalar
        def _(act):
            own = Own(act, sem("act_steps"))
            load_consts(act)
            act.wait_ge(sem("eps_set"), 1)
            norm_act(act, own, 0, lambda e: e.wait_ge(sem("h_ready"), KC))
            even_proj_act(act, own)
            even_turn_act(act, own)
            retention_act(act, own)
            prompt_attn_act(act, own)
            sample_attn_act(act, own)
            norm_act(act, own, 1, lambda e: e.wait_ge(sem("h_ready"), 2 * KC))
            moe_act(act, own, 0)
            norm_act(act, own, 2, lambda e: e.wait_ge(sem("acc_done"), 8 * N_EXPERTS))
            odd_setup_act(act, own)
            odd_groups_act(act, own)
            odd_out_act(act, own)
            norm_act(act, own, 3, lambda e: e.wait_ge(sem("h_ready"), 3 * KC))
            act.wait_ge(sem("tails_stored"), 32)
            moe_act(act, own, 1)
            finish_act(act, own)

        @block.vector
        def _(dve):
            own = Own(dve, sem("dve_steps"))
            dve.memset(eps[:, :], EPS).then_inc(sem("eps_set"), 1)
            transpose_x_dve(dve, own)
            dve.wait_ge(sem("consts_loaded"), 16 * N_CONSTS)
            norm_dve(dve, own, 0, g_mix[:, 0, :])
            even_rope_dve(dve, own)
            retention_dve(dve, own)
            prompt_attn_dve(dve, own)
            sample_setup_dve(dve, own)
            sample_attn_dve(dve, own)
            even_out_dve(dve, own)
            norm_dve(dve, own, 1, g_ffn[:, 0, :])
            moe_dve(dve, own, 0)
            norm_dve(dve, own, 2, g_mix[:, 1, :])
            odd_setup_dve(dve, own)
            odd_groups_dve(dve, own)
            odd_out_dve(dve, own)
            norm_dve(dve, own, 3, g_ffn[:, 1, :])
            moe_dve(dve, own, 1)

        @block.gpsimd
        def _(pool):
            for l in range(2):
                pool.dma_start(wr[:, l, :, 0:4], d["w_router_group"][l].rearrange("(k p) n -> p k n", p=P)).then_inc(sem("wr_loaded"), 16)
                pool.dma_start(wr[:, l, :, 4:20], d["w_router_expert"][l].rearrange("(k p) n -> p k n", p=P)).then_inc(sem("wr_loaded"), 16)
            kv_pool(pool)
            retention_pool(pool)
            pool.wait_ge(sem("ret_s_state"), HEADS)
            pool.dma_start(maskp, d["c_maskp"]).then_inc(sem("maskp_loaded"), 16)
            pool.dma_start(sc_mask[R], d["c_masks"]).then_inc(sem("masks_loaded"), 16)
            pool.dma_start(before[R], d["c_before"]).then_inc(sem("masks_loaded"), 16)
            odd_setup_pool(pool)


N_CONSTS = 15
_CONSTS = shape_constants()
_OUTS = [("y_prompt", (1, SEQ, D_MODEL)), ("y_sample", (8, 8, D_MODEL)),
         ("ret_prompt", (1, 1, 8, 64, 128)), ("ret_sample", (1, 8, 8, 64, 128)),
         ("k_prompt", (1, 1, SEQ, 8, 64)), ("v_prompt", (1, 1, SEQ, 8, 64)),
         ("k_sample", (1, 8, 8, 8, 64)), ("v_sample", (1, 8, 8, 8, 64)),
         ("ssm_prompt", (1, 1, 32, 64, 128)), ("ssm_sample", (1, 8, 32, 64, 128)),
         ("conv_prompt", (1, 1, 3, 4096)), ("conv_sample", (1, 8, 3, 4096))]


def kernel(**inputs):
    import concourse.bacc as _bacc
    from concourse.bass_utils import run_bass_kernel_spmd as _run

    by_part = {"norm_mix": lambda a: a.reshape(2, KC, P).transpose(2, 0, 1),
               "norm_ffn": lambda a: a.reshape(2, KC, P).transpose(2, 0, 1),
               "conv_w": lambda a: a[0].reshape(CONV_W, 32, P).transpose(2, 1, 0),
               "conv_b": lambda a: a[0].reshape(32, P).transpose(1, 0),
               "ssd_norm": lambda a: a[0].reshape(16, P).transpose(1, 0),
               "dt_bias": lambda a: a.reshape(SSM_HEADS, 1), "a_log": lambda a: a.reshape(SSM_HEADS, 1),
               "d_skip": lambda a: a.reshape(16, 2).transpose(1, 0)}
    nc = _bacc.Bacc("TRN2", target_bir_lowering=False, num_devices=1)
    arrays, d = {}, {}
    for name, a in list(inputs.items()) + [("c_" + k, v) for k, v in _CONSTS.items()]:
        a = np.ascontiguousarray(by_part.get(name, lambda x: x)(np.asarray(a)))
        arrays[f"in_{name}"] = a
        d[name] = nc.dram_tensor(f"in_{name}", a.shape, mybir.dt.from_np(a.dtype), kind="ExternalInput").ap()
    for name, shape in _OUTS:
        d[name] = nc.dram_tensor(f"out_{name}", shape, F32, kind="ExternalOutput").ap()
    build(nc, d)
    r = _run(nc, [arrays], core_ids=[0])
    return tuple(r.results[0][f"out_{name}"] for name, _ in _OUTS)
```
